# Optimizing a Trainium2 kernel written in Bass

```python
import math
import jax, jax.numpy as jnp
from jax import lax
import numpy as np

D_MODEL = 1024
BATCH = 1
SEQ = 256
DEPTH = 2

N_MIXERS = 2
N_GLA_LAYERS = (DEPTH + 1) // 2
N_ATTN_LAYERS = DEPTH // 2

GRID_W = 64

GLA_HEADS = 4
GLA_KEY_DIM = D_MODEL // 2
GLA_VAL_DIM = D_MODEL
GLA_DK = GLA_KEY_DIM // GLA_HEADS
GLA_DV = GLA_VAL_DIM // GLA_HEADS
GLA_GATE_RANK = 16
GLA_GATE_NORMALIZER = 16.0
GLA_CHUNK = 64
GLA_IN_DIM = 2 * GLA_KEY_DIM + 2 * GLA_VAL_DIM + 2 * GLA_GATE_RANK

ATTN_HEAD_DIM = 128
ATTN_Q_HEADS = D_MODEL // ATTN_HEAD_DIM
ATTN_KV_HEADS = 2
ATTN_GROUP = ATTN_Q_HEADS // ATTN_KV_HEADS
ATTN_QKV_DIM = (ATTN_Q_HEADS + 2 * ATTN_KV_HEADS) * ATTN_HEAD_DIM
QUERY_BLOCK = 128
ROPE_THETA = 10000.0
ROPE_PAIRS_PER_AXIS = ATTN_HEAD_DIM // 4

D_FF = 2816
CONV_WIDTH = 3

NORM_EPS = 1e-6


def rmsnorm(x, w):
    xf = x.astype(jnp.float32)
    y = xf * lax.rsqrt(jnp.mean(xf * xf, axis=-1, keepdims=True) + NORM_EPS)
    return (y * w.astype(jnp.float32)).astype(x.dtype)

def gla_chunked(q, k, v, log_a, strict):
    B, H, S, dk = q.shape
    dv = v.shape[-1]
    n = S // GLA_CHUNK
    c = lambda t: t.reshape(B, H, n, GLA_CHUNK, t.shape[-1])
    q, k, v, log_a = c(q), c(k), c(v), c(log_a)
    b = jnp.cumsum(log_a, axis=3)
    b_end = b[:, :, :, -1:, :]
    q_dec = q * jnp.exp(b)
    k_inv = k * jnp.exp(-b)
    mask = jnp.tril(jnp.ones((GLA_CHUNK, GLA_CHUNK), dtype=bool), k=-1 if strict else 0)
    att = jnp.where(mask, jnp.einsum('bhncd,bhnsd->bhncs', q_dec, k_inv), 0.0)
    o_intra = jnp.einsum('bhncs,bhnsv->bhncv', att, v)
    kv_chunk = jnp.einsum('bhncd,bhncv->bhndv', k * jnp.exp(b_end - b), v)
    decay_chunk = jnp.exp(b_end[:, :, :, 0, :])

    def step(state, inp):
        d, kv_c = inp
        return d[..., None] * state + kv_c, state

    _, s_prev = lax.scan(step, jnp.zeros((B, H, dk, dv), jnp.float32),
                         (jnp.moveaxis(decay_chunk, 2, 0), jnp.moveaxis(kv_chunk, 2, 0)))
    s_prev = jnp.moveaxis(s_prev, 0, 2)
    o_inter = jnp.einsum('bhncd,bhndv->bhncv', q_dec, s_prev)
    return (o_intra + o_inter).reshape(B, H, S, dv)

def gla_mixer(h, w_in, w_gate_up_f, b_gate_f, w_gate_up_b, b_gate_b, norm_w, w_out):
    B, S, _ = h.shape
    f32 = jnp.float32
    proj = h @ w_in
    q, k, v, g, r = jnp.split(
        proj, [GLA_KEY_DIM, 2 * GLA_KEY_DIM, 2 * GLA_KEY_DIM + GLA_VAL_DIM,
               2 * GLA_KEY_DIM + 2 * GLA_VAL_DIM], axis=-1)
    r_f, r_b = jnp.split(r, 2, axis=-1)

    def heads(t, d):
        return t.reshape(B, S, GLA_HEADS, d).transpose(0, 2, 1, 3).astype(f32)

    def log_decay(r_dir, w_up, b_up):
        logits = (r_dir @ w_up + b_up).astype(f32)
        return heads(jax.nn.log_sigmoid(logits) / GLA_GATE_NORMALIZER, GLA_DK)

    q = heads(q, GLA_DK) * (GLA_DK ** -0.5)
    k = heads(k, GLA_DK)
    v = heads(v, GLA_DV)
    la_f = log_decay(r_f, w_gate_up_f, b_gate_f)
    la_b = log_decay(r_b, w_gate_up_b, b_gate_b)
    flip = lambda t: jnp.flip(t, axis=2)
    o_f = gla_chunked(q, k, v, la_f, strict=False)
    o_b = flip(gla_chunked(flip(q), flip(k), flip(v), flip(la_b), strict=True))
    o = (o_f + o_b).transpose(0, 2, 1, 3)
    o = rmsnorm(o, norm_w) * jax.nn.silu(g.astype(f32).reshape(B, S, GLA_HEADS, GLA_DV))
    return o.reshape(B, S, GLA_VAL_DIM).astype(h.dtype) @ w_out

def apply_rope(x, cos, sin):
    half = x.shape[-1] // 2
    x1, x2 = x[..., :half], x[..., half:]
    return jnp.concatenate([x1 * cos - x2 * sin, x1 * sin + x2 * cos], axis=-1)

def attn_mixer(h, w_qkv, q_norm, k_norm, w_out, cos, sin):
    B, S, _ = h.shape
    proj = h @ w_qkv
    q, k, v = jnp.split(proj, [ATTN_Q_HEADS * ATTN_HEAD_DIM,
                               (ATTN_Q_HEADS + ATTN_KV_HEADS) * ATTN_HEAD_DIM], axis=-1)
    q = q.reshape(B, S, ATTN_Q_HEADS, ATTN_HEAD_DIM)
    k = k.reshape(B, S, ATTN_KV_HEADS, ATTN_HEAD_DIM)
    v = v.reshape(B, S, ATTN_KV_HEADS, ATTN_HEAD_DIM)
    q = apply_rope(rmsnorm(q, q_norm).astype(jnp.float32), cos, sin).astype(h.dtype)
    k = apply_rope(rmsnorm(k, k_norm).astype(jnp.float32), cos, sin).astype(h.dtype)
    n_blk = S // QUERY_BLOCK
    qb = q.reshape(B, S, ATTN_KV_HEADS, ATTN_GROUP, ATTN_HEAD_DIM).transpose(0, 2, 3, 1, 4)
    qb = qb.reshape(B, ATTN_KV_HEADS, ATTN_GROUP, n_blk, QUERY_BLOCK, ATTN_HEAD_DIM)
    qb = qb.transpose(3, 0, 1, 2, 4, 5)
    k = k.transpose(0, 2, 1, 3)
    v = v.transpose(0, 2, 1, 3)
    scale = ATTN_HEAD_DIM ** -0.5

    def block(q_blk):
        s = jnp.einsum('bkgqd,bksd->bkgqs', q_blk, k).astype(jnp.float32) * scale
        p = jax.nn.softmax(s, axis=-1).astype(v.dtype)
        return jnp.einsum('bkgqs,bksd->bkgqd', p, v)

    o = lax.map(block, qb)
    o = o.transpose(1, 0, 4, 2, 3, 5).reshape(B, S, ATTN_Q_HEADS * ATTN_HEAD_DIM)
    return o @ w_out

def conv_ffn(h, w_up, w_conv, b_conv, w_down):
    u = h @ w_up
    u = lax.conv_general_dilated(
        u, w_conv[:, None, :], window_strides=(1,), padding=[(1, 1)],
        dimension_numbers=('NWC', 'WIO', 'NWC'), feature_group_count=u.shape[-1]) + b_conv
    val, gate = jnp.split(u, 2, axis=-1)
    return (jax.nn.silu(gate) * val) @ w_down

def first_inputs(seed: int = 0) -> dict:
    key = jax.random.key(seed)
    ks = jax.random.split(key, 20)
    nrm = lambda k, shape, s: jax.random.normal(k, shape, jnp.float32) * s
    NG, NA = N_GLA_LAYERS, N_ATTN_LAYERS
    return {
        'x': nrm(ks[0], (BATCH, SEQ, D_MODEL), 1.0),
        'norm_mix': 1.0 + nrm(ks[1], (DEPTH, D_MODEL), 0.01),
        'norm_ffn': 1.0 + nrm(ks[2], (DEPTH, D_MODEL), 0.01),
        'gla_w_in': nrm(ks[3], (NG, D_MODEL, GLA_IN_DIM), D_MODEL ** -0.5),
        'gla_w_gate_up_f': nrm(ks[4], (NG, GLA_GATE_RANK, GLA_KEY_DIM), GLA_GATE_RANK ** -0.5),
        'gla_b_gate_f': nrm(ks[5], (NG, GLA_KEY_DIM), 0.1),
        'gla_w_gate_up_b': nrm(ks[6], (NG, GLA_GATE_RANK, GLA_KEY_DIM), GLA_GATE_RANK ** -0.5),
        'gla_b_gate_b': nrm(ks[7], (NG, GLA_KEY_DIM), 0.1),
        'gla_norm': 1.0 + nrm(ks[8], (NG, GLA_DV), 0.01),
        'gla_w_out': nrm(ks[9], (NG, GLA_VAL_DIM, D_MODEL), GLA_VAL_DIM ** -0.5),
        'attn_w_qkv': nrm(ks[10], (NA, D_MODEL, ATTN_QKV_DIM), D_MODEL ** -0.5),
        'attn_q_norm': 1.0 + nrm(ks[11], (NA, ATTN_HEAD_DIM), 0.01),
        'attn_k_norm': 1.0 + nrm(ks[12], (NA, ATTN_HEAD_DIM), 0.01),
        'attn_w_out': nrm(ks[13], (NA, ATTN_Q_HEADS * ATTN_HEAD_DIM, D_MODEL),
                          (ATTN_Q_HEADS * ATTN_HEAD_DIM) ** -0.5),
        'ffn_w_up': nrm(ks[14], (DEPTH, D_MODEL, 2 * D_FF), D_MODEL ** -0.5),
        'ffn_w_conv': nrm(ks[15], (DEPTH, CONV_WIDTH, 2 * D_FF), CONV_WIDTH ** -0.5),
        'ffn_b_conv': nrm(ks[16], (DEPTH, 2 * D_FF), 0.01),
        'ffn_w_down': nrm(ks[17], (DEPTH, D_FF, D_MODEL), D_FF ** -0.5),
    }

def first_block(x, norm_mix, norm_ffn, gla_w_in, gla_w_gate_up_f, gla_b_gate_f,
              gla_w_gate_up_b, gla_b_gate_b, gla_norm, gla_w_out,
              attn_w_qkv, attn_q_norm, attn_k_norm, attn_w_out,
              ffn_w_up, ffn_w_conv, ffn_b_conv, ffn_w_down):
    S = x.shape[1]
    rows = S // GRID_W
    f32 = jnp.float32
    row_idx = jnp.repeat(jnp.arange(rows, dtype=f32), GRID_W)
    col_idx = jnp.tile(jnp.arange(GRID_W, dtype=f32), rows)
    inv_freq = ROPE_THETA ** (-jnp.arange(ROPE_PAIRS_PER_AXIS, dtype=f32) / ROPE_PAIRS_PER_AXIS)
    ang = jnp.concatenate([row_idx[:, None] * inv_freq, col_idx[:, None] * inv_freq], axis=-1)
    cos = jnp.cos(ang)[None, :, None, :]
    sin = jnp.sin(ang)[None, :, None, :]

    for i in range(DEPTH):
        h = rmsnorm(x, norm_mix[i])
        j = i // N_MIXERS
        if i % N_MIXERS == 0:
            x = x + gla_mixer(h, gla_w_in[j], gla_w_gate_up_f[j], gla_b_gate_f[j],
                              gla_w_gate_up_b[j], gla_b_gate_b[j], gla_norm[j], gla_w_out[j])
        else:
            x = x + attn_mixer(h, attn_w_qkv[j], attn_q_norm[j], attn_k_norm[j],
                               attn_w_out[j], cos, sin)
        x = x + conv_ffn(rmsnorm(x, norm_ffn[i]), ffn_w_up[i], ffn_w_conv[i],
                         ffn_b_conv[i], ffn_w_down[i])
    return x


DEPTH_2 = 1

D_CONV = 1024
CONV_WIDTH_2 = 31
RWKV_HEAD = 64
RWKV_HEADS = D_MODEL // RWKV_HEAD
D_RWKV = RWKV_HEADS * RWKV_HEAD
DECAY_LORA = 64
AAA_LORA = 64
TS_WIDTH = 3 * D_RWKV + DECAY_LORA + AAA_LORA
SPLITS = (D_CONV, 2 * D_CONV, 3 * D_CONV, 3 * D_CONV + TS_WIDTH, 3 * D_CONV + TS_WIDTH + D_RWKV, 3 * D_CONV + TS_WIDTH + D_RWKV + D_MODEL)
D_IN = 3 * D_CONV + TS_WIDTH + D_RWKV + 2 * D_MODEL
RWKV_SPLITS = (D_RWKV, 2 * D_RWKV, 3 * D_RWKV, 3 * D_RWKV + DECAY_LORA)

RMS_EPS = 1e-6
LN_EPS = 1e-5
GN_EPS = 64e-5
L2_EPS = 1e-12


def _rmsnorm(x, g):
    xf = x.astype(jnp.float32)
    y = xf * lax.rsqrt(jnp.mean(xf * xf, axis=-1, keepdims=True) + RMS_EPS)
    return (y * g.astype(jnp.float32)).astype(x.dtype)

def _layernorm(x, g, b, eps):
    xf = x.astype(jnp.float32)
    mu = jnp.mean(xf, axis=-1, keepdims=True)
    var = jnp.mean(jnp.square(xf - mu), axis=-1, keepdims=True)
    y = (xf - mu) * lax.rsqrt(var + eps) * g.astype(jnp.float32) + b.astype(jnp.float32)
    return y.astype(x.dtype)

def _causal_depthwise_conv(u, w, b):
    y = lax.conv_general_dilated(
        u, w[:, None, :].astype(u.dtype), window_strides=(1,),
        padding=((CONV_WIDTH_2 - 1, 0),), dimension_numbers=('NWC', 'WIO', 'NWC'),
        feature_group_count=u.shape[-1])
    return y + b

def _token_shift(z, mu):
    prev = jnp.pad(z, ((0, 0), (1, 0), (0, 0)))[:, :-1]
    return z + mu * (prev - z)

def _rwkv7_scan(r, decay, k, v, kk, b):
    bsz, _, h, n = r.shape

    def step(state, inp):
        r_t, w_t, k_t, v_t, kk_t, b_t = inp
        sk = jnp.einsum('bhvk,bhk->bhv', state, kk_t)
        state = (state * w_t[:, :, None, :] - sk[..., None] * b_t[:, :, None, :]
                 + v_t[..., None] * k_t[:, :, None, :])
        return state, jnp.einsum('bhvk,bhk->bhv', state, r_t)

    xs = tuple(jnp.moveaxis(t, 1, 0) for t in (r, decay, k, v, kk, b))
    s0 = jnp.zeros((bsz, h, n, n), jnp.float32)
    _, out = lax.scan(step, s0, xs)
    return jnp.moveaxis(out, 0, 1)

def _rwkv7_branch(ts, og, mu, w0, w2, a0, a2, k_k, k_a, r_k, gn_g, gn_b, w_o):
    f32 = jnp.float32
    bsz, seq, _ = ts.shape
    hd = (bsz, seq, RWKV_HEADS, RWKV_HEAD)
    r, k, v, w_low, a_low = jnp.split(_token_shift(ts, mu), RWKV_SPLITS, axis=-1)
    w_pre = (w0 + jnp.tanh(w_low) @ w2).astype(f32)
    decay = jnp.exp(-jnp.exp(-jax.nn.softplus(-w_pre) - 0.5))
    a = jax.nn.sigmoid((a0 + a_low @ a2).astype(f32))
    kk = (k * k_k).astype(f32).reshape(hd)
    kk = kk / jnp.maximum(jnp.sqrt(jnp.sum(kk * kk, axis=-1, keepdims=True)), L2_EPS)
    k = (k.astype(f32) * (1.0 + (a - 1.0) * k_a.astype(f32))).reshape(hd)
    r = r.astype(f32).reshape(hd)
    v = v.astype(f32).reshape(hd)
    a = a.reshape(hd)
    o = _rwkv7_scan(r, decay.reshape(hd), k, v, kk, kk * a)
    o = _layernorm(o, gn_g.reshape(RWKV_HEADS, RWKV_HEAD), gn_b.reshape(RWKV_HEADS, RWKV_HEAD), GN_EPS)
    o = o + jnp.sum(r * k * r_k.astype(f32), axis=-1, keepdims=True) * v
    o = o.reshape(bsz, seq, D_RWKV).astype(og.dtype) * jax.nn.silu(og)
    return o @ w_o

def _conv_branch(val, gate, og, conv_k, conv_b, ln_g, ln_b, w_o):
    u = val * jax.nn.sigmoid(gate)
    u = _causal_depthwise_conv(u, conv_k, conv_b)
    u = _layernorm(u, ln_g, ln_b, LN_EPS)
    u = jax.nn.silu(u) * jax.nn.silu(og)
    return u @ w_o

def second_inputs(seed: int = 0) -> dict:
    key = jax.random.key(seed)
    ks = jax.random.split(key, 24)
    f32 = jnp.float32
    nrm = lambda k, shape, s: jax.random.normal(k, shape, f32) * s
    L = DEPTH_2
    return {
        'x': nrm(ks[0], (BATCH, SEQ, D_MODEL), 1.0),
        'c': nrm(ks[1], (BATCH, D_MODEL), 1.0),
        'ada_w': nrm(ks[2], (L, D_MODEL, 3 * D_MODEL), 0.5 * D_MODEL ** -0.5),
        'ada_b': nrm(ks[3], (L, 3 * D_MODEL), 0.01),
        'norm_g': 1.0 + nrm(ks[4], (L, D_MODEL), 0.1),
        'w_in': nrm(ks[5], (L, D_MODEL, D_IN), D_MODEL ** -0.5),
        'conv_k': nrm(ks[6], (L, CONV_WIDTH_2, D_CONV), CONV_WIDTH_2 ** -0.5),
        'conv_b': nrm(ks[7], (L, D_CONV), 0.01),
        'conv_ln_g': 1.0 + nrm(ks[8], (L, D_CONV), 0.1),
        'conv_ln_b': nrm(ks[9], (L, D_CONV), 0.01),
        'w_conv_out': nrm(ks[10], (L, D_CONV, D_MODEL), D_CONV ** -0.5),
        'rwkv_mu': jax.random.uniform(ks[11], (L, TS_WIDTH), f32, 0.0, 1.0),
        'rwkv_w0': jax.random.uniform(ks[12], (L, D_RWKV), f32, -6.0, -1.0),
        'rwkv_w2': nrm(ks[13], (L, DECAY_LORA, D_RWKV), 0.1 * DECAY_LORA ** -0.5),
        'rwkv_a0': nrm(ks[14], (L, D_RWKV), 0.1),
        'rwkv_a2': nrm(ks[15], (L, AAA_LORA, D_RWKV), 0.5 * AAA_LORA ** -0.5),
        'rwkv_k_k': 0.85 + nrm(ks[16], (L, D_RWKV), 0.05),
        'rwkv_k_a': 1.0 + nrm(ks[17], (L, D_RWKV), 0.05),
        'rwkv_r_k': nrm(ks[18], (L, RWKV_HEADS, RWKV_HEAD), 0.1),
        'rwkv_gn_g': 1.0 + nrm(ks[19], (L, D_RWKV), 0.1),
        'rwkv_gn_b': nrm(ks[20], (L, D_RWKV), 0.01),
        'w_rwkv_out': nrm(ks[21], (L, D_RWKV, D_MODEL), D_RWKV ** -0.5),
        'w_out': nrm(ks[22], (L, D_MODEL, D_MODEL), D_MODEL ** -0.5),
        'final_g': 1.0 + nrm(ks[23], (D_MODEL,), 0.1),
    }

def second_block(x, c, ada_w, ada_b, norm_g, w_in, conv_k, conv_b, conv_ln_g, conv_ln_b, w_conv_out,
              rwkv_mu, rwkv_w0, rwkv_w2, rwkv_a0, rwkv_a2, rwkv_k_k, rwkv_k_a, rwkv_r_k,
              rwkv_gn_g, rwkv_gn_b, w_rwkv_out, w_out, final_g):
    for l in range(DEPTH_2):
        mod = jnp.einsum('bd,de->be', jax.nn.silu(c), ada_w[l]) + ada_b[l]
        shift, scale, gate = jnp.split(mod, 3, axis=-1)
        h = _rmsnorm(x, norm_g[l]) * (1.0 + scale[:, None, :]) + shift[:, None, :]
        p = jnp.einsum('bsd,de->bse', h, w_in[l])
        c_val, c_gate, c_og, ts, r_og, g_conv, g_rwkv = jnp.split(p, SPLITS, axis=-1)
        y_conv = _conv_branch(c_val, c_gate, c_og, conv_k[l], conv_b[l], conv_ln_g[l], conv_ln_b[l],
                              w_conv_out[l])
        y_rwkv = _rwkv7_branch(ts, r_og, rwkv_mu[l], rwkv_w0[l], rwkv_w2[l], rwkv_a0[l], rwkv_a2[l],
                               rwkv_k_k[l], rwkv_k_a[l], rwkv_r_k[l], rwkv_gn_g[l], rwkv_gn_b[l],
                               w_rwkv_out[l])
        m = jax.nn.sigmoid(g_conv) * y_conv + jax.nn.sigmoid(g_rwkv) * y_rwkv
        out = jnp.einsum('bsd,de->bse', m, w_out[l])
        x = x + gate[:, None, :] * out
    return _rmsnorm(x, final_g)


def setup_inputs(seed=0):
    out = dict(first_inputs(seed))
    for name, value in second_inputs(seed + 1).items():
        if name != "x":
            out[name + "_2"] = value
    return out


def reference(
    x, norm_mix, norm_ffn, gla_w_in, gla_w_gate_up_f, gla_b_gate_f, gla_w_gate_up_b,
    gla_b_gate_b, gla_norm, gla_w_out, attn_w_qkv, attn_q_norm, attn_k_norm, attn_w_out,
    ffn_w_up, ffn_w_conv, ffn_b_conv, ffn_w_down, c_2, ada_w_2, ada_b_2, norm_g_2, w_in_2,
    conv_k_2, conv_b_2, conv_ln_g_2, conv_ln_b_2, w_conv_out_2, rwkv_mu_2, rwkv_w0_2, rwkv_w2_2,
    rwkv_a0_2, rwkv_a2_2, rwkv_k_k_2, rwkv_k_a_2, rwkv_r_k_2, rwkv_gn_g_2, rwkv_gn_b_2,
    w_rwkv_out_2, w_out_2, final_g_2,
):
    x = first_block(
        x, norm_mix, norm_ffn, gla_w_in, gla_w_gate_up_f, gla_b_gate_f, gla_w_gate_up_b,
        gla_b_gate_b, gla_norm, gla_w_out, attn_w_qkv, attn_q_norm, attn_k_norm, attn_w_out,
        ffn_w_up, ffn_w_conv, ffn_b_conv, ffn_w_down,
    )
    return second_block(
        x, c_2, ada_w_2, ada_b_2, norm_g_2, w_in_2, conv_k_2, conv_b_2, conv_ln_g_2,
        conv_ln_b_2, w_conv_out_2, rwkv_mu_2, rwkv_w0_2, rwkv_w2_2, rwkv_a0_2, rwkv_a2_2,
        rwkv_k_k_2, rwkv_k_a_2, rwkv_r_k_2, rwkv_gn_g_2, rwkv_gn_b_2, w_rwkv_out_2, w_out_2,
        final_g_2,
    )


_drawn_inputs = setup_inputs


def setup_inputs(seed=0):
    import zlib

    import numpy as np

    out = dict(_drawn_inputs(seed))
    spreads = {}
    factors = {'norm_mix': 4.296,
     'norm_ffn': 5.729,
     'gla_b_gate_f': 2.891,
     'gla_b_gate_b': 2.954,
     'gla_norm': 8.0,
     'attn_q_norm': 23.378,
     'attn_k_norm': 28.658,
     'ffn_b_conv': 5.969,
     'ada_b_2': 8.0,
     'norm_g_2': 3.24,
     'conv_b_2': 64.0,
     'conv_ln_g_2': 64.0,
     'conv_ln_b_2': 64.0,
     'rwkv_w2_2': 64.0,
     'rwkv_a0_2': 8.0,
     'rwkv_a2_2': 3.282,
     'rwkv_k_k_2': 64.0,
     'rwkv_k_a_2': 8.0,
     'rwkv_gn_g_2': 52.12,
     'rwkv_gn_b_2': 64.0}
    for name, (base, spread) in spreads.items():
        noise = np.random.default_rng([zlib.crc32(name.encode()), seed]).standard_normal(out[name].shape)
        drawn = base * np.exp(spread * noise) if base else spread * noise
        out[name] = __import__('jax').numpy.asarray(drawn.astype(out[name].dtype))
    for name, factor in factors.items():
        out[name] = (out[name] * factor).astype(out[name].dtype)
    return out
```

```python
from contextlib import ExitStack

import numpy as np

import concourse.bass as bass
from concourse import mybir

F32 = mybir.dt.float32
F32R = mybir.dt.float32r
I32 = mybir.dt.int32
ALU = mybir.AluOpType
ACT = mybir.ActivationFunctionType
AX_X = mybir.AxisListType.X

P = 128
D = 1024
T = 256
KT = D // P
FF = 2816
FI = FF // 256
CH = 64
NC = T // CH
GH_ = 4
QH, KVH = 8, 2
RING = 3
BW = 256
EPS = 1e-6
LN_EPS = 1e-5
GN_EPS = 64e-5
DECAY = -float(np.exp(np.float32(-0.5)))
W2 = 1024
N_GIN = 0
N_GOUT = N_GIN + 12
N_F0 = N_GOUT + 4
N_QKV = N_F0 + 3 * FI
N_AOUT = N_QKV + 6
N_F1 = N_AOUT + 4
N_RKV = N_F1 + 3 * FI
N_ROG = N_RKV + 12
N_ROUT = N_ROG + 4
N_GR = N_ROUT + 4
N_CV = N_GR + 4
N_CG = N_CV + 4
N_COG = N_CG + 4
N_COUT = N_COG + 4
N_GC = N_COUT + 4
N_OUT = N_GC + 4
N_END = N_OUT + 4

VECS = [("norm_mix", 16), ("norm_ffn", 16), ("gla_b_gate_f", 4), ("gla_b_gate_b", 4), ("gla_norm", 2),
        ("attn_q_norm", 1), ("attn_k_norm", 1), ("ffn_w_conv", 264), ("ffn_b_conv", 88), ("c_2", 8),
        ("ada_b_2", 24), ("norm_g_2", 8), ("conv_k_2", 248), ("conv_b_2", 8), ("conv_ln_g_2", 8),
        ("conv_ln_b_2", 8), ("rwkv_mu_2", 25), ("rwkv_w0_2", 8), ("rwkv_a0_2", 8), ("rwkv_k_k_2", 8),
        ("rwkv_k_a_2", 8), ("rwkv_r_k_2", 8), ("rwkv_gn_g_2", 8), ("rwkv_gn_b_2", 8), ("final_g_2", 8)]
COL = {}
_at = 0
for _name, _n in VECS:
    COL[_name] = _at
    _at += _n
NV = _at

CONSTS = [("ident", 128), ("ones", 128), ("blk", 128), ("rot", 128), ("cos", 256), ("sin", 256),
          ("scan", 256), ("scmask", 128), ("lev", 6 * 64), ("mask_f", 128), ("mask_b", 128)]
CC = {}
_at = 0
for _name, _n in CONSTS:
    CC[_name] = (_at, _at + _n)
    _at += _n
NCST = _at


def constants():
    c = np.zeros((P, NCST), np.float32)
    i = np.arange(P)

    def put(name, a):
        c[:, CC[name][0]:CC[name][1]] = a

    put("ident", np.eye(P))
    put("ones", 1.0)
    put("blk", i[:, None] // 64 == i[None, :] // 64)
    rot = np.zeros((P, P), np.float32)
    rot[i[64:], i[:64]] = -1.0
    rot[i[:64], i[64:]] = 1.0
    put("rot", rot)
    f = np.float32
    tok = np.arange(T)
    inv = f(10000.0) ** (-np.arange(32, dtype=f) / f(32))
    ang = np.concatenate([(tok // 64).astype(f)[:, None] * inv, (tok % 64).astype(f)[:, None] * inv], -1)
    put("cos", np.tile(np.cos(ang).T, (2, 1)))
    put("sin", np.tile(np.sin(ang).T, (2, 1)))
    put("scan", (np.arange(T) % CH != 0)[None, :])
    s, t = i[:, None], i[None, :]
    src = s % CH
    put("scmask", np.where(t < CH, src < t % CH, src <= t % CH))
    for lev in range(6):
        a, b = np.arange(P)[:, None], np.arange(64)[None, :]
        h = 1 << lev
        c[:, CC["lev"][0] + 64 * lev:CC["lev"][0] + 64 * (lev + 1)] = (
            (a // (2 * h) == b // (2 * h)) & (a // h % 2 == 0) & (b // h % 2 == 1))
    same = s // CH == t // CH
    c.view(np.int32)[:, CC["mask_f"][0]:CC["mask_f"][1]] = same & (s <= t)
    c.view(np.int32)[:, CC["mask_b"][0]:CC["mask_b"][1]] = same & (s > t)
    return c


class Chain:

    def __init__(self, eng, sem):
        self.eng, self.sem, self.n, self.turn = eng, sem, 0, None

    def done(self, ins):
        ins.then_inc(self.sem, 1)
        self.n += 1

    def value(self, back=0):
        n = self.n - back
        return n if self.turn is None else self.turn[0] * self.turn[1] + n

    def all(self, back=0):
        self.eng.wait_ge(self.sem, self.value(back))

    def step(self, ins):
        self.done(ins)
        self.all()

    def enter(self, i, per):
        self.turn, self.first = (i, per), self.n

    def leave(self, trips):
        assert self.n - self.first == self.turn[1], (self.n - self.first, self.turn[1])
        self.n = self.first + trips * self.turn[1]
        self.turn = None


def program(nc, a, out):
    with ExitStack() as ctx:
        def sb(name, shape, dt=F32):
            return ctx.enter_context(nc.sbuf_tensor(name, shape, dt))[:]

        sems = {}

        def sem(name):
            if name not in sems:
                sems[name] = ctx.enter_context(nc.semaphore(name))
            return sems[name]

        X = sb("x", [P, KT, T])
        HF = sb("hf", [P, KT, T])
        XH, XL = sb("xh", [P, KT, T], F32R), sb("xl", [P, KT, T], F32R)
        GH, GL = sb("gh", [P, KT, T], F32R), sb("gl", [P, KT, T], F32R)
        RAW = sb("raw", [P, RING, KT, BW])
        WH, WL = sb("wh", [P, RING, KT, BW], F32R), sb("wl", [P, RING, KT, BW], F32R)
        BIG = sb("big", [P, 8, KT, T])
        V = sb("vecs", [P, NV])
        C = sb("consts", [P, NCST])
        U = sb("u", [P, 2, 2, T + 2])
        RS = sb("rs", [P, T])
        small = sb("small", [P, 64])
        mod = sb("mod", [P, 32])
        PS = [ctx.enter_context(nc.psum_tensor(f"bank{i}", [P, 512], F32)) for i in range(8)]

        def cst(name):
            return C[:, CC[name][0]:CC[name][1]]

        def vec(name, j=0, n=1):
            return V[:, COL[name] + j:COL[name] + j + n]

        ident, ones, blk, rot = cst("ident"), cst("ones"), cst("blk"), cst("rot")

        def big(j, n=KT):
            return BIG[:, j, 0:n, :]

        BT = BIG[:, :, :, :].rearrange("p j k t -> p (j k) t")

        def tiles(j, n=1):
            return BT[:, j:j + n, :]

        def flat(j, n):
            return BT[:, j:j + n, :].rearrange("p k t -> p (k t)")

        raw_landed = [sem(f"raw_landed{i}") for i in range(RING)]
        w_hi_ready, w_lo_ready, block_done = sem("w_hi_ready"), sem("w_lo_ready"), sem("block_done")
        evacuated = sem("evacuated")
        out_added = sem("out_added")
        consts_landed = sem("consts_landed")

        def split_hi(act, n, i=0):
            act.wait_ge(raw_landed[n % RING], 16 * (n // RING + 1) + 16 * i)
            if n >= RING:
                act.wait_ge(block_done, n - RING + 1 + RING * i)
            nc.scalar.activation(WH[:, n % RING, :, :], RAW[:, n % RING, :, :], ACT.Copy)\
                .then_inc(w_hi_ready, 1)

        def split_lo(dve, n, i=0):
            dve.wait_ge(w_hi_ready, n + 1 + RING * i)
            nc.vector.tensor_tensor(WL[:, n % RING, :, :], RAW[:, n % RING, :, :],
                                    WH[:, n % RING, :, :].bitcast(F32), ALU.subtract)\
                .then_inc(w_lo_ready, 1)

        def load(sp, n, src, i=0):
            if n >= RING:
                sp.wait_ge(w_lo_ready, n - RING + 1 + RING * i)
            dst = RAW[:, n % RING, :, :]
            if len(src.shape) == 4:
                dst = dst.rearrange("p (k c) n -> p k c n", k=2)
            sp.dma_start(dst, src).then_inc(raw_landed[n % RING], 16)

        def cols(w, c0):
            return w[:, c0:c0 + BW].rearrange("(k p) n -> p k n", p=P)

        def three(ps, wh, wl, xh, xl, start, stop, moving_weights=False):
            if moving_weights:
                nc.tensor.matmul(ps, xh, wh, start=start, stop=False)
                nc.tensor.matmul(ps, xh, wl, start=False, stop=False)
                return nc.tensor.matmul(ps, xl, wh, start=False, stop=stop)
            nc.tensor.matmul(ps, wh, xh, start=start, stop=False)
            nc.tensor.matmul(ps, wh, xl, start=False, stop=False)
            return nc.tensor.matmul(ps, wl, xh, start=False, stop=stop)

        def product(pe, n, bank, xh, xl, i=0, moving_weights=False):
            pe.wait_ge(w_lo_ready, n + 1 + RING * i)
            s = n % RING
            for m in range(2):
                ps = PS[bank][:, m * T:(m + 1) * T]
                ms = slice(m * P, (m + 1) * P)
                for k in range(KT):
                    if moving_weights:
                        last = three(ps, WH[:, s, k, :], WL[:, s, k, :], xh[:, k, ms], xl[:, k, ms],
                                     k == 0, k == KT - 1, True)
                    else:
                        last = three(ps, WH[:, s, k, ms], WL[:, s, k, ms], xh[:, k, :], xl[:, k, :],
                                     k == 0, k == KT - 1)
            last.then_inc(block_done, 1)

        E_GIN = 0
        E_F0 = E_GIN + 12
        E_QKV = E_F0 + 2 * FI
        E_F1 = E_QKV + 6
        E_RKV = E_F1 + 2 * FI
        E_ROG = E_RKV + 12
        E_GR = E_ROG + 4
        E_CV = E_GR + 4
        E_CG = E_CV + 4
        E_COG = E_CG + 4
        E_GC = E_COG + 4

        w_r = sb("w_r", [P, KT, 32])
        w_up = BT[0:16, 48:52, :].rearrange("p (d a) t -> p d (a t)", d=2)
        w_lora = BT[:, 24:28, :].rearrange("p a (b c) -> p (a b) c", c=128)
        w2a2 = BT[:, 28:32, :].rearrange("p a b -> p (a b)")

        w_in = a["w_in_2"]
        block = ctx.enter_context(nc.Block())

        @block.sync
        def _(sp):
            sp.dma_start(V[:, :], a["vecs"]).then_inc(consts_landed, 16)
            sp.dma_start(C[:, :], a["consts"]).then_inc(consts_landed, 16)
            sp.dma_start(X[:, :, :], a["x"]).then_inc(consts_landed, 16)
            sp.dma_start(w_r[:, :, :], a["gla_w_in"][:, 3072:3104].rearrange("(k p) n -> p k n", p=P))\
                .then_inc(consts_landed, 16)
            sp.dma_start(w_up[:, 0, :], a["gla_w_gate_up_f"]).then_inc(consts_landed, 16)
            sp.dma_start(w_up[:, 1, :], a["gla_w_gate_up_b"]).then_inc(consts_landed, 16)

            def columns(w, n0, c0, count):
                for j in range(count):
                    load(sp, n0 + j, cols(w, c0 + j * BW))

            columns(a["gla_w_in"], N_GIN, 0, 12)
            columns(a["gla_w_out"], N_GOUT, 0, 4)

            def mlp(layer, n0):
                up, down = a["ffn_w_up"][layer], a["ffn_w_down"][layer]
                down_b = down.rearrange("(i k p) n -> i p k n", k=2, p=P)
                load(sp, n0, cols(up, 0))
                load(sp, n0 + 1, cols(up, FF))
                with sp.Fori(0, FI - 1) as i:
                    def upc(first):
                        return up[:, bass.ds(i * BW + (first + BW), BW)].rearrange("(k p) n -> p k n", p=P)
                    load(sp, n0 + 2, upc(0), i)
                    load(sp, n0 + 3, upc(FF), i)
                    load(sp, n0 + 4, down[bass.ds(i * BW, BW), :].rearrange("(k p) (c n) -> p k c n", p=P, n=BW), i)
                load(sp, n0 + 3 * FI - 1, down[(FI - 1) * BW:FF, :].rearrange("(k p) (c n) -> p k c n", p=P, n=BW))

            mlp(0, N_F0)
            columns(a["attn_w_qkv"], N_QKV, 0, 6)
            columns(a["attn_w_out"], N_AOUT, 0, 4)
            mlp(1, N_F1)
            sp.wait_ge(sem("attn_split"), QH)
            sp.dma_start(w_lora, w_in[:, 6 * D:6 * D + P].rearrange("(k p) n -> p k n", p=P))\
                .then_inc(sem("lora_landed"), 16)
            sp.dma_start(w2a2[0:64, :], a["rwkv_w2_2"]).then_inc(sem("lora_landed"), 16)
            sp.dma_start(w2a2[64:128, :], a["rwkv_a2_2"]).then_inc(sem("lora_landed"), 16)
            columns(w_in, N_RKV, 3 * D, 12)
            columns(w_in, N_ROG, 6 * D + P, 4)
            columns(a["w_rwkv_out_2"], N_ROUT, 0, 4)
            columns(w_in, N_GR, 8 * D + P, 4)
            columns(w_in, N_CV, 0, 4)
            columns(w_in, N_CG, D, 4)
            columns(w_in, N_COG, 2 * D, 4)
            columns(a["w_conv_out_2"], N_COUT, 0, 4)
            columns(w_in, N_GC, 7 * D + P, 4)
            columns(a["w_out_2"], N_OUT, 0, 4)
            sp.wait_ge(sem("result_ready"), 1)
            sp.dma_start(out, HF[:, :, :]).then_inc(sem("result_stored"), 16)
            sp.wait_ge(sem("result_stored"), 16)

        ada_acc = [flat(40 + 4 * h, 4) for h in range(3)]
        ada_ring = [flat(52 + 4 * h, 4) for h in range(2)]
        ada_tmp = flat(60, 4)
        sc_col = small[:, 0:8]
        ADA_STEPS = 3 + 21 * 2
        ada_v = a["ada_w_2"].rearrange("(k p) (h n) -> p k h n", p=P, h=3)

        @block.gpsimd
        def _(pool):
            ch = Chain(pool, sem("ada_steps"))
            pool.wait_ge(sem("rms_split"), 4 * 2)
            pool.wait_ge(sem("silu_c_ready"), 1)
            for n in range(24):
                k, h = n // 3, n % 3
                if n < 2:
                    pool.dma_start(ada_ring[n], ada_v[:, k, h, :]).then_inc(sem(f"ada_landed{n % 2}"), 16)
            for n in range(24):
                k, h = n // 3, n % 3
                pool.wait_ge(sem(f"ada_landed{n % 2}"), 16 * (n // 2 + 1))
                if k == 0:
                    ch.step(nc.gpsimd.tensor_scalar(ada_acc[h], ada_ring[n % 2], sc_col[:, k:k + 1], None, ALU.mult))
                else:
                    ch.step(nc.gpsimd.tensor_scalar(ada_tmp, ada_ring[n % 2], sc_col[:, k:k + 1], None, ALU.mult))
                    ch.step(nc.gpsimd.tensor_tensor(ada_acc[h], ada_acc[h], ada_tmp, ALU.add))
                if n + 2 < 24:
                    pool.dma_start(ada_ring[n % 2], ada_v[:, (n + 2) // 3, (n + 2) % 3, :])\
                        .then_inc(sem(f"ada_landed{n % 2}"), 16)

        Q, K = tiles(0, 4), tiles(4, 4)
        VT = BIG[:, 1, :, :].rearrange("p (a b) t -> p a (b t)", a=2)
        SG = tiles(16, 8)
        LA = tiles(24, 8)
        QD, KI, KE = tiles(32, 8), tiles(40, 8), tiles(48, 8)
        E1 = HF
        TMP8 = tiles(56, 8)
        OT = tiles(56, 8)
        SF = HF[:, 0:3, :]
        SBK = HF[:, 3:6, :]
        KET = HF[:, 6:8, :].rearrange("p a t -> p (a t)")
        ATT = sb("att", [P, 2, P])
        DEC = small[:, 8:40]
        R16 = U[0:16, 0, :, 1:T + 1]
        CV, CG = tiles(32, 2), tiles(34, 2)
        SGT, HID = tiles(36, 2), tiles(38, 2)

        def kv_piece(q):
            bank, at = [(5, 0), (7, 0), (5, 1), (7, 1), (6, 0), (2, 0)][q]
            return PS[bank][:, at * T:(at + 1) * T]

        QK = tiles(0, 10)
        VA = tiles(16, 2)
        PR, PT = tiles(18, 2), tiles(20, 2)
        SQ10 = tiles(24, 10)
        RKV = tiles(0, 24)
        R_, K_, V_ = tiles(0, 8), tiles(8, 8), tiles(16, 8)
        (SIG, AA, CUM, CEX, EA, EB, EC, ED, KK, K2, BB, TMP) = (flat(40 + j, 1) for j in range(12))
        KR = flat(52, 2).rearrange("p (c s t) -> p c s t", c=NC, s=2)
        BK = flat(54, 2).rearrange("p (c s t) -> p c s t", c=NC, s=2)
        BKE = flat(56, 2).rearrange("p (c s t) -> p c s t", c=NC, s=2)
        SC = [flat(58 + 2 * h, 2).rearrange("p (c n) -> p c n", c=NC) for h in range(2)]
        TK = flat(62, 2).rearrange("p (c n) -> p c n", c=NC)
        XI, XT, YI = (flat(32 + 2 * j, 2)[0:64, :] for j in range(3))
        LM = flat(38, 2)[0:64, :]
        UV = U[:, :, :, :].rearrange("p a b t -> p (a b t)")[:, 0:512].rearrange("p (c h v) -> p c h v", c=NC, h=2)
        ST = ATT[:, 0, :]
        LORA = RS
        RHS = ATT[0:64, 1, :]
        DECR = small[:, 40:44]
        OG = tiles(32, 8)
        YM = tiles(48, 8)
        U31 = flat(0, 9)[:, 0:KT * (T + 30)].rearrange("p (k t) -> p k t", k=KT)
        CONV = tiles(16, 8)
        YC = tiles(24, 8)
        GT = tiles(40, 8)

        @block.tensor
        def _(pe):
            def sums(i):
                for g in range(4):
                    pe.wait_ge(sem("squares_ready"), 4 * i + g + 1)
                    for k in (2 * g, 2 * g + 1):
                        last = nc.tensor.matmul(PS[3][:, 0:T], ones, HF[:, k, :], start=k == 0, stop=k == KT - 1)
                last.then_inc(sem("square_sums"), 1)

            def projected(n0, count, e0, xh, xl, free=None, moving=()):
                for j in range(count):
                    if j >= RING:
                        pe.wait_ge(evacuated, e0 + j - RING + 1)
                    product(pe, n0 + j, (n0 + j) % RING, xh, xl, moving_weights=j in moving)

            def out_projection(n0, a0, xh, xl):
                for j in range(4):
                    if j >= RING:
                        pe.wait_ge(out_added, a0 + j - RING + 1)
                    product(pe, n0 + j, (n0 + j) % RING, xh, xl)

            def mlp(layer, n0, e0):
                g0 = layer * FI
                pe.wait_ge(sem("rms_split"), 4 * (2 * layer + 2))

                def up(n, s, i=0):
                    if s:
                        pe.wait_ge(evacuated, e0 + 2 * s - 1 + 2 * i)
                    product(pe, n, 0, XH, XL, i)
                    if s:
                        pe.wait_ge(evacuated, e0 + 2 * s + 2 * i)
                    product(pe, n + 1, 1, XH, XL, i)

                def down(n, s, i=0, first=False, last=False):
                    pe.wait_ge(w_lo_ready, n + 1 + RING * i)
                    pe.wait_ge(sem("hidden_split"), g0 + s + 1 + i)
                    wh = WH[:, n % RING, :, :].rearrange("p (k c) n -> p k (c n)", k=2)
                    wl = WL[:, n % RING, :, :].rearrange("p (k c) n -> p k (c n)", k=2)
                    for k in range(2):
                        for m in range(KT):
                            ps = PS[4 + m // 2][:, (m % 2) * T:(m % 2 + 1) * T]
                            ms = slice(m * P, (m + 1) * P)
                            start = first and k == 0 and m % 2 == 0
                            stop = last and k == 1
                            nc.tensor.matmul(ps, wh[:, k, ms], GH[:, k, :], start=start, stop=False,
                                             skip_group_check=True)
                            nc.tensor.matmul(ps, wh[:, k, ms], GL[:, k, :], start=False, stop=False,
                                             skip_group_check=True)
                            ins = nc.tensor.matmul(ps, wl[:, k, ms], GH[:, k, :], start=False, stop=stop,
                                                   skip_group_check=True)
                    ins.then_inc(block_done, 1)

                up(n0, 0)
                up(n0 + 2, 1)
                down(n0 + 4, 0, first=True)
                with pe.Fori(1, FI - 1) as i:
                    up(n0 + 2, 1, i)
                    down(n0 + 4, 0, i)
                down(n0 + 3 * FI - 1, FI - 1, last=True)

            pe.wait_ge(consts_landed, 16 * 6)
            sums(0)
            pe.wait_ge(sem("rms_split"), 4)
            for d in range(2):
                for k in range(KT):
                    last = nc.tensor.matmul(PS[3][0:16, d * T:(d + 1) * T], w_r[:, k, 16 * d:16 * d + 16],
                                            HF[:, k, :], start=k == 0, stop=k == KT - 1)
            last.then_inc(sem("rank_rows"), 1)
            pe.wait_ge(sem("rank_rows_taken"), 1)
            for d in range(2):
                for h in range(GH_):
                    last = nc.tensor.matmul(PS[4 + 2 * d + h // 2][:, (h % 2) * T:(h % 2 + 1) * T],
                                            w_up[:, d, h * P:(h + 1) * P], R16[:, d, :], start=True, stop=True)
            last.then_inc(sem("gate_logits"), 1)
            projected(N_GIN, 12, E_GIN, XH, XL, moving=(4, 5, 6, 7))

            def gla_scores(h):
                if h:
                    pe.wait_ge(sem("att_masked"), h)
                for d in range(2):
                    for tt in range(2):
                        ts = slice(tt * P, (tt + 1) * P)
                        last = nc.tensor.matmul(PS[3][:, (2 * d + tt) * P:(2 * d + tt + 1) * P],
                                                KI[:, 4 * d + h, ts], QD[:, 4 * d + h, ts], start=True, stop=True)
                last.then_inc(sem("att_scores"), 1)
                if h:
                    pe.wait_ge(sem("ket_taken"), h)
                for d in range(2):
                    for tt in range(2):
                        last = nc.tensor.transpose(PS[4][:, (2 * d + tt) * P:(2 * d + tt + 1) * P],
                                                   KE[:, 4 * d + h, tt * P:(tt + 1) * P], ident)
                last.then_inc(sem("ke_turned"), 1)

            def gla_states(h):
                pe.wait_ge(sem("ket_taken"), h + 1)
                if h:
                    pe.wait_ge(sem("states_ready"), h)
                for d in range(2):
                    for j in range(3):
                        c = j if d == 0 else 3 - j
                        q = 3 * d + j
                        rows = slice(64 * (c % 2), 64 * (c % 2) + 64)
                        last = nc.tensor.matmul(kv_piece(q),
                                                KET[rows, (2 * d + c // 2) * P:(2 * d + c // 2 + 1) * P],
                                                VT[rows, c // 2, h * 256:(h + 1) * 256], start=True, stop=True)
                last.then_inc(sem("chunk_kv"), 1)

            def gla_out(h):
                bank = PS[h % 2]
                if h >= 2:
                    pe.wait_ge(sem("gla_out_taken"), h - 1)
                pe.wait_ge(sem("att_masked"), h + 1)
                pe.wait_ge(sem("states_ready"), h + 1)
                for v in range(2):
                    c0 = h * 256 + v * P
                    for tt in range(2):
                        nc.tensor.matmul(bank[:, v * T + tt * P:v * T + (tt + 1) * P], VT[:, tt, c0:c0 + P],
                                         ATT[:, tt, :], start=tt == 0, stop=False, skip_group_check=True)
                    for c in range(1, NC):
                        nc.tensor.matmul(bank[:, v * T + c * CH:v * T + (c + 1) * CH],
                                         SF[:, c - 1, v * P:(v + 1) * P], QD[:, h, c * CH:(c + 1) * CH],
                                         start=False, stop=False, skip_group_check=True)
                    for c in range(NC - 1):
                        last = nc.tensor.matmul(bank[:, v * T + c * CH:v * T + (c + 1) * CH],
                                                SBK[:, 2 - c, v * P:(v + 1) * P],
                                                QD[:, 4 + h, c * CH:(c + 1) * CH],
                                                start=False, stop=c == NC - 2, skip_group_check=True)
                last.then_inc(sem("gla_out_summed"), 1)

            pe.wait_ge(sem("gla_decayed"), 1)
            pe.wait_ge(evacuated, E_GIN + 12)
            for h in range(GH_):
                gla_scores(h)
                gla_states(h)
                gla_out(h)
            for h in range(GH_):
                pe.wait_ge(sem("gla_squares"), h + 1)
                for v in range(2):
                    last = nc.tensor.matmul(PS[4 + h // 2][:, (h % 2) * T:(h % 2 + 1) * T], ones,
                                            HF[:, 2 * h + v, :], start=v == 0, stop=v == 1)
            last.then_inc(sem("gla_square_sums"), 1)
            pe.wait_ge(sem("gla_out_split"), 1)
            out_projection(N_GOUT, 0, GH, GL)

            sums(1)
            mlp(0, N_F0, E_F0)

            sums(2)
            pe.wait_ge(sem("rms_split"), 12)
            projected(N_QKV, 6, E_QKV, XH, XL, moving=(5,))
            for g in range(5):
                pe.wait_ge(sem("qk_squares"), g + 1)
                nc.tensor.matmul(PS[3 + g][:, :], ones, SQ10[:, 2 * g:2 * g + 2, :], start=True, stop=True)\
                    .then_inc(sem("qk_square_sums"), 1)
            for g in range(5):
                pe.wait_ge(sem("qk_normed"), g + 1)
                nc.tensor.matmul(PS[3 + g][:, :], rot, QK[:, 2 * g:2 * g + 2, :], start=True, stop=True)\
                    .then_inc(sem("qk_turned"), 1)
            pe.wait_ge(sem("qk_roped"), 5)
            pe.wait_ge(evacuated, E_QKV + 6)

            def attend_scores(h):
                if h >= 2:
                    pe.wait_ge(sem("probs_ready"), h - 1)
                for tt in range(2):
                    last = nc.tensor.matmul(PS[3 + h % 2][:, tt * T:(tt + 1) * T], QK[:, h, tt * P:(tt + 1) * P],
                                            QK[:, 8 + h // 4, :], start=True, stop=True)
                last.then_inc(sem("scores_ready"), 1)

            def attend_out(h):
                pe.wait_ge(sem("probs_ready"), h + 1)
                if h >= 2:
                    pe.wait_ge(sem("probs_t_taken"), h - 1)
                for st in range(2):
                    for tt in range(2):
                        last = nc.tensor.transpose(PS[5 + h % 2][:, st * T + tt * P:st * T + (tt + 1) * P],
                                                   PR[:, tt, st * P:(st + 1) * P], ident)
                last.then_inc(sem("probs_turned"), 1)
                pe.wait_ge(sem("probs_t_taken"), h + 1)
                if h >= 2:
                    pe.wait_ge(sem("attn_split"), h - 1)
                bank = PS[7] if h % 2 else PS[0]
                for st in range(2):
                    last = nc.tensor.matmul(bank[:, 0:T], VA[:, st, (h // 4) * P:(h // 4 + 1) * P], PT[:, st, :],
                                            start=st == 0, stop=st == 1)
                last.then_inc(sem("attn_out"), 1)

            attend_scores(0)
            for h in range(QH):
                if h + 1 < QH:
                    attend_scores(h + 1)
                attend_out(h)
            pe.wait_ge(sem("attn_split"), QH)
            out_projection(N_AOUT, 4, GH, GL)

            sums(3)
            mlp(1, N_F1, E_F1)

            pe.wait_ge(sem("ada_steps"), ADA_STEPS)
            for j in range(24):
                last = nc.tensor.matmul(PS[2][:, j:j + 1], ada_acc[j // 8][:, (j % 8) * P:(j % 8 + 1) * P],
                                        ones[:, 0:1], start=True, stop=True)
            last.then_inc(sem("mod_summed"), 1)
            sums(4)
            pe.wait_ge(sem("rms_split"), 20)

            pe.wait_ge(sem("lora_landed"), 48)
            for k in range(KT):
                last = nc.tensor.matmul(PS[3][:, 0:T], w_lora[:, k, :], HF[:, k, :], start=k == 0, stop=k == KT - 1)
            last.then_inc(sem("lora_rows"), 1)
            projected(N_RKV, 12, E_RKV, XH, XL)
            pe.wait_ge(sem("shifted"), 12)
            pe.wait_ge(sem("lora_ready"), 1)
            for p in range(8):
                if p:
                    pe.wait_ge(sem("sigmoids_ready"), p)
                nc.tensor.matmul(PS[3][:, 0:T], w2a2[0:64, p * P:(p + 1) * P], LORA[0:64, :], start=True, stop=True)
                nc.tensor.matmul(PS[4][:, 0:T], w2a2[64:128, p * P:(p + 1) * P], LORA[64:128, :],
                                 start=True, stop=True).then_inc(sem("pre_acts"), 1)
                pe.wait_ge(sem("kk_squares"), p + 1)
                nc.tensor.matmul(PS[5][:, 0:T], blk, TMP, start=True, stop=True).then_inc(sem("kk_sums"), 1)
                pe.wait_ge(sem("rkrk_ready"), p + 1)
                nc.tensor.matmul(PS[6][:, 0:T], blk, TMP, start=True, stop=True).then_inc(sem("rkrk_sums"), 1)
                if p:
                    pe.wait_ge(sem("o_taken"), p)
                for tt in range(2):
                    last = nc.tensor.transpose(PS[7][:, tt * P:(tt + 1) * P], V_[:, p, tt * P:(tt + 1) * P], ident)
                last.then_inc(sem("v_turned"), 1)
                pe.wait_ge(sem("rwkv_decayed"), p + 1)
                for h in range(2):
                    rows = slice(64 * h, 64 * h + 64)
                    for c in range(NC):
                        last = nc.tensor.matmul(PS[h][:, c * P:(c + 1) * P], BK[rows, c, :, :], KR[rows, c, :, :],
                                                start=True, stop=True)
                last.then_inc(sem("rwkv_scores"), 1)
                pe.wait_ge(sem("bke_ready"), p + 1)
                for c in range(NC):
                    last = nc.tensor.transpose(PS[2][:, c * P:(c + 1) * P], BKE[:, c, :, :], ident)
                last.then_inc(sem("bke_turned"), 1)
                q0 = p * 5
                for lev in range(5):
                    pe.wait_ge(sem("xt_ready"), q0 + lev + 1)
                    if lev == 0:
                        for s in range(8):
                            last = nc.tensor.transpose(PS[3][0:64, s * 64:(s + 1) * 64], XT[:, s * 64:(s + 1) * 64],
                                                       ident[0:64, 0:64])
                        last.then_inc(sem("xt_turned"), 1)
                    pe.wait_ge(sem("x_inv_ready"), q0 + lev + 1)
                    pe.wait_ge(sem("level_ready"), q0 + lev + 1)
                    for s in range(8):
                        ss = slice(s * 64, (s + 1) * 64)
                        last = nc.tensor.matmul(PS[4][0:64, ss], LM[:, ss], XI[:, ss], start=True, stop=True)
                    last.then_inc(sem("y_summed"), 1)
                    pe.wait_ge(sem("y_ready"), q0 + lev + 1)
                    for s in range(8):
                        ss = slice(s * 64, (s + 1) * 64)
                        last = nc.tensor.matmul(PS[5][0:64, ss], YI[:, ss], XT[:, ss], start=True, stop=True)
                        if lev < 4:
                            last = nc.tensor.matmul(PS[6][0:64, ss], XT[:, ss], YI[:, ss], start=True, stop=True)
                    last.then_inc(sem("xy_summed"), 1)
                pe.wait_ge(sem("inverse_ready"), p + 1)
                pe.wait_ge(sem("uv_ready"), p + 1)
                for c in range(NC):
                    r0 = 4 * p + c
                    pe.wait_ge(sem("state_ready"), r0 + 1)
                    nc.tensor.matmul(PS[3][0:64, 0:P], KR[:, c, 0, :], ST, start=True, stop=False,
                                     skip_group_check=True)
                    for h in range(2):
                        last = nc.tensor.matmul(PS[3][0:64, h * 64:(h + 1) * 64], SC[h][:, c, 0:64], UV[:, c, h, :],
                                                start=False, stop=True, skip_group_check=True)
                    last.then_inc(sem("rhs_summed"), 1)
                    pe.wait_ge(sem("rhs_ready"), r0 + 1)
                    for h in range(2):
                        s = h * NC + c
                        last = nc.tensor.matmul(PS[4][0:64, h * 64:(h + 1) * 64], XT[:, s * 64:(s + 1) * 64],
                                                RHS[:, h * 64:(h + 1) * 64], start=True, stop=True)
                    last.then_inc(sem("u_summed"), 1)
                    oc = slice(c * CH, (c + 1) * CH)
                    nc.tensor.matmul(PS[7][:, oc], ST, KR[:, c, 1, :], start=c == 0, stop=False,
                                     skip_group_check=True)
                    pe.wait_ge(sem("u_ready"), r0 + 1)
                    nc.tensor.matmul(PS[5][:, 0:P], TK[:, c, :], UV[:, c, :, :], start=True, stop=True)\
                        .then_inc(sem("update_summed"), 1)
                    for h in range(2):
                        last = nc.tensor.matmul(PS[7][64 * h:64 * h + 64, oc], UV[:, c, h, :], SC[h][:, c, 64:128],
                                                start=False, stop=c == NC - 1, skip_group_check=True)
                last.then_inc(sem("rwkv_out_summed"), 1)
            for k in range(2):
                for g in range(4):
                    if k == 0:
                        pe.wait_ge(sem("o_taken"), 8)
                    else:
                        pe.wait_ge(sem("gn_in"), g + 1)
                    nc.tensor.matmul(PS[3 + g][:, :], blk, R_[:, 2 * g:2 * g + 2, :] if k == 0 else
                                     HF[:, 2 * g:2 * g + 2, :], start=True, stop=True).then_inc(sem("gn_sums"), 1)
            projected(N_ROG, 4, E_ROG, XH, XL)
            pe.wait_ge(sem("rwkv_y_split"), 4)
            out_projection(N_ROUT, 8, GH, GL)
            pe.wait_ge(out_added, 12)
            projected(N_GR, 4, E_GR, XH, XL)
            pe.wait_ge(evacuated, E_GR + 4)
            projected(N_CV, 4, E_CV, XH, XL)
            pe.wait_ge(evacuated, E_CV + 4)
            projected(N_CG, 4, E_CG, XH, XL)
            pe.wait_ge(evacuated, E_CG + 4)
            projected(N_COG, 4, E_COG, XH, XL)
            for k in range(2):
                for g in range(KT):
                    if k == 0:
                        pe.wait_ge(sem("conv_done"), 1)
                    else:
                        pe.wait_ge(sem("ln_in"), g + 1)
                    last = nc.tensor.matmul(PS[3 + k][:, 0:T], ones, CONV[:, g, :] if k == 0 else HF[:, g, :],
                                            start=g == 0, stop=g == KT - 1)
                last.then_inc(sem("ln_sums"), 1)
            pe.wait_ge(sem("conv_y_split"), 4)
            out_projection(N_COUT, 12, GH, GL)
            pe.wait_ge(out_added, 16)
            projected(N_GC, 4, E_GC, XH, XL)
            pe.wait_ge(sem("m_split"), 4)
            out_projection(N_OUT, 16, GH, GL)
            sums(5)

        @block.scalar
        def _(act):
            ch = Chain(act, sem("act_steps"))

            def squares(i):
                if i:
                    act.wait_ge(sem("x_ready"), i)
                for g in range(4):
                    nc.scalar.activation(HF[:, 2 * g:2 * g + 2, :], X[:, 2 * g:2 * g + 2, :], ACT.Square)\
                        .then_inc(sem("squares_ready"), 1)

            def norm_split(i, last=False):
                act.wait_ge(sem("inv_ms_ready"), i + 1)
                nc.scalar.activation(RS[:, :], RS[:, :], ACT.Sqrt).then_inc(sem("rstd_ready"), 1)
                if last:
                    return
                for g in range(4):
                    act.wait_ge(sem("normed"), 4 * i + g + 1)
                    nc.scalar.activation(XH[:, 2 * g:2 * g + 2, :], HF[:, 2 * g:2 * g + 2, :], ACT.Copy)\
                        .then_inc(sem("rms_hi"), 1)

            def take(n, j, e0, dst, func=ACT.Copy, scale=1.0):
                if n + 2 < N_END:
                    split_hi(act, n + 2)
                act.wait_ge(block_done, n + 1)
                src = PS[n % RING][:, :].rearrange("p (m t) -> p m t", m=2)
                nc.scalar.activation(dst, src, func, scale=scale).then_inc(evacuated, 1)

            def split_for_projection(n0):
                for j in range(4):
                    if n0 + j + 2 < N_END:
                        split_hi(act, n0 + j + 2)

            def hidden_hi(g0, s, i=0):
                act.wait_ge(sem("gate_convolved"), g0 + s + 1 + i)
                nc.scalar.activation(SGT, CG, ACT.Silu).then_inc(sem("gate_silu"), 1)

            def hidden_copy(g0, s, n, i=0):
                act.wait_ge(sem("hidden_ready"), g0 + s + 1 + i)
                nc.scalar.activation(GH[:, 0:2, :], HID, ACT.Copy).then_inc(sem("hidden_hi"), 1)

            def mlp(layer, n0):
                g0 = layer * FI

                def take_val(n, s, i=0):
                    act.wait_ge(block_done, n + 1 + RING * i)
                    if s:
                        act.wait_ge(sem("val_convolved"), g0 + s + i)
                    nc.scalar.activation(U[:, 0, :, 1:T + 1], PS[0][:, :].rearrange("p (m t) -> p m t", m=2),
                                         ACT.Copy).then_inc(evacuated, 1)

                def take_gate(n, s, i=0):
                    act.wait_ge(block_done, n + 1 + RING * i)
                    if s:
                        act.wait_ge(sem("gate_convolved"), g0 + s + i)
                    nc.scalar.activation(U[:, 1, :, 1:T + 1], PS[1][:, :].rearrange("p (m t) -> p m t", m=2),
                                         ACT.Copy).then_inc(evacuated, 1)

                act.wait_ge(sem("u_zeroed"), 1)
                split_hi(act, n0 + 2)
                take_val(n0, 0)
                split_hi(act, n0 + 3)
                take_gate(n0 + 1, 0)
                with act.Fori(0, FI - 1) as i:
                    split_hi(act, n0 + 4, i)
                    hidden_hi(g0, 0, i)
                    take_val(n0 + 2, 1, i)
                    act.wait_ge(block_done, n0 + 2 + RING * i)
                    hidden_copy(g0, 0, n0, i)
                    split_hi(act, n0 + 5, i)
                    take_gate(n0 + 3, 1, i)
                    split_hi(act, n0 + 6, i)
                hidden_hi(g0, FI - 1)
                act.wait_ge(block_done, n0 + 3 * FI - 1)
                hidden_copy(g0, FI - 1, n0)
                split_hi(act, n0 + 3 * FI + 1)

            act.wait_ge(consts_landed, 16 * 6)
            split_hi(act, 0)
            split_hi(act, 1)
            squares(0)
            nc.scalar.activation(small[:, 0:8], vec("c_2", 0, 8), ACT.Silu).then_inc(sem("silu_c_ready"), 1)
            norm_split(0)
            act.wait_ge(sem("rank_rows"), 1)
            nc.scalar.activation(R16, PS[3][0:16, :].rearrange("p (d t) -> p d t", d=2), ACT.Copy)\
                .then_inc(sem("rank_rows_taken"), 1)
            act.wait_ge(sem("gate_logits"), 1)
            for d in range(2):
                name = "gla_b_gate_b" if d else "gla_b_gate_f"
                for h in range(GH_):
                    last = nc.scalar.activation(LA[:, 4 * d + h, :], PS[4 + 2 * d + h // 2][:, (h % 2) * T:(h % 2 + 1) * T],
                                                ACT.Identity, bias=vec(name, h))
            ch.step(last)
            ch.step(nc.scalar.activation(TMP8, LA, ACT.Abs))
            ch.step(nc.scalar.activation(TMP8, TMP8, ACT.Exp, scale=-1.0))
            nc.scalar.activation(TMP8, TMP8, ACT.Ln, bias=1.0).then_inc(sem("softplus_ready"), 1)
            for j in range(2):
                take(N_GIN + j, j, E_GIN, Q[:, 2 * j:2 * j + 2, :], scale=float(P) ** -0.5)
            for j in range(2):
                take(N_GIN + 2 + j, j, E_GIN, K[:, 2 * j:2 * j + 2, :])
            act.wait_ge(sem("gla_sums_ready"), 1)
            nc.scalar.activation(QD, HF, ACT.Exp, scale=1.0 / 16).then_inc(sem("gla_exps"), 1)
            nc.scalar.activation(KI, HF, ACT.Exp, scale=-1.0 / 16).then_inc(sem("gla_exps"), 1)
            nc.scalar.activation(DEC[:, 0:16].rearrange("p (h c) -> p h c", c=NC),
                                 HF[:, 0:4, CH - 1:T:CH], ACT.Exp, scale=1.0 / 16)
            nc.scalar.activation(DEC[:, 16:32].rearrange("p (h c) -> p h c", c=NC),
                                 HF[:, 4:8, 0:T:CH], ACT.Exp, scale=1.0 / 16)
            act.wait_ge(sem("gla_to_end"), 1)
            nc.scalar.activation(KE, KE, ACT.Exp, scale=1.0 / 16).then_inc(sem("gla_exps"), 1)
            for j in range(4):
                take(N_GIN + 4 + j, j, E_GIN, VT[:, :, j * 256:(j + 1) * 256])
            for j in range(4):
                take(N_GIN + 8 + j, j, E_GIN, SG[:, 2 * j:2 * j + 2, :], ACT.Silu)
            for h in range(GH_):
                act.wait_ge(sem("ke_turned"), h + 1)
                if h:
                    act.wait_ge(sem("chunk_kv"), h)
                else:
                    act.wait_ge(sem("gla_decayed"), 1)
                nc.scalar.activation(KET, PS[4][:, :], ACT.Copy).then_inc(sem("ket_taken"), 1)
                act.wait_ge(sem("gla_out_summed"), h + 1)
                nc.scalar.activation(OT[:, 2 * h:2 * h + 2, :], PS[h % 2][:, :].rearrange("p (v t) -> p v t", v=2),
                                     ACT.Copy).then_inc(sem("gla_out_taken"), 1)
            for h in range(GH_):
                act.wait_ge(sem("gla_out_taken"), h + 1)
                nc.scalar.activation(HF[:, 2 * h:2 * h + 2, :], OT[:, 2 * h:2 * h + 2, :], ACT.Square)\
                    .then_inc(sem("gla_squares"), 1)
            act.wait_ge(sem("gla_inv_ms"), 1)
            nc.scalar.activation(tiles(0, 4), tiles(0, 4), ACT.Sqrt).then_inc(sem("gla_rstd"), 1)
            act.wait_ge(sem("gla_out_normed"), 1)
            nc.scalar.activation(GH[:, :, :], OT, ACT.Copy).then_inc(sem("gla_out_hi"), 1)
            split_for_projection(N_GOUT)

            squares(1)
            norm_split(1)
            mlp(0, N_F0)

            squares(2)
            norm_split(2)
            for j in range(5):
                take(N_QKV + j, j, E_QKV, QK[:, 2 * j:2 * j + 2, :])
            take(N_QKV + 5, 5, E_QKV, VA)
            act.wait_ge(evacuated, E_QKV + 5)
            for g in range(5):
                nc.scalar.activation(SQ10[:, 2 * g:2 * g + 2, :], QK[:, 2 * g:2 * g + 2, :], ACT.Square)\
                    .then_inc(sem("qk_squares"), 1)
            for g in range(5):
                act.wait_ge(sem("qk_inv_ms"), g + 1)
                nc.scalar.activation(SQ10[:, 2 * g:2 * g + 2, :], SQ10[:, 2 * g:2 * g + 2, :], ACT.Sqrt)\
                    .then_inc(sem("qk_rstd"), 1)
            for h in range(QH):
                act.wait_ge(sem("neg_max_ready"), h + 1)
                if h:
                    act.wait_ge(sem("probs_turned"), h)
                for tt in range(2):
                    last = nc.scalar.activation(PR[:, tt, :], PS[3 + h % 2][:, tt * T:(tt + 1) * T], ACT.Exp,
                                                bias=small[:, 44 + 2 * (h % 2) + tt:45 + 2 * (h % 2) + tt],
                                                scale=float(P) ** -0.5,
                                                accum_out=small[:, 48 + 2 * (h % 2) + tt:49 + 2 * (h % 2) + tt])
                last.then_inc(sem("exps_ready"), 1)
                act.wait_ge(sem("probs_turned"), h + 1)
                if h:
                    act.wait_ge(sem("attn_out"), h)
                nc.scalar.activation(PT, PS[5 + h % 2][:, :].rearrange("p (s q) -> p s q", s=2), ACT.Copy)\
                    .then_inc(sem("probs_t_taken"), 1)
                act.wait_ge(sem("attn_out"), h + 1)
                nc.scalar.activation(GH[:, h, :], (PS[7] if h % 2 else PS[0])[:, 0:T], ACT.Copy)\
                    .then_inc(sem("attn_hi"), 1)
            split_for_projection(N_AOUT)

            squares(3)
            norm_split(3)
            mlp(1, N_F1)

            squares(4)
            norm_split(4)
            act.wait_ge(sem("lora_rows"), 1)
            act.wait_ge(sem("gate_convolved"), 2 * FI)
            nc.scalar.activation(U[:, 0, 0, 1:T + 1], PS[3][:, 0:T], ACT.Copy).then_inc(sem("lora_taken"), 1)
            act.wait_ge(sem("lora_shifted"), 1)
            ch.step(nc.scalar.activation(LORA[0:64, :], LORA[0:64, :], ACT.Tanh))
            for j in range(12):
                n = N_RKV + j
                split_hi(act, n + 2)
                act.wait_ge(block_done, n + 1)
                if j > 1:
                    act.wait_ge(sem("shifted"), j - 1)
                nc.scalar.activation(U[:, 1 - j % 2, :, 1:T + 1],
                                     PS[n % RING][:, :].rearrange("p (m t) -> p m t", m=2), ACT.Copy)\
                    .then_inc(evacuated, 1)
            for p in range(8):
                act.wait_ge(sem("pre_acts"), p + 1)
                if p:
                    act.wait_ge(sem("rwkv_decayed"), p)
                nc.scalar.activation(SIG, PS[3][:, 0:T], ACT.Sigmoid, bias=vec("rwkv_w0_2", p))
                nc.scalar.activation(AA, PS[4][:, 0:T], ACT.Sigmoid, bias=vec("rwkv_a0_2", p))\
                    .then_inc(sem("sigmoids_ready"), 1)
                act.wait_ge(sem("kk_inv_ready"), p + 1)
                nc.scalar.activation(EA, BB, ACT.Sqrt).then_inc(sem("kk_rsqrt"), 1)
                act.wait_ge(sem("cums_ready"), p + 1)
                nc.scalar.activation(EA, CUM, ACT.Exp, scale=DECAY)
                nc.scalar.activation(EB, CEX, ACT.Exp, scale=DECAY)
                nc.scalar.activation(EC, CUM, ACT.Exp, scale=-DECAY)
                nc.scalar.activation(DECR, CUM[:, CH - 1:T:CH], ACT.Exp, scale=DECAY)
                nc.scalar.activation(ED, SIG, ACT.Exp, scale=DECAY).then_inc(sem("rwkv_exps"), 1)
                act.wait_ge(sem("v_turned"), p + 1)
                act.wait_ge(sem("uv_zeroed"), p + 1)
                for c in range(NC):
                    r = 64 * (c % 2)
                    nc.scalar.activation(UV[64:128, c, :, :],
                                         PS[7][r:r + 64, (c // 2) * P:(c // 2 + 1) * P].rearrange("p (h v) -> p h v", h=2),
                                         ACT.Copy)
                act.wait_ge(sem("bke_turned"), p + 1)
                nc.scalar.activation(TK, PS[2][:, :].rearrange("p (c n) -> p c n", c=NC), ACT.Copy)\
                    .then_inc(sem("uv_ready"), 1)
                act.wait_ge(sem("xt_turned"), p + 1)
                nc.scalar.activation(XI, PS[3][0:64, :], ACT.Copy).then_inc(sem("x_inv_ready"), 1)
                for lev in range(5):
                    act.wait_ge(sem("y_summed"), 5 * p + lev + 1)
                    nc.scalar.activation(YI, PS[4][0:64, :], ACT.Copy).then_inc(sem("y_ready"), 1)
                for c in range(NC):
                    act.wait_ge(sem("u_summed"), 4 * p + c + 1)
                    nc.scalar.activation(UV[0:64, c, :, :], PS[4][0:64, 0:P].rearrange("p (h v) -> p h v", h=2),
                                         ACT.Copy, scale=-1.0).then_inc(sem("u_ready"), 1)
                act.wait_ge(sem("rwkv_out_summed"), p + 1)
                nc.scalar.activation(R_[:, p, :], PS[7][:, 0:T], ACT.Copy).then_inc(sem("o_taken"), 1)
            for g in range(4):
                act.wait_ge(sem("gn_centred"), g + 1)
                nc.scalar.activation(HF[:, 2 * g:2 * g + 2, :], R_[:, 2 * g:2 * g + 2, :], ACT.Square)\
                    .then_inc(sem("gn_in"), 1)
            act.wait_ge(sem("gn_inv_var"), 1)
            nc.scalar.activation(HF[:, :, :], HF[:, :, :], ACT.Sqrt).then_inc(sem("gn_rstd"), 1)
            for j in range(4):
                take(N_ROG + j, j, E_ROG, OG[:, 2 * j:2 * j + 2, :], ACT.Silu)
            for g in range(4):
                act.wait_ge(sem("rwkv_y_ready"), g + 1)
                nc.scalar.activation(GH[:, 2 * g:2 * g + 2, :], R_[:, 2 * g:2 * g + 2, :], ACT.Copy)\
                    .then_inc(sem("rwkv_y_hi"), 1)
            split_for_projection(N_ROUT)
            for j in range(4):
                take(N_GR + j, j, E_GR, GT[:, 2 * j:2 * j + 2, :], ACT.Sigmoid)
            act.wait_ge(sem("u31_zeroed"), 1)
            for j in range(4):
                take(N_CV + j, j, E_CV, U31[:, 2 * j:2 * j + 2, 30:], ACT.Copy)
            act.wait_ge(sem("gate_r_applied"), 1)
            for j in range(4):
                take(N_CG + j, j, E_CG, GT[:, 2 * j:2 * j + 2, :], ACT.Sigmoid)
            for j in range(4):
                take(N_COG + j, j, E_COG, OG[:, 2 * j:2 * j + 2, :], ACT.Silu)
            for g in range(KT):
                act.wait_ge(sem("conv_centred"), g + 1)
                nc.scalar.activation(HF[:, g, :], CONV[:, g, :], ACT.Square).then_inc(sem("ln_in"), 1)
            act.wait_ge(sem("ln_inv_var"), 1)
            nc.scalar.activation(RS[:, :], RS[:, :], ACT.Sqrt).then_inc(sem("ln_rstd"), 1)
            for g in range(KT):
                act.wait_ge(sem("conv_normed"), g + 1)
                nc.scalar.activation(CONV[:, g, :], CONV[:, g, :], ACT.Silu).then_inc(sem("conv_silu"), 1)
            for g in range(4):
                act.wait_ge(sem("conv_y_ready"), g + 1)
                nc.scalar.activation(GH[:, 2 * g:2 * g + 2, :], CONV[:, 2 * g:2 * g + 2, :], ACT.Copy)\
                    .then_inc(sem("conv_y_hi"), 1)
            split_for_projection(N_COUT)
            for j in range(4):
                take(N_GC + j, j, E_GC, GT[:, 2 * j:2 * j + 2, :], ACT.Sigmoid)
            for g in range(4):
                act.wait_ge(sem("m_ready"), g + 1)
                nc.scalar.activation(GH[:, 2 * g:2 * g + 2, :], YM[:, 2 * g:2 * g + 2, :], ACT.Copy)\
                    .then_inc(sem("m_hi"), 1)
            split_for_projection(N_OUT)
            squares(5)
            norm_split(5, last=True)

        @block.vector
        def _(dve):
            ch = Chain(dve, sem("dve_steps"))
            v = nc.vector

            def spread(ap, shape):
                return ap.broadcast_to(shape)

            def inverse_of(dst, sums, scale, eps, name):
                ch.step(v.tensor_scalar(dst, sums, scale, eps, ALU.mult, ALU.add))
                v.reciprocal(dst, dst).then_inc(sem(name), 1)

            def norm(i, w, modulate=False, last=False):
                dve.wait_ge(sem("square_sums"), i + 1)
                inverse_of(RS[:, :], PS[3][:, 0:T], 1.0 / D, EPS, "inv_ms_ready")
                dve.wait_ge(sem("rstd_ready"), i + 1)
                for g in range(4):
                    for k in (2 * g, 2 * g + 1):
                        ins = v.scalar_tensor_tensor(HF[:, k, :], X[:, k, :], vec(*w(k)), RS[:, :], ALU.mult, ALU.mult)
                        if modulate:
                            ch.step(ins)
                            ins = v.tensor_scalar(HF[:, k, :], HF[:, k, :], mod[:, 24 + k:25 + k], mod[:, k:k + 1],
                                                  ALU.mult, ALU.add)
                    ins.then_inc(sem("normed"), 1)
                if last:
                    return
                for g in range(4):
                    gs = slice(2 * g, 2 * g + 2)
                    dve.wait_ge(sem("rms_hi"), 4 * i + g + 1)
                    v.tensor_tensor(XL[:, gs, :], HF[:, gs, :], XH[:, gs, :].bitcast(F32), ALU.subtract)\
                        .then_inc(sem("rms_split"), 1)

            def lo(n):
                if n < N_END:
                    split_lo(dve, n)

            def add_projection(n0, a0, dst, add=True):
                for j in range(4):
                    lo(n0 + j + 2)
                    dve.wait_ge(block_done, n0 + j + 1)
                    ps = PS[(n0 + j) % RING][:, :].rearrange("p (m t) -> p m t", m=2)
                    d = dst[:, 2 * j:2 * j + 2, :]
                    if add:
                        ins = v.tensor_tensor(d, d, ps, ALU.add)
                    else:
                        ins = v.tensor_copy(d, ps)
                    ins.then_inc(out_added, 1)

            def mlp(layer, n0, e0):
                g0 = layer * FI
                cw, cb = COL["ffn_w_conv"] + 132 * layer, COL["ffn_b_conv"] + 44 * layer

                def tap(j, half, s, m, i):
                    base = (cb if j is None else cw + 44 * j) + 22 * half + 2 * s + m
                    return V[:, bass.ds(i * 2 + base, 1)] if not isinstance(i, int) else V[:, base:base + 1]

                def convolve(dst, half, s, ch, i=0):
                    for m in range(2):
                        ch.done(v.tensor_scalar(dst[:, m, :], U[:, half, m, 1:T + 1], tap(1, half, s, m, i),
                                                tap(None, half, s, m, i), ALU.mult, ALU.add))
                    for j, at in ((0, 0), (2, 2)):
                        for m in range(2):
                            ch.all(1)
                            ins = v.scalar_tensor_tensor(dst[:, m, :], U[:, half, m, at:at + T],
                                                         tap(j, half, s, m, i), dst[:, m, :], ALU.mult, ALU.add)
                            if j == 2 and m == 1:
                                ins.then_inc(sem("gate_convolved" if half else "val_convolved"), 1)
                            else:
                                ch.done(ins)

                def hidden(s, i=0):
                    dve.wait_ge(sem("gate_silu"), g0 + s + 1 + i)
                    if s or not isinstance(i, int):
                        dve.wait_ge(sem("val_convolved"), g0 + s + 1 + i)
                    v.tensor_tensor(HID, SGT, CV, ALU.mult).then_inc(sem("hidden_ready"), 1)
                    dve.wait_ge(sem("hidden_hi"), g0 + s + 1 + i)
                    v.tensor_tensor(GL[:, 0:2, :], HID, GH[:, 0:2, :].bitcast(F32), ALU.subtract)\
                        .then_inc(sem("hidden_split"), 1)

                split_lo(dve, n0 + 2)
                dve.wait_ge(evacuated, e0 + 1)
                convolve(CV, 0, 0, ch)
                split_lo(dve, n0 + 3)
                dve.wait_ge(evacuated, e0 + 2)
                convolve(CG, 1, 0, ch)
                with dve.Fori(0, FI - 1) as i:
                    ch.enter(i, 10)
                    split_lo(dve, n0 + 4, i)
                    hidden(0, i)
                    dve.wait_ge(evacuated, e0 + 3 + 2 * i)
                    convolve(CV, 0, 1, ch, i)
                    split_lo(dve, n0 + 5, i)
                    dve.wait_ge(evacuated, e0 + 4 + 2 * i)
                    convolve(CG, 1, 1, ch, i)
                    split_lo(dve, n0 + 6, i)
                ch.leave(FI - 1)
                hidden(FI - 1)
                split_lo(dve, n0 + 3 * FI + 1)
                dve.wait_ge(block_done, n0 + 3 * FI)
                for q in range(4):
                    x = X[:, 2 * q:2 * q + 2, :]
                    ins = v.tensor_tensor(x, x, PS[4 + q][:, :].rearrange("p (m t) -> p m t", m=2), ALU.add)
                ins.then_inc(sem("x_ready"), 1)

            ch.done(v.memset(ATT[:, :, :], 0.0))
            ch.done(v.memset(U[:, :, :, 0:1], 0.0))
            ch.step(v.memset(U[:, :, :, T + 1:T + 2], 0.0))
            dve.sem_inc(sem("u_zeroed"), 1)
            dve.wait_ge(consts_landed, 16 * 6)
            lo(0)
            lo(1)
            norm(0, lambda k: ("norm_mix", k))
            dve.wait_ge(sem("softplus_ready"), 1)
            ch.step(v.scalar_tensor_tensor(LA, LA, 0.0, TMP8, ALU.min, ALU.subtract))
            dve.wait_ge(sem("rank_rows"), 1)
            for t in range(8):
                ins = v.tensor_tensor_scan(HF[:, t, :], cst("scan"), LA[:, t, :], 0.0, ALU.mult, ALU.add)
            ch.step(ins)

            def chunks(ap):
                return ap.rearrange("p k (c t) -> p (k c) t", t=CH)

            hf, hb = chunks(HF[:, 0:4, :]), chunks(HF[:, 4:8, :])
            shape = [P, 16, CH]
            ch.step(v.tensor_tensor(chunks(TMP8[:, 0:4, :]), spread(hb[:, :, CH - 1:CH], shape), hb, ALU.subtract))
            ins = v.tensor_tensor(HF[:, 4:8, :], TMP8[:, 0:4, :], LA[:, 4:8, :], ALU.add)
            ins.then_inc(sem("gla_sums_ready"), 1)
            dve.wait_ge(sem("gla_sums_ready"), 1)
            v.tensor_tensor(chunks(KE[:, 0:4, :]), spread(hf[:, :, CH - 1:CH], shape), hf, ALU.subtract)
            v.tensor_tensor(chunks(KE[:, 4:8, :]), spread(hb[:, :, 0:1], shape), hb, ALU.subtract)\
                .then_inc(sem("gla_to_end"), 1)
            for n in range(2, 6):
                lo(n)
            dve.wait_ge(evacuated, E_GIN + 4)
            for e, (dst, src) in enumerate(((QD, Q), (KI, K), (KE, K))):
                dve.wait_ge(sem("gla_exps"), e + 1)
                for d in range(2):
                    ins = v.tensor_tensor(dst[:, 4 * d:4 * d + 4, :], dst[:, 4 * d:4 * d + 4, :], src, ALU.mult)
            ins.then_inc(sem("gla_decayed"), 1)
            for n in range(6, 14):
                lo(n)
            for h in range(GH_):
                dve.wait_ge(sem("att_scores"), h + 1)
                if h:
                    dve.wait_ge(sem("gla_out_summed"), h)
                for d, m in enumerate(("mask_f", "mask_b")):
                    mask = cst(m).bitcast(I32).unsqueeze(1)
                    ins = v.copy_predicated(ATT[:, :, :], spread(mask, [P, 2, P]),
                                            PS[3][:, 2 * d * P:(2 * d + 2) * P].rearrange("p (a b) -> p a b", a=2))
                    if d == 0:
                        ch.step(ins)
                ins.then_inc(sem("att_masked"), 1)
                dve.wait_ge(sem("chunk_kv"), h + 1)

                def decay(d, c):
                    j = 16 * d + 4 * h + c
                    return DEC[:, j:j + 1]

                ch.done(v.tensor_copy(SF[:, 0, :], kv_piece(0)))
                ch.done(v.tensor_copy(SBK[:, 0, :], kv_piece(3)))
                for j in range(1, 3):
                    ch.all(1)
                    ch.done(v.scalar_tensor_tensor(SF[:, j, :], SF[:, j - 1, :], decay(0, j), kv_piece(j), ALU.mult, ALU.add))
                    ch.all(1)
                    ins = v.scalar_tensor_tensor(SBK[:, j, :], SBK[:, j - 1, :], decay(1, 3 - j), kv_piece(3 + j),
                                                 ALU.mult, ALU.add)
                    if j == 1:
                        ch.done(ins)
                ins.then_inc(sem("states_ready"), 1)
            dve.wait_ge(sem("gla_square_sums"), 1)
            r4 = tiles(0, 4)
            for q in range(2):
                ins = v.tensor_scalar(r4[:, 2 * q:2 * q + 2, :], PS[4 + q][:, :].rearrange("p (m t) -> p m t", m=2),
                                      1.0 / 256, EPS, ALU.mult, ALU.add)
            ch.step(ins)
            v.reciprocal(r4, r4).then_inc(sem("gla_inv_ms"), 1)
            dve.wait_ge(sem("gla_rstd"), 1)
            for w in range(2):
                o = OT.rearrange("p (h w) t -> p h w t", w=2)[:, :, w, :]
                ins = v.scalar_tensor_tensor(o, o, vec("gla_norm", w), r4, ALU.mult, ALU.mult)
            ch.step(ins)
            v.tensor_tensor(OT, OT, SG, ALU.mult).then_inc(sem("gla_out_normed"), 1)
            dve.wait_ge(sem("gla_out_hi"), 1)
            v.tensor_tensor(GL[:, :, :], OT, GH[:, :, :].bitcast(F32), ALU.subtract).then_inc(sem("gla_out_split"), 1)
            add_projection(N_GOUT, 0, X)
            dve.wait_ge(out_added, 4)
            dve.sem_inc(sem("x_ready"), 1)

            norm(1, lambda k: ("norm_ffn", k))
            mlp(0, N_F0, E_F0)

            norm(2, lambda k: ("norm_mix", 8 + k))
            for n in range(N_QKV + 2, N_QKV + 8):
                lo(n)
            for g in range(5):
                dve.wait_ge(sem("qk_square_sums"), g + 1)
                inverse_of(SQ10[:, 2 * g:2 * g + 2, :], PS[3 + g][:, :].rearrange("p (m t) -> p m t", m=2),
                           1.0 / P, EPS, "qk_inv_ms")
            for g in range(5):
                gs = slice(2 * g, 2 * g + 2)
                dve.wait_ge(sem("qk_rstd"), g + 1)
                v.scalar_tensor_tensor(QK[:, gs, :], QK[:, gs, :], vec("attn_k_norm" if g == 4 else "attn_q_norm"),
                                       SQ10[:, gs, :], ALU.mult, ALU.mult).then_inc(sem("qk_normed"), 1)
            for g in range(5):
                gs = slice(2 * g, 2 * g + 2)
                hs = slice(2 * (g % 4), 2 * (g % 4) + 2)
                dve.wait_ge(sem("qk_turned"), g + 1)
                two = [P, 2, T]
                ch.done(v.tensor_tensor(HF[:, hs, :], PS[3 + g][:, :].rearrange("p (m t) -> p m t", m=2),
                                        spread(cst("sin").unsqueeze(1), two), ALU.mult))
                ch.step(v.tensor_tensor(QK[:, gs, :], QK[:, gs, :], spread(cst("cos").unsqueeze(1), two), ALU.mult))
                v.tensor_tensor(QK[:, gs, :], QK[:, gs, :], HF[:, hs, :], ALU.add).then_inc(sem("qk_roped"), 1)
            for h in range(QH):
                dve.wait_ge(sem("scores_ready"), h + 1)
                mx = small[:, 44 + 2 * (h % 2):46 + 2 * (h % 2)]
                den = small[:, 48 + 2 * (h % 2):50 + 2 * (h % 2)]
                ch.step(v.tensor_reduce(mx, PS[3 + h % 2][:, :].rearrange("p (m t) -> p m t", m=2), AX_X, ALU.max))
                v.tensor_scalar(mx, mx, -float(P) ** -0.5, None, ALU.mult).then_inc(sem("neg_max_ready"), 1)
                dve.wait_ge(sem("exps_ready"), h + 1)
                ch.step(v.reciprocal(den, den))
                for tt in range(2):
                    ins = v.tensor_scalar(PR[:, tt, :], PR[:, tt, :], den[:, tt:tt + 1], None, ALU.mult)
                ins.then_inc(sem("probs_ready"), 1)
                dve.wait_ge(sem("attn_hi"), h + 1)
                v.tensor_tensor(GL[:, h, :], (PS[7] if h % 2 else PS[0])[:, 0:T], GH[:, h, :].bitcast(F32),
                                ALU.subtract).then_inc(sem("attn_split"), 1)
            add_projection(N_AOUT, 4, X)
            dve.wait_ge(out_added, 8)
            dve.sem_inc(sem("x_ready"), 1)

            norm(3, lambda k: ("norm_ffn", 8 + k))
            mlp(1, N_F1, E_F1)

            dve.wait_ge(sem("mod_summed"), 1)
            ch.step(v.tensor_tensor(mod[:, 0:24], PS[2][:, 0:24], vec("ada_b_2", 0, 24), ALU.add))
            ch.step(v.tensor_scalar(mod[:, 24:32], mod[:, 8:16], 1.0, None, ALU.add))
            norm(4, lambda k: ("norm_g_2", k), modulate=True)

            def shift(dst, half, mu0, name, m_count=2):
                z, before = U[:, half, 0:m_count, 1:T + 1], U[:, half, 0:m_count, 0:T]
                ch.step(v.tensor_tensor(dst, before, z, ALU.subtract))
                for m in range(m_count):
                    ins = v.scalar_tensor_tensor(dst[:, m, :], dst[:, m, :], vec("rwkv_mu_2", mu0 + m), z[:, m, :],
                                                 ALU.mult, ALU.add)
                ins.then_inc(sem(name), 1)

            dve.wait_ge(sem("lora_taken"), 1)
            shift(LORA[:, :].unsqueeze(1), 0, 24, "lora_shifted", 1)
            for j in range(12):
                lo(N_RKV + j + 2)
                dve.wait_ge(evacuated, E_RKV + j + 1)
                shift(RKV[:, 2 * j:2 * j + 2, :], 1 - j % 2, 2 * j, "shifted")
            dve.wait_ge(sem("act_steps"), 4)
            dve.sem_inc(sem("lora_ready"), 1)

            def ck(ap):
                return ap.rearrange("p (c t) -> p c t", c=NC)

            def systems(ap, h):
                return ap[:, h * 256:(h + 1) * 256].rearrange("p (c t) -> p c t", c=NC)

            lev_shape = [64, NC, 64]
            for p in range(8):
                ch.step(v.tensor_scalar(KK, K_[:, p, :], vec("rwkv_k_k_2", p), None, ALU.mult))
                if p:
                    dve.wait_ge(sem("rwkv_out_summed"), p)
                v.tensor_tensor(TMP, KK, KK, ALU.mult).then_inc(sem("kk_squares"), 1)
                dve.wait_ge(sem("kk_sums"), p + 1)
                ch.step(v.tensor_scalar(BB, PS[5][:, 0:T], 1e-24, None, ALU.max))
                v.reciprocal(BB, BB).then_inc(sem("kk_inv_ready"), 1)
                dve.wait_ge(sem("sigmoids_ready"), p + 1)
                ch.step(v.tensor_scalar(K2, AA, -1.0, vec("rwkv_k_a_2", p), ALU.add, ALU.mult))
                ch.step(v.scalar_tensor_tensor(K2, K2, 1.0, K_[:, p, :], ALU.add, ALU.mult))
                v.scalar_tensor_tensor(TMP, R_[:, p, :], vec("rwkv_r_k_2", p), K2, ALU.mult, ALU.mult)\
                    .then_inc(sem("rkrk_ready"), 1)
                ch.step(v.tensor_tensor_scan(CUM, cst("scan"), SIG, 0.0, ALU.mult, ALU.add))
                ch.step(v.tensor_tensor(CEX, CUM, SIG, ALU.subtract))
                dve.wait_ge(sem("kk_rsqrt"), p + 1)
                ch.step(v.tensor_tensor(KK, KK, EA, ALU.mult))
                v.tensor_tensor(ck(SIG), spread(ck(CUM)[:, :, CH - 1:CH], [P, NC, CH]), ck(CUM), ALU.subtract)\
                    .then_inc(sem("cums_ready"), 1)
                ch.step(v.tensor_tensor(BB, KK, AA, ALU.mult))
                dve.wait_ge(sem("rwkv_exps"), p + 1)
                v.tensor_tensor(KR[:, :, 0, :], ck(KK), ck(EB), ALU.mult)
                v.tensor_tensor(KR[:, :, 1, :], ck(R_[:, p, :]), ck(EA), ALU.mult)
                v.tensor_tensor(BK[:, :, 0, :], ck(BB), ck(EC), ALU.mult)
                v.tensor_tensor(BK[:, :, 1, :], ck(K2), ck(EC), ALU.mult).then_inc(sem("rwkv_decayed"), 1)
                v.tensor_tensor(BKE[:, :, 0, :], ck(BB), ck(ED), ALU.mult)
                v.tensor_tensor(BKE[:, :, 1, :], ck(K2), ck(ED), ALU.mult).then_inc(sem("bke_ready"), 1)
                dve.wait_ge(sem("rkrk_sums"), p + 1)
                v.tensor_tensor(K_[:, p, :], PS[6][:, 0:T], V_[:, p, :], ALU.mult)
                v.memset(UV[0:64, :, :, :], 0.0).then_inc(sem("uv_zeroed"), 1)
                v.memset(ST, 0.0).then_inc(sem("state_ready"), 1)
                dve.wait_ge(sem("rwkv_scores"), p + 1)
                for h in range(2):
                    ins = v.tensor_tensor(SC[h], PS[h][:, :].rearrange("p (c n) -> p c n", c=NC),
                                          spread(cst("scmask").unsqueeze(1), [P, NC, P]), ALU.mult)
                ch.step(ins)

                def level(lev):
                    m = spread(cst("lev")[0:64, 64 * lev:64 * (lev + 1)].unsqueeze(1), lev_shape)
                    for h in range(2):
                        ins = v.tensor_tensor(systems(LM, h), SC[h][0:64, :, 0:64], m, ALU.mult)
                    return ins

                ch.step(level(0))
                for h in range(2):
                    ins = v.tensor_tensor(systems(XT, h), spread(ident[0:64, 0:64].unsqueeze(1), lev_shape),
                                          systems(LM, h), ALU.subtract)
                ins.then_inc(sem("xt_ready"), 1)
                dve.wait_ge(sem("xt_ready"), 5 * p + 1)
                for lev in range(5):
                    q = 5 * p + lev + 1
                    if lev:
                        dve.wait_ge(sem("y_summed"), q - 1)
                    level(lev + 1).then_inc(sem("level_ready"), 1)
                    dve.wait_ge(sem("xy_summed"), q)
                    v.tensor_tensor(XT, XT, PS[5][0:64, :], ALU.subtract)\
                        .then_inc(sem("xt_ready" if lev < 4 else "inverse_ready"), 1)
                    if lev < 4:
                        v.tensor_tensor(XI, XI, PS[6][0:64, :], ALU.subtract).then_inc(sem("x_inv_ready"), 1)
                for c in range(NC):
                    dve.wait_ge(sem("rhs_summed"), 4 * p + c + 1)
                    v.tensor_copy(RHS, PS[3][0:64, 0:P]).then_inc(sem("rhs_ready"), 1)
                    if c < NC - 1:
                        dve.wait_ge(sem("update_summed"), 4 * p + c + 1)
                        for h in range(2):
                            hs = slice(64 * h, 64 * h + 64)
                            ins = v.scalar_tensor_tensor(ST[hs, hs], ST[hs, hs], DECR[hs, c:c + 1], PS[5][hs, hs],
                                                         ALU.mult, ALU.add)
                        ins.then_inc(sem("state_ready"), 1)

            for k in range(2):
                for g in range(4):
                    gs = slice(2 * g, 2 * g + 2)
                    dve.wait_ge(sem("gn_sums"), 4 * k + g + 1)
                    ps = PS[3 + g][:, :].rearrange("p (m t) -> p m t", m=2)
                    if k == 0:
                        v.scalar_tensor_tensor(R_[:, gs, :], ps, -1.0 / 64, R_[:, gs, :], ALU.mult, ALU.add)\
                            .then_inc(sem("gn_centred"), 1)
                    else:
                        ins = v.tensor_scalar(HF[:, gs, :], ps, 1.0 / 64, GN_EPS, ALU.mult, ALU.add)
            ch.step(ins)
            v.reciprocal(HF[:, :, :], HF[:, :, :]).then_inc(sem("gn_inv_var"), 1)
            for n in range(N_ROG + 2, N_ROG + 6):
                lo(n)
            dve.wait_ge(sem("gn_rstd"), 1)
            for k in range(KT):
                ins = v.scalar_tensor_tensor(R_[:, k, :], R_[:, k, :], vec("rwkv_gn_g_2", k), HF[:, k, :],
                                             ALU.mult, ALU.mult)
            ch.step(ins)
            for k in range(KT):
                ins = v.scalar_tensor_tensor(R_[:, k, :], R_[:, k, :], vec("rwkv_gn_b_2", k), K_[:, k, :],
                                             ALU.add, ALU.add)
            ch.step(ins)
            dve.wait_ge(evacuated, E_ROG + 4)

            def gated(dst, gate, name):
                for g in range(4):
                    gs = slice(2 * g, 2 * g + 2)
                    v.tensor_tensor(dst[:, gs, :], dst[:, gs, :], gate[:, gs, :], ALU.mult)\
                        .then_inc(sem(name + "_ready"), 1)
                low(dst, name)

            def low(dst, name):
                for g in range(4):
                    gs = slice(2 * g, 2 * g + 2)
                    dve.wait_ge(sem(name + "_hi"), g + 1)
                    v.tensor_tensor(GL[:, gs, :], dst[:, gs, :], GH[:, gs, :].bitcast(F32), ALU.subtract)\
                        .then_inc(sem(name + "_split"), 1)

            gated(R_, OG, "rwkv_y")
            add_projection(N_ROUT, 8, YM, add=False)
            v.memset(U31[:, :, 0:30], 0.0).then_inc(sem("u31_zeroed"), 1)
            for n in range(N_GR + 2, N_GR + 6):
                lo(n)
            dve.wait_ge(evacuated, E_GR + 4)
            dve.wait_ge(out_added, 12)
            v.tensor_tensor(YM, YM, GT, ALU.mult).then_inc(sem("gate_r_applied"), 1)
            for n in range(N_CV + 2, N_CV + 6):
                lo(n)
            for j in range(4):
                lo(N_CG + 2 + j)
                dve.wait_ge(evacuated, E_CG + j + 1)
                js = slice(2 * j, 2 * j + 2)
                ins = v.tensor_tensor(U31[:, js, 30:], U31[:, js, 30:], GT[:, js, :], ALU.mult)
            ch.step(ins)
            for n in range(N_COG + 2, N_COG + 6):
                lo(n)
            for k in range(KT):
                ins = v.tensor_scalar(CONV[:, k, :], U31[:, k, 0:T], vec("conv_k_2", k), vec("conv_b_2", k),
                                      ALU.mult, ALU.add)
                ch.done(ins)
            with dve.Fori(0, 30) as i:
                ch.enter(i, KT)
                for k in range(KT):
                    ch.all(KT - 1)
                    ch.done(v.scalar_tensor_tensor(CONV[:, k, :], U31[:, k, bass.ds(i + 1, T)],
                                                   V[:, bass.ds(i * KT + (COL["conv_k_2"] + KT + k), 1)],
                                                   CONV[:, k, :], ALU.mult, ALU.add))
            ch.leave(30)
            ch.all()
            dve.sem_inc(sem("conv_done"), 1)
            dve.wait_ge(sem("ln_sums"), 1)
            for g in range(KT):
                v.scalar_tensor_tensor(CONV[:, g, :], PS[3][:, 0:T], -1.0 / D, CONV[:, g, :], ALU.mult, ALU.add)\
                    .then_inc(sem("conv_centred"), 1)
            dve.wait_ge(sem("ln_sums"), 2)
            inverse_of(RS[:, :], PS[4][:, 0:T], 1.0 / D, LN_EPS, "ln_inv_var")
            dve.wait_ge(sem("ln_rstd"), 1)
            for g in range(KT):
                ch.done(v.scalar_tensor_tensor(CONV[:, g, :], CONV[:, g, :], vec("conv_ln_g_2", g), RS[:, :],
                                               ALU.mult, ALU.mult))
            ch.all()
            for g in range(KT):
                v.tensor_scalar(CONV[:, g, :], CONV[:, g, :], vec("conv_ln_b_2", g), None, ALU.add)\
                    .then_inc(sem("conv_normed"), 1)
            dve.wait_ge(sem("conv_silu"), KT)
            dve.wait_ge(evacuated, E_COG + 4)
            gated(CONV, OG, "conv_y")
            add_projection(N_COUT, 12, YC, add=False)
            for n in range(N_GC + 2, N_GC + 6):
                lo(n)
            dve.wait_ge(evacuated, E_GC + 4)
            dve.wait_ge(out_added, 16)
            ch.step(v.tensor_tensor(YC, YC, GT, ALU.mult))
            for g in range(4):
                gs = slice(2 * g, 2 * g + 2)
                v.tensor_tensor(YM[:, gs, :], YM[:, gs, :], YC[:, gs, :], ALU.add).then_inc(sem("m_ready"), 1)
            low(YM, "m")
            for j in range(4):
                n = N_OUT + j
                lo(n + 2)
                dve.wait_ge(block_done, n + 1)
                for m in range(2):
                    k = 2 * j + m
                    ins = v.scalar_tensor_tensor(X[:, k, :], PS[n % RING][:, m * T:(m + 1) * T], mod[:, 16 + k:17 + k],
                                                 X[:, k, :], ALU.mult, ALU.add)
                ins.then_inc(out_added, 1)
            dve.wait_ge(out_added, 20)
            dve.sem_inc(sem("x_ready"), 1)
            norm(5, lambda k: ("final_g_2", k), last=True)
            dve.wait_ge(sem("normed"), 24)
            dve.sem_inc(sem("result_ready"), 1)


_WEIGHTS = ["gla_w_in", "gla_w_gate_up_f", "gla_w_gate_up_b", "gla_w_out", "attn_w_qkv", "attn_w_out", "ada_w_2",
            "w_in_2", "w_conv_out_2", "rwkv_w2_2", "rwkv_a2_2", "w_rwkv_out_2", "w_out_2"]


def kernel(**inputs):
    import concourse.bacc as bacc
    from concourse.bass_utils import run_bass_kernel_spmd as run

    x = np.asarray(inputs["x"])
    arrays = {
        "in_x": np.ascontiguousarray(x[0].T.reshape(KT, P, T).transpose(1, 0, 2)),
        "in_vecs": np.ascontiguousarray(
            np.concatenate([np.asarray(inputs[n]).reshape(-1, P) for n, _ in VECS], axis=0).T),
        "in_consts": constants(),
    }
    for n in _WEIGHTS:
        arrays["in_" + n] = np.ascontiguousarray(np.asarray(inputs[n])[0])
    for n in ("ffn_w_up", "ffn_w_down"):
        arrays["in_" + n] = np.ascontiguousarray(inputs[n])
    nc = bacc.Bacc("TRN2", target_bir_lowering=False, num_devices=1)
    a = {n[3:]: nc.dram_tensor(n, v.shape, mybir.dt.from_np(v.dtype), kind="ExternalInput").ap()
         for n, v in arrays.items()}
    out = nc.dram_tensor("out", (P, KT, T), F32, kind="ExternalOutput").ap()
    program(nc, a, out)
    r = run(nc, [arrays], core_ids=[0])
    y = r.results[0]["out"]
    return np.ascontiguousarray(y.transpose(1, 0, 2).reshape(D, T).T)[None]
```

```python
from contextlib import ExitStack

import numpy as np

import concourse.bass as bass
from concourse import mybir

F32 = mybir.dt.float32
F32R = mybir.dt.float32r
I32 = mybir.dt.int32
ALU = mybir.AluOpType
ACT = mybir.ActivationFunctionType
AX_X = mybir.AxisListType.X

P = 128
D = 1024
T = 256
KT = D // P
FF = 2816
FI = FF // 256
CH = 64
NC = T // CH
GH_ = 4
QH, KVH = 8, 2
RING = 3
BW = 256
EPS = 1e-6
LN_EPS = 1e-5
GN_EPS = 64e-5
DECAY = -float(np.exp(np.float32(-0.5)))
W2 = 1024
N_GIN = 0
N_GOUT = N_GIN + 12
N_F0 = N_GOUT + 4
N_QKV = N_F0 + 3 * FI
N_AOUT = N_QKV + 6
N_F1 = N_AOUT + 4
N_L3 = N_F1 + 3 * FI
N_CV = N_L3
N_CG = N_CV + 4
N_RKV = N_CG + 4
ORDER = []
for _j in range(1, 4):
    ORDER += [("r", _j), ("k", _j), ("v", _j)]
    ORDER += [("rog", 2 * _j - 2), ("rog", 2 * _j - 1)] if _j < 3 else []
for _name in ("og", "cout", "gc", "rout", "gr", "out"):
    ORDER += [(_name, _j) for _j in range(4)]
PLACE = {_item: N_RKV + 3 + _i for _i, _item in enumerate(ORDER)}
PLACE.update({("r", 0): N_RKV, ("k", 0): N_RKV + 1, ("v", 0): N_RKV + 2})
N_END = N_RKV + 3 + len(ORDER)
NAME_AT = {_n: _item for _item, _n in PLACE.items()}
for _j in range(4):
    NAME_AT[N_CV + _j], NAME_AT[N_CG + _j] = ("val", _j), ("gate", _j)


def bank_of(n):
    if N_GIN + 8 <= n < N_GOUT:
        return 1
    return n % RING if n < N_L3 else n % 2


VECS = [("norm_mix", 16), ("norm_ffn", 16), ("gla_b_gate_f", 4), ("gla_b_gate_b", 4), ("gla_norm", 2),
        ("attn_q_norm", 1), ("attn_k_norm", 1), ("ffn_w_conv", 264), ("ffn_b_conv", 88), ("c_2", 8),
        ("ada_b_2", 24), ("norm_g_2", 8), ("conv_k_2", 248), ("conv_b_2", 8), ("conv_ln_g_2", 8),
        ("conv_ln_b_2", 8), ("rwkv_mu_2", 25), ("rwkv_w0_2", 8), ("rwkv_a0_2", 8), ("rwkv_k_k_2", 8),
        ("rwkv_k_a_2", 8), ("rwkv_r_k_2", 8), ("rwkv_gn_g_2", 8), ("rwkv_gn_b_2", 8), ("final_g_2", 8)]
COL = {}
_at = 0
for _name, _n in VECS:
    COL[_name] = _at
    _at += _n
NV = _at

CONSTS = [("ident", 128), ("ones", 128), ("blk", 128), ("rot", 128), ("cos", 256), ("sin", 256),
          ("scan", 256), ("scmask", 128), ("lev", 6 * 64), ("mask_f", 128), ("mask_b", 128), ("eps", 4)]
CC = {}
_at = 0
for _name, _n in CONSTS:
    CC[_name] = (_at, _at + _n)
    _at += _n
NCST = _at


def constants():
    c = np.zeros((P, NCST), np.float32)
    i = np.arange(P)

    def put(name, a):
        c[:, CC[name][0]:CC[name][1]] = a

    put("eps", np.array([[EPS, LN_EPS, GN_EPS, 0.5 * np.log(65536.0)]]))
    put("ident", np.eye(P))
    put("ones", 1.0)
    put("blk", i[:, None] // 64 == i[None, :] // 64)
    rot = np.zeros((P, P), np.float32)
    rot[i[64:], i[:64]] = -1.0
    rot[i[:64], i[64:]] = 1.0
    put("rot", rot)
    f = np.float32
    tok = np.arange(T)
    inv = f(10000.0) ** (-np.arange(32, dtype=f) / f(32))
    ang = np.concatenate([(tok // 64).astype(f)[:, None] * inv, (tok % 64).astype(f)[:, None] * inv], -1)
    put("cos", np.tile(np.cos(ang).T, (2, 1)))
    put("sin", np.tile(np.sin(ang).T, (2, 1)))
    put("scan", (np.arange(T) % CH != 0)[None, :])
    s, t = i[:, None], i[None, :]
    src = s % CH
    put("scmask", np.where(t < CH, src < t % CH, src <= t % CH))
    for lev in range(6):
        a, b = np.arange(P)[:, None], np.arange(64)[None, :]
        h = 1 << lev
        c[:, CC["lev"][0] + 64 * lev:CC["lev"][0] + 64 * (lev + 1)] = (
            (a // (2 * h) == b // (2 * h)) & (a // h % 2 == 0) & (b // h % 2 == 1))
    same = s // CH == t // CH
    c.view(np.int32)[:, CC["mask_f"][0]:CC["mask_f"][1]] = same & (s <= t)
    c.view(np.int32)[:, CC["mask_b"][0]:CC["mask_b"][1]] = same & (s > t)
    return c


class Chain:

    def __init__(self, eng, sem):
        self.eng, self.sem, self.n, self.turn = eng, sem, 0, None

    def done(self, ins):
        ins.then_inc(self.sem, 1)
        self.n += 1

    def value(self, back=0):
        n = self.n - back
        return n if self.turn is None else self.turn[0] * self.turn[1] + n

    def all(self, back=0):
        self.eng.wait_ge(self.sem, self.value(back))

    def step(self, ins):
        self.done(ins)
        self.all()

    def enter(self, i, per):
        self.turn, self.first = (i, per), self.n

    def leave(self, trips):
        assert self.n - self.first == self.turn[1], (self.n - self.first, self.turn[1])
        self.n = self.first + trips * self.turn[1]
        self.turn = None


def program(nc, a, out):
    with ExitStack() as ctx:
        def sb(name, shape, dt=F32):
            return ctx.enter_context(nc.sbuf_tensor(name, shape, dt))[:]

        sems = {}

        def sem(name):
            if name not in sems:
                sems[name] = ctx.enter_context(nc.semaphore(name))
            return sems[name]

        X = sb("x", [P, KT, T])
        HF = sb("hf", [P, KT, T])
        XH, XL = sb("xh", [P, KT, T], F32R), sb("xl", [P, KT, T], F32R)
        GH, GL = sb("gh", [P, KT, T], F32R), sb("gl", [P, KT, T], F32R)
        RAW = sb("raw", [P, RING, KT, BW])
        WH, WL = sb("wh", [P, RING, KT, BW], F32R), sb("wl", [P, RING, KT, BW], F32R)
        BIG = sb("big", [P, 8, KT, T])
        V = sb("vecs", [P, NV])
        C = sb("consts", [P, NCST])
        U = sb("u", [P, 2, 2, T + 2])
        RS = sb("rs", [P, T])
        small = sb("small", [P, 64])
        mod = sb("mod", [P, 32])
        LNR = sb("ln_rstd_tile", [P, T])
        eps_rms, eps_ln, eps_gn, half_ln = (C[:, NCST - 4 + j:NCST - 3 + j] for j in range(4))
        PS = [ctx.enter_context(nc.psum_tensor(f"bank{i}", [P, 512], F32)) for i in range(8)]

        def cst(name):
            return C[:, CC[name][0]:CC[name][1]]

        def vec(name, j=0, n=1):
            return V[:, COL[name] + j:COL[name] + j + n]

        ident, ones, blk, rot = cst("ident"), cst("ones"), cst("blk"), cst("rot")

        def big(j, n=KT):
            return BIG[:, j, 0:n, :]

        BT = BIG[:, :, :, :].rearrange("p j k t -> p (j k) t")

        def tiles(j, n=1):
            return BT[:, j:j + n, :]

        def flat(j, n):
            return BT[:, j:j + n, :].rearrange("p k t -> p (k t)")

        raw_landed = [sem(f"raw_landed{i}") for i in range(RING)]
        w_hi_ready, w_lo_ready, block_done = sem("w_hi_ready"), sem("w_lo_ready"), sem("block_done")
        evacuated = sem("evacuated")
        out_added = sem("out_added")
        consts_landed = sem("consts_landed")

        def split_hi(act, n, i=0):
            act.wait_ge(raw_landed[n % RING], 16 * (n // RING + 1) + 16 * i)
            if n >= RING:
                act.wait_ge(block_done, n - RING + 1 + RING * i)
            nc.scalar.activation(WH[:, n % RING, :, :], RAW[:, n % RING, :, :], ACT.Copy)\
                .then_inc(w_hi_ready, 1)

        def split_lo(eng, n, i=0):
            eng.wait_ge(w_hi_ready, n + 1 + RING * i)
            eng.tensor_tensor(WL[:, n % RING, :, :], RAW[:, n % RING, :, :],
                              WH[:, n % RING, :, :].bitcast(F32), ALU.subtract).then_inc(w_lo_ready, 1)

        def load(sp, n, src, i=0):
            if n >= RING:
                sp.wait_ge(w_lo_ready, n - RING + 1 + RING * i)
            dst = RAW[:, n % RING, :, :]
            if len(src.shape) == 4:
                dst = dst.rearrange("p (k c) n -> p k c n", k=2)
            sp.dma_start(dst, src).then_inc(raw_landed[n % RING], 16)

        def cols(w, c0):
            return w[:, c0:c0 + BW].rearrange("(k p) n -> p k n", p=P)

        def three(ps, wh, wl, xh, xl, start, stop, moving_weights=False):
            if moving_weights:
                nc.tensor.matmul(ps, xh, wh, start=start, stop=False)
                nc.tensor.matmul(ps, xh, wl, start=False, stop=False)
                return nc.tensor.matmul(ps, xl, wh, start=False, stop=stop)
            nc.tensor.matmul(ps, wh, xh, start=start, stop=False)
            nc.tensor.matmul(ps, wh, xl, start=False, stop=False)
            return nc.tensor.matmul(ps, wl, xh, start=False, stop=stop)

        def product(pe, n, bank, xh, xl, i=0, moving_weights=False, ready=None):
            pe.wait_ge(w_lo_ready, n + 1 + RING * i)
            s = n % RING
            for m in range(2):
                ps = PS[bank][:, m * T:(m + 1) * T]
                ms = slice(m * P, (m + 1) * P)
                for k in range(KT):
                    if ready and m == 0:
                        ready(k)
                    if moving_weights:
                        last = three(ps, WH[:, s, k, :], WL[:, s, k, :], xh[:, k, ms], xl[:, k, ms],
                                     k == 0, k == KT - 1, True)
                    else:
                        last = three(ps, WH[:, s, k, ms], WL[:, s, k, ms], xh[:, k, :], xl[:, k, :],
                                     k == 0, k == KT - 1)
            last.then_inc(block_done, 1)

        E_GIN = 0
        E_F0 = E_GIN + 12
        E_QKV = E_F0 + 2 * FI
        E_F1 = E_QKV + 6
        E_L3 = E_F1 + 2 * FI

        def taken(n):
            return E_L3 + n - N_L3 + 1

        w_r = sb("w_r", [P, KT, 32])
        w_up = BT[0:16, 48:52, :].rearrange("p (d a) t -> p d (a t)", d=2)
        w_lora = BT[:, 24:28, :].rearrange("p a (b c) -> p (a b) c", c=128)
        w2a2 = BT[:, 28:32, :].rearrange("p a b -> p (a b)")

        w_in = a["w_in_2"]
        block = ctx.enter_context(nc.Block())

        @block.sync
        def _(sp):
            sp.dma_start(V[:, :], a["vecs"]).then_inc(consts_landed, 16)
            sp.dma_start(C[:, :], a["consts"]).then_inc(consts_landed, 16)
            sp.dma_start(X[:, :, :], a["x"]).then_inc(consts_landed, 16)
            sp.dma_start(w_r[:, :, :], a["gla_w_in"][:, 3072:3104].rearrange("(k p) n -> p k n", p=P))\
                .then_inc(consts_landed, 16)
            sp.dma_start(w_up[:, 0, :], a["gla_w_gate_up_f"]).then_inc(consts_landed, 16)
            sp.dma_start(w_up[:, 1, :], a["gla_w_gate_up_b"]).then_inc(consts_landed, 16)

            def columns(w, n0, c0, count):
                for j in range(count):
                    load(sp, n0 + j, cols(w, c0 + j * BW))

            columns(a["gla_w_in"], N_GIN, 0, 12)
            columns(a["gla_w_out"], N_GOUT, 0, 4)

            def mlp(layer, n0):
                up, down = a["ffn_w_up"][layer], a["ffn_w_down"][layer]
                down_b = down.rearrange("(i k p) n -> i p k n", k=2, p=P)
                load(sp, n0, cols(up, 0))
                load(sp, n0 + 1, cols(up, FF))
                with sp.Fori(0, FI - 1) as i:
                    def upc(first):
                        return up[:, bass.ds(i * BW + (first + BW), BW)].rearrange("(k p) n -> p k n", p=P)
                    load(sp, n0 + 2, upc(0), i)
                    load(sp, n0 + 3, upc(FF), i)
                    load(sp, n0 + 4, down[bass.ds(i * BW, BW), :].rearrange("(k p) (c n) -> p k c n", p=P, n=BW), i)
                load(sp, n0 + 3 * FI - 1, down[(FI - 1) * BW:FF, :].rearrange("(k p) (c n) -> p k c n", p=P, n=BW))

            mlp(0, N_F0)
            columns(a["attn_w_qkv"], N_QKV, 0, 6)
            columns(a["attn_w_out"], N_AOUT, 0, 4)
            mlp(1, N_F1)
            sp.wait_ge(sem("attn_split"), QH)
            sp.dma_start(w_lora, w_in[:, 6 * D:6 * D + P].rearrange("(k p) n -> p k n", p=P))\
                .then_inc(sem("lora_landed"), 16)
            sp.dma_start(w2a2[0:64, :], a["rwkv_w2_2"]).then_inc(sem("lora_landed"), 16)
            sp.dma_start(w2a2[64:128, :], a["rwkv_a2_2"]).then_inc(sem("lora_landed"), 16)
            sources = {"val": (w_in, 0), "gate": (w_in, D), "og": (w_in, 2 * D), "r": (w_in, 3 * D),
                       "k": (w_in, 4 * D), "v": (w_in, 5 * D), "rog": (w_in, 6 * D + P),
                       "gc": (w_in, 7 * D + P), "gr": (w_in, 8 * D + P), "cout": (a["w_conv_out_2"], 0),
                       "rout": (a["w_rwkv_out_2"], 0), "out": (a["w_out_2"], 0)}
            for n in range(N_L3, N_END):
                name, j = NAME_AT[n]
                w, c0 = sources[name]
                load(sp, n, cols(w, c0 + j * BW))
                if n == N_RKV - 2:
                    sp.wait_ge(sem("normed"), 20)
                    sp.dma_start(a["x_aside"], X[:, :, :]).then_inc(sem("x_aside_stored"), 16)
                if NAME_AT[n] == ("gr", 2):
                    sp.wait_ge(sem("rwkv_y_split"), 4)
                    sp.wait_ge(sem("x_aside_stored"), 16)
                    sp.dma_start(X[:, :, :], a["x_aside"]).then_inc(sem("x_back"), 16)
            sp.wait_ge(sem("result_ready"), 1)
            sp.dma_start(out, HF[:, :, :]).then_inc(sem("result_stored"), 16)
            sp.wait_ge(sem("result_stored"), 16)

        Q, K = tiles(0, 4), tiles(4, 4)
        VT = BIG[:, 1, :, :].rearrange("p (a b) t -> p a (b t)", a=2)
        SG = tiles(16, 8)
        LA = tiles(24, 8)
        QD, KI, KE = tiles(32, 8), tiles(40, 8), tiles(48, 8)
        E1 = HF
        TMP8 = tiles(56, 8)
        OT = tiles(56, 8)
        SF = [tiles(24, 3), tiles(0, 3)]
        SBK = [tiles(27, 3), flat(3, 3).rearrange("p (a t) -> p a t", a=3)]
        KET = [flat(30, 2), flat(6, 2)]
        ATT = sb("att", [P, 2, P])
        ATTS = [ATT, HF[:, 6, :].rearrange("p (a t) -> p a t", a=2)]
        GSQ = [HF[:, 2 * h:2 * h + 2, :] for h in range(3)] + [tiles(44, 2)]
        GRS = tiles(40, 4)
        DEC = small[:, 8:40]
        R16 = U[0:16, 0, :, 1:T + 1]
        CV, CG = tiles(32, 2), tiles(34, 2)
        SGT, HID = tiles(36, 2), tiles(38, 2)

        def kv_piece(q):
            bank, at = [(5, 0), (7, 0), (5, 1), (7, 1), (6, 0), (2, 0)][q]
            return PS[bank][:, at * T:(at + 1) * T]

        QK = tiles(0, 10)
        VA = tiles(16, 2)
        PR, PT = tiles(18, 2), tiles(20, 2)
        SQ10 = tiles(24, 10)
        RKV = tiles(0, 24)
        R_, K_, V_ = tiles(0, 8), tiles(8, 8), tiles(16, 8)
        SIG, AA, CUM, KK, K2, BB, TMP = (flat(40 + j, 1) for j in range(7))
        KR = flat(47, 2).rearrange("p (c s t) -> p c s t", c=NC, s=2)
        BK = flat(49, 2).rearrange("p (c s t) -> p c s t", c=NC, s=2)
        BKE = flat(51, 2).rearrange("p (c s t) -> p c s t", c=NC, s=2)
        SC = [flat(24 + 2 * h, 2).rearrange("p (c n) -> p c n", c=NC) for h in range(2)]
        TK = flat(53, 2).rearrange("p (c n) -> p c n", c=NC)
        XI, XT, YI = (flat(32 + 2 * j, 2)[0:64, :] for j in range(3))
        LM = flat(38, 2)[0:64, :]
        UV = U[:, :, :, :].rearrange("p a b t -> p (a b t)")[:, 0:512].rearrange("p (c h v) -> p c h v", c=NC, h=2)
        ST = ATT[:, 0, :]
        LORA = RS
        RHS = ATT[0:64, 1, :]
        DECR = small[:, 40:44]
        ROG = X
        YM = tiles(32, 8)
        U31 = flat(55, 9)[:, 0:KT * (T + 30)].rearrange("p (k t) -> p k t", k=KT)
        S8 = tiles(55, 8)
        CONV = HF
        GT = sb("gate_tiles", [P, 2, 2, T])
        TAPS = 31 * KT

        ada_acc = [flat(40 + 4 * h, 4) for h in range(3)]
        ada_ring = [flat(52 + 4 * h, 4) for h in range(2)]
        ada_tmp = flat(60, 4)
        sc_col = small[:, 0:8]
        ADA_STEPS = 3 + 21 * 2
        ada_v = a["ada_w_2"].rearrange("(k p) (h n) -> p k h n", p=P, h=3)

        @block.gpsimd
        def _(pool):
            for h in range(GH_):
                pool.wait_ge(sem("gla_out_taken"), h + 1)
                if h == GH_ - 1:
                    pool.wait_ge(sem("att_scores"), GH_)
                o = OT[:, 2 * h:2 * h + 2, :]
                nc.gpsimd.tensor_tensor(GSQ[h], o, o, ALU.mult).then_inc(sem("gla_squares"), 1)
            ch = Chain(pool, sem("ada_steps"))
            pool.wait_ge(sem("rms_split"), 4 * 2)
            pool.wait_ge(sem("silu_c_ready"), 1)
            for n in range(24):
                k, h = n // 3, n % 3
                if n < 2:
                    pool.dma_start(ada_ring[n], ada_v[:, k, h, :]).then_inc(sem(f"ada_landed{n % 2}"), 16)
            for n in range(24):
                k, h = n // 3, n % 3
                pool.wait_ge(sem(f"ada_landed{n % 2}"), 16 * (n // 2 + 1))
                if k == 0:
                    ch.step(nc.gpsimd.tensor_scalar(ada_acc[h], ada_ring[n % 2], sc_col[:, k:k + 1], None, ALU.mult))
                else:
                    ch.step(nc.gpsimd.tensor_scalar(ada_tmp, ada_ring[n % 2], sc_col[:, k:k + 1], None, ALU.mult))
                    ch.step(nc.gpsimd.tensor_tensor(ada_acc[h], ada_acc[h], ada_tmp, ALU.add))
                if n + 2 < 24:
                    pool.dma_start(ada_ring[n % 2], ada_v[:, (n + 2) // 3, (n + 2) % 3, :])\
                        .then_inc(sem(f"ada_landed{n % 2}"), 16)

            pool.wait_ge(w_lo_ready, N_L3 + 2)
            for n in range(N_L3 + 2, N_END):
                split_lo(pool, n)

        SLOTS = 18
        between = {}

        def put(p, slot, item):
            between.setdefault((p, slot), []).append(item)

        def put_blocks(p, names, first=0, step=1):
            slot = first
            for name in names:
                n = PLACE[name]
                for q in range(4):
                    put(p, min(slot, SLOTS - 1), ("quarter", n, q))
                    slot += step
                put(p, min(slot, SLOTS - 1), ("take", n))

        put_blocks(0, [("r", 1), ("k", 1), ("v", 1)])
        put_blocks(1, [("rog", 0), ("rog", 1)], 1, 2)
        put_blocks(2, [("r", 2), ("k", 2), ("v", 2)])
        put_blocks(3, [("rog", 2), ("rog", 3)], 1, 2)
        put_blocks(4, [("r", 3), ("k", 3), ("v", 3)])
        for k in range(7):
            put(4, 10 + k, ("ln", k))
        put_blocks(5, [("og", j) for j in range(4)])
        put_blocks(6, [("cout", j) for j in range(4)])
        put_blocks(7, [("gc", j) for j in range(4)])
        TAP_SLOTS = 4 * SLOTS + 8
        TAPS_BEFORE = 40
        for k in range(TAP_SLOTS):
            a0 = TAPS_BEFORE + (TAPS - TAPS_BEFORE) * k // TAP_SLOTS
            a1 = TAPS_BEFORE + (TAPS - TAPS_BEFORE) * (k + 1) // TAP_SLOTS
            put(k // SLOTS, k % SLOTS, ("taps", a0, a1))

        @block.tensor
        def _(pe):
            def sums(i):
                for g in range(4):
                    pe.wait_ge(sem("squares_ready"), 4 * i + g + 1)
                    for k in (2 * g, 2 * g + 1):
                        last = nc.tensor.matmul(PS[3][:, 0:T], ones, HF[:, k, :], start=k == 0, stop=k == KT - 1)
                last.then_inc(sem("square_sums"), 1)

            def projected(n0, count, e0, xh, xl, free=None, moving=()):
                for j in range(count):
                    if j >= RING:
                        pe.wait_ge(evacuated, e0 + j - RING + 1)
                    product(pe, n0 + j, bank_of(n0 + j), xh, xl, moving_weights=j in moving)

            def out_projection(n0, a0, xh, xl, ready=None):
                for j in range(4):
                    if j >= RING:
                        pe.wait_ge(out_added, a0 + j - RING + 1)
                    product(pe, n0 + j, bank_of(n0 + j), xh, xl, ready=None if j else ready)

            def mlp(layer, n0, e0):
                g0 = layer * FI
                pe.wait_ge(sem("rms_split"), 4 * (2 * layer + 2))

                def up(n, s, i=0):
                    if s:
                        pe.wait_ge(evacuated, e0 + 2 * s - 1 + 2 * i)
                    product(pe, n, 0, XH, XL, i)
                    if s:
                        pe.wait_ge(evacuated, e0 + 2 * s + 2 * i)
                    product(pe, n + 1, 1, XH, XL, i)

                def down(n, s, i=0, first=False, last=False):
                    pe.wait_ge(w_lo_ready, n + 1 + RING * i)
                    pe.wait_ge(sem("hidden_split"), g0 + s + 1 + i)
                    wh = WH[:, n % RING, :, :].rearrange("p (k c) n -> p k (c n)", k=2)
                    wl = WL[:, n % RING, :, :].rearrange("p (k c) n -> p k (c n)", k=2)
                    for k in range(2):
                        for m in range(KT):
                            ps = PS[4 + m // 2][:, (m % 2) * T:(m % 2 + 1) * T]
                            ms = slice(m * P, (m + 1) * P)
                            start = first and k == 0 and m % 2 == 0
                            stop = last and k == 1
                            nc.tensor.matmul(ps, wh[:, k, ms], GH[:, k, :], start=start, stop=False,
                                             skip_group_check=True)
                            nc.tensor.matmul(ps, wh[:, k, ms], GL[:, k, :], start=False, stop=False,
                                             skip_group_check=True)
                            ins = nc.tensor.matmul(ps, wl[:, k, ms], GH[:, k, :], start=False, stop=stop,
                                                   skip_group_check=True)
                    ins.then_inc(block_done, 1)

                up(n0, 0)
                up(n0 + 2, 1)
                down(n0 + 4, 0, first=True)
                with pe.Fori(1, FI - 1) as i:
                    up(n0 + 2, 1, i)
                    down(n0 + 4, 0, i)
                down(n0 + 3 * FI - 1, FI - 1, last=True)

            pe.wait_ge(consts_landed, 16 * 6)
            sums(0)
            pe.wait_ge(sem("rms_split"), 4)
            for d in range(2):
                for k in range(KT):
                    last = nc.tensor.matmul(PS[3][0:16, d * T:(d + 1) * T], w_r[:, k, 16 * d:16 * d + 16],
                                            HF[:, k, :], start=k == 0, stop=k == KT - 1)
            last.then_inc(sem("rank_rows"), 1)
            pe.wait_ge(sem("rank_rows_taken"), 1)
            for d in range(2):
                for h in range(GH_):
                    last = nc.tensor.matmul(PS[4 + 2 * d + h // 2][:, (h % 2) * T:(h % 2 + 1) * T],
                                            w_up[:, d, h * P:(h + 1) * P], R16[:, d, :], start=True, stop=True)
            last.then_inc(sem("gate_logits"), 1)
            projected(N_GIN, 8, E_GIN, XH, XL, moving=(4, 5, 6, 7))

            def gla_scores(h):
                if h:
                    pe.wait_ge(sem("att_masked"), h)
                for d in range(2):
                    for tt in range(2):
                        ts = slice(tt * P, (tt + 1) * P)
                        last = nc.tensor.matmul(PS[3][:, (2 * d + tt) * P:(2 * d + tt + 1) * P],
                                                KI[:, 4 * d + h, ts], QD[:, 4 * d + h, ts], start=True, stop=True)
                last.then_inc(sem("att_scores"), 1)
                if h:
                    pe.wait_ge(sem("ket_taken"), h)
                for d in range(2):
                    for tt in range(2):
                        last = nc.tensor.transpose(PS[4][:, (2 * d + tt) * P:(2 * d + tt + 1) * P],
                                                   KE[:, 4 * d + h, tt * P:(tt + 1) * P], ident)
                last.then_inc(sem("ke_turned"), 1)

            def gla_states(h):
                pe.wait_ge(sem("ket_taken"), h + 1)
                if h:
                    pe.wait_ge(sem("states_ready"), h)
                for d in range(2):
                    for j in range(3):
                        c = j if d == 0 else 3 - j
                        q = 3 * d + j
                        rows = slice(64 * (c % 2), 64 * (c % 2) + 64)
                        last = nc.tensor.matmul(kv_piece(q),
                                                KET[h % 2][rows, (2 * d + c // 2) * P:(2 * d + c // 2 + 1) * P],
                                                VT[rows, c // 2, h * 256:(h + 1) * 256], start=True, stop=True)
                last.then_inc(sem("chunk_kv"), 1)

            def gla_out(h):
                bank = PS[0]
                sf, sbk, att = SF[h % 2], SBK[h % 2], ATTS[h % 2]
                if h:
                    pe.wait_ge(sem("gla_out_taken"), h)
                pe.wait_ge(sem("att_masked"), h + 1)
                pe.wait_ge(sem("states_ready"), h + 1)
                for v in range(2):
                    c0 = h * 256 + v * P
                    for tt in range(2):
                        nc.tensor.matmul(bank[:, v * T + tt * P:v * T + (tt + 1) * P], VT[:, tt, c0:c0 + P],
                                         att[:, tt, :], start=tt == 0, stop=False, skip_group_check=True)
                    for c in range(1, NC):
                        nc.tensor.matmul(bank[:, v * T + c * CH:v * T + (c + 1) * CH],
                                         sf[:, c - 1, v * P:(v + 1) * P], QD[:, h, c * CH:(c + 1) * CH],
                                         start=False, stop=False, skip_group_check=True)
                    for c in range(NC - 1):
                        last = nc.tensor.matmul(bank[:, v * T + c * CH:v * T + (c + 1) * CH],
                                                sbk[:, 2 - c, v * P:(v + 1) * P],
                                                QD[:, 4 + h, c * CH:(c + 1) * CH],
                                                start=False, stop=c == NC - 2, skip_group_check=True)
                last.then_inc(sem("gla_out_summed"), 1)

            def gla_gate(j, m):
                n = N_GIN + 8 + j
                if m == 0:
                    pe.wait_ge(w_lo_ready, n + 1)
                    pe.wait_ge(evacuated, E_GIN + 8 + j)
                for k in range(KT):
                    last = three(PS[1][:, m * T:(m + 1) * T], WH[:, n % RING, k, m * P:(m + 1) * P],
                                 WL[:, n % RING, k, m * P:(m + 1) * P], XH[:, k, :], XL[:, k, :],
                                 k == 0, k == KT - 1)
                if m:
                    last.then_inc(block_done, 1)

            def gla_sums(pair):
                pe.wait_ge(sem("gla_squares"), 2 * pair + 2)
                for h in (2 * pair, 2 * pair + 1):
                    for v in range(2):
                        last = nc.tensor.matmul(PS[5 + pair][:, (h % 2) * T:(h % 2 + 1) * T], ones,
                                                GSQ[h][:, v, :], start=v == 0, stop=v == 1)
                last.then_inc(sem("gla_square_sums"), 1)

            pe.wait_ge(sem("gla_decayed"), 1)
            pe.wait_ge(evacuated, E_GIN + 8)
            gla_scores(0)
            for h in range(GH_):
                gla_gate(h, 0)
                gla_states(h)
                if h + 1 < GH_:
                    gla_scores(h + 1)
                gla_gate(h, 1)
                if h == GH_ - 1:
                    pe.wait_ge(sem("states_ready"), GH_)
                    gla_sums(0)
                gla_out(h)
            gla_sums(1)
            out_projection(N_GOUT, 0, GH, GL,
                           lambda k: k % 4 == 0 and pe.wait_ge(sem("gla_out_split"), k // 4 + 1))

            sums(1)
            mlp(0, N_F0, E_F0)

            sums(2)
            pe.wait_ge(sem("rms_split"), 12)
            projected(N_QKV, 6, E_QKV, XH, XL, moving=(5,))
            for g in range(5):
                pe.wait_ge(sem("qk_squares"), g + 1)
                nc.tensor.matmul(PS[3 + g][:, :], ones, SQ10[:, 2 * g:2 * g + 2, :], start=True, stop=True)\
                    .then_inc(sem("qk_square_sums"), 1)
            for g in range(5):
                pe.wait_ge(sem("qk_normed"), g + 1)
                nc.tensor.matmul(PS[3 + g][:, :], rot, QK[:, 2 * g:2 * g + 2, :], start=True, stop=True)\
                    .then_inc(sem("qk_turned"), 1)
            pe.wait_ge(sem("qk_roped"), 5)
            pe.wait_ge(evacuated, E_QKV + 6)

            def attend_scores(h):
                if h >= 2:
                    pe.wait_ge(sem("probs_ready"), h - 1)
                for tt in range(2):
                    last = nc.tensor.matmul(PS[3 + h % 2][:, tt * T:(tt + 1) * T], QK[:, h, tt * P:(tt + 1) * P],
                                            QK[:, 8 + h // 4, :], start=True, stop=True)
                last.then_inc(sem("scores_ready"), 1)

            def attend_out(h):
                pe.wait_ge(sem("probs_ready"), h + 1)
                if h >= 2:
                    pe.wait_ge(sem("probs_t_taken"), h - 1)
                for st in range(2):
                    for tt in range(2):
                        last = nc.tensor.transpose(PS[5 + h % 2][:, st * T + tt * P:st * T + (tt + 1) * P],
                                                   PR[:, tt, st * P:(st + 1) * P], ident)
                last.then_inc(sem("probs_turned"), 1)
                pe.wait_ge(sem("probs_t_taken"), h + 1)
                if h >= 2:
                    pe.wait_ge(sem("attn_split"), h - 1)
                bank = PS[7] if h % 2 else PS[0]
                for st in range(2):
                    last = nc.tensor.matmul(bank[:, 0:T], VA[:, st, (h // 4) * P:(h // 4 + 1) * P], PT[:, st, :],
                                            start=st == 0, stop=st == 1)
                last.then_inc(sem("attn_out"), 1)

            attend_scores(0)
            for h in range(QH):
                if h + 1 < QH:
                    attend_scores(h + 1)
                attend_out(h)
            pe.wait_ge(sem("attn_split"), QH)
            out_projection(N_AOUT, 4, GH, GL)

            sums(3)
            mlp(1, N_F1, E_F1)

            pe.wait_ge(sem("ada_steps"), ADA_STEPS)
            for j in range(24):
                last = nc.tensor.matmul(PS[2][:, j:j + 1], ada_acc[j // 8][:, (j % 8) * P:(j % 8 + 1) * P],
                                        ones[:, 0:1], start=True, stop=True)
            last.then_inc(sem("mod_summed"), 1)
            sums(4)
            pe.wait_ge(sem("rms_split"), 20)

            pe.wait_ge(sem("lora_landed"), 48)
            for k in range(KT):
                last = nc.tensor.matmul(PS[3][:, 0:T], w_lora[:, k, :], HF[:, k, :], start=k == 0, stop=k == KT - 1)
            last.then_inc(sem("lora_rows"), 1)

            needs = {"cout": "conv_y_split", "rout": "rwkv_y_split", "out": "m_split"}

            def quarter(n, q):
                name, j = NAME_AT[n]
                if q == 0:
                    pe.wait_ge(w_lo_ready, n + 1)
                    if name in needs:
                        pe.wait_ge(sem(needs[name]), 4)
                    if n >= N_L3 + 2:
                        pe.wait_ge(*((out_added, 8 + j - 1) if name == "out" and j >= 2 else (evacuated, taken(n - 2))))
                xh, xl = (GH, GL) if name in needs else (XH, XL)
                s, m = n % RING, q // 2
                ms = slice(m * P, (m + 1) * P)
                for k in range(4 * (q % 2), 4 * (q % 2) + 4):
                    last = three(PS[bank_of(n)][:, m * T:(m + 1) * T], WH[:, s, k, ms], WL[:, s, k, ms],
                                 xh[:, k, :], xl[:, k, :], k == 0, k == KT - 1)
                if q == 3:
                    last.then_inc(block_done, 1)

            def whole(n):
                for q in range(4):
                    quarter(n, q)

            def ln(step):
                if step == 0:
                    pe.wait_ge(sem("conv_done"), 1)
                    for g in range(KT):
                        last = nc.tensor.matmul(PS[2][:, 0:T], ones, CONV[:, g, :], start=g == 0, stop=g == KT - 1)
                    last.then_inc(sem("ln_sums"), 1)
                if step == 3:
                    pe.wait_ge(sem("ln_squares"), 1)
                    for g in range(KT):
                        last = nc.tensor.matmul(PS[2][:, 0:T], ones, S8[:, g, :], start=g == 0, stop=g == KT - 1)
                    last.then_inc(sem("ln_sums"), 1)

            def slot(p, k):
                for item in between.get((p, k), ()):
                    if item[0] == "quarter":
                        quarter(item[1], item[2])
                    elif item[0] == "ln":
                        ln(item[1])

            def front(p, part):
                if part == 0:
                    pe.wait_ge(sem("shifted"), 3 * (p // 2) + 3)
                    if p:
                        pe.wait_ge(sem("uv_ready"), p)
                        pe.wait_ge(sem("inverse_ready"), p)
                    nc.tensor.matmul(PS[6][:, 0:T], w2a2[0:64, p * P:(p + 1) * P], LORA[0:64, :],
                                     start=True, stop=True)
                    nc.tensor.matmul(PS[2][:, 0:T], w2a2[64:128, p * P:(p + 1) * P], LORA[64:128, :],
                                     start=True, stop=True).then_inc(sem("pre_acts"), 1)
                elif part == 1:
                    pe.wait_ge(sem("kk_squares"), p + 1)
                    pe.wait_ge(sem("sigmoids_ready"), p + 1)
                    nc.tensor.matmul(PS[6][:, 0:T], blk, TMP, start=True, stop=True).then_inc(sem("kk_sums"), 1)
                else:
                    pe.wait_ge(sem("rkrk_ready"), p + 1)
                    nc.tensor.matmul(PS[2][:, 0:T], blk, TMP, start=True, stop=True).then_inc(sem("rkrk_sums"), 1)

            def middle(p):
                slot(p, 0)
                if p:
                    pe.wait_ge(sem("o_taken"), p)
                for tt in range(2):
                    last = nc.tensor.transpose(PS[7][:, tt * P:(tt + 1) * P], V_[:, p, tt * P:(tt + 1) * P], ident)
                last.then_inc(sem("v_turned"), 1)
                slot(p, 1)
                slot(p, 2)
                pe.wait_ge(sem("rwkv_decayed"), p + 1)
                for h in range(2):
                    rows = slice(64 * h, 64 * h + 64)
                    for c in range(NC):
                        last = nc.tensor.matmul(PS[5 + h][:, c * P:(c + 1) * P], BK[rows, c, :, :], KR[rows, c, :, :],
                                                start=True, stop=True)
                last.then_inc(sem("rwkv_scores"), 1)
                slot(p, 3)
                pe.wait_ge(sem("bke_ready"), p + 1)
                for c in range(NC):
                    last = nc.tensor.transpose(PS[2][:, c * P:(c + 1) * P], BKE[:, c, :, :], ident)
                last.then_inc(sem("bke_turned"), 1)
                slot(p, 4)
                q0 = p * 5
                for lev in range(5):
                    pe.wait_ge(sem("xt_ready"), q0 + lev + 1)
                    if lev == 0:
                        for s in range(8):
                            last = nc.tensor.transpose(PS[3][0:64, s * 64:(s + 1) * 64], XT[:, s * 64:(s + 1) * 64],
                                                       ident[0:64, 0:64])
                        last.then_inc(sem("xt_turned"), 1)
                    pe.wait_ge(sem("x_inv_ready"), q0 + lev + 1)
                    pe.wait_ge(sem("level_ready"), q0 + lev + 1)
                    for s in range(8):
                        ss = slice(s * 64, (s + 1) * 64)
                        last = nc.tensor.matmul(PS[4][0:64, ss], LM[:, ss], XI[:, ss], start=True, stop=True)
                    last.then_inc(sem("y_summed"), 1)
                    slot(p, 5 + 2 * lev)
                    pe.wait_ge(sem("y_ready"), q0 + lev + 1)
                    for s in range(8):
                        ss = slice(s * 64, (s + 1) * 64)
                        last = nc.tensor.matmul(PS[5][0:64, ss], YI[:, ss], XT[:, ss], start=True, stop=True)
                    last.then_inc(sem("xt_summed"), 1)
                    if lev < 4:
                        for s in range(8):
                            ss = slice(s * 64, (s + 1) * 64)
                            last = nc.tensor.matmul(PS[6][0:64, ss], XT[:, ss], YI[:, ss], start=True, stop=True)
                        last.then_inc(sem("x_summed"), 1)
                    slot(p, 6 + 2 * lev)

            def chain(p, c):
                r0 = 4 * p + c
                if c == 0:
                    pe.wait_ge(sem("inverse_ready"), p + 1)
                    pe.wait_ge(sem("uv_ready"), p + 1)
                pe.wait_ge(sem("state_ready"), r0 + 1)
                nc.tensor.matmul(PS[3][0:64, 0:P], KR[:, c, 0, :], ST, start=True, stop=False,
                                 skip_group_check=True)
                for h in range(2):
                    last = nc.tensor.matmul(PS[3][0:64, h * 64:(h + 1) * 64], SC[h][:, c, 0:64], UV[:, c, h, :],
                                            start=False, stop=True, skip_group_check=True)
                last.then_inc(sem("rhs_summed"), 1)
                oc = slice(c * CH, (c + 1) * CH)
                nc.tensor.matmul(PS[7][:, oc], ST, KR[:, c, 1, :], start=c == 0, stop=False,
                                 skip_group_check=True)
                pe.wait_ge(sem("rhs_ready"), r0 + 1)
                for h in range(2):
                    s = h * NC + c
                    last = nc.tensor.matmul(PS[4][0:64, h * 64:(h + 1) * 64], XT[:, s * 64:(s + 1) * 64],
                                            RHS[:, h * 64:(h + 1) * 64], start=True, stop=True)
                last.then_inc(sem("u_summed"), 1)
                if c < NC - 1:
                    slot(p, 15 + c)
                pe.wait_ge(sem("u_ready"), r0 + 1)
                nc.tensor.matmul(PS[5][:, 0:P], TK[:, c, :], UV[:, c, :, :], start=True, stop=True)\
                    .then_inc(sem("update_summed"), 1)
                for h in range(2):
                    last = nc.tensor.matmul(PS[7][64 * h:64 * h + 64, oc], UV[:, c, h, :], SC[h][:, c, 64:128],
                                            start=False, stop=c == NC - 1, skip_group_check=True)
                if c == NC - 1:
                    last.then_inc(sem("rwkv_out_summed"), 1)

            pe.wait_ge(evacuated, E_L3)
            for n in range(N_L3, N_RKV + 3):
                whole(n)
            pe.wait_ge(sem("lora_ready"), 1)
            for part in range(3):
                front(0, part)
            for p in range(8):
                middle(p)
                for c in range(NC):
                    chain(p, c)
                    if p < 7 and c < 3:
                        front(p + 1, c)
            pe.wait_ge(sem("o_taken"), 8)
            for k in range(2):
                for g in range(4):
                    if k:
                        pe.wait_ge(sem("gn_squares"), g + 1)
                    nc.tensor.matmul(PS[3 + g][:, :], blk, (S8 if k else R_)[:, 2 * g:2 * g + 2, :],
                                     start=True, stop=True).then_inc(sem("gn_sums"), 1)
            for n in range(PLACE["rout", 0], N_END):
                whole(n)
            sums(5)

        @block.scalar
        def _(act):
            ch = Chain(act, sem("act_steps"))

            def ck(ap):
                return ap.rearrange("p (c t) -> p c t", c=NC)

            def rsqrt(dst, sums, scale, eps, name):
                ch.step(nc.scalar.activation(dst, sums, ACT.Ln, scale=scale, bias=eps))
                nc.scalar.activation(dst, dst, ACT.Exp, scale=-0.5).then_inc(sem(name), 1)

            def squares(i):
                if i:
                    act.wait_ge(sem("x_ready"), i)
                for g in range(4):
                    nc.scalar.activation(HF[:, 2 * g:2 * g + 2, :], X[:, 2 * g:2 * g + 2, :], ACT.Square)\
                        .then_inc(sem("squares_ready"), 1)

            def norm_split(i, last=False):
                act.wait_ge(sem("square_sums"), i + 1)
                rsqrt(RS, PS[3][:, 0:T], 1.0 / D, eps_rms, "rstd_ready")
                if last:
                    return
                for g in range(4):
                    act.wait_ge(sem("normed"), 4 * i + g + 1)
                    nc.scalar.activation(XH[:, 2 * g:2 * g + 2, :], HF[:, 2 * g:2 * g + 2, :], ACT.Copy)\
                        .then_inc(sem("rms_hi"), 1)

            def take(n, j, e0, dst, func=ACT.Copy, scale=1.0):
                if n + 2 < N_END:
                    split_hi(act, n + 2)
                act.wait_ge(block_done, n + 1)
                src = PS[bank_of(n)][:, :].rearrange("p (m t) -> p m t", m=2)
                nc.scalar.activation(dst, src, func, scale=scale).then_inc(evacuated, 1)

            def split_for_projection(n0):
                for j in range(4):
                    if n0 + j + 2 < N_END:
                        split_hi(act, n0 + j + 2)

            def hidden_hi(g0, s, i=0):
                act.wait_ge(sem("gate_convolved"), g0 + s + 1 + i)
                nc.scalar.activation(SGT, CG, ACT.Silu).then_inc(sem("gate_silu"), 1)

            def hidden_copy(g0, s, n, i=0):
                act.wait_ge(sem("hidden_ready"), g0 + s + 1 + i)
                nc.scalar.activation(GH[:, 0:2, :], HID, ACT.Copy).then_inc(sem("hidden_hi"), 1)

            def mlp(layer, n0):
                g0 = layer * FI

                def take_val(n, s, i=0):
                    act.wait_ge(block_done, n + 1 + RING * i)
                    if s:
                        act.wait_ge(sem("val_convolved"), g0 + s + i)
                    nc.scalar.activation(U[:, 0, :, 1:T + 1], PS[0][:, :].rearrange("p (m t) -> p m t", m=2),
                                         ACT.Copy).then_inc(evacuated, 1)

                def take_gate(n, s, i=0):
                    act.wait_ge(block_done, n + 1 + RING * i)
                    if s:
                        act.wait_ge(sem("gate_convolved"), g0 + s + i)
                    nc.scalar.activation(U[:, 1, :, 1:T + 1], PS[1][:, :].rearrange("p (m t) -> p m t", m=2),
                                         ACT.Copy).then_inc(evacuated, 1)

                act.wait_ge(sem("u_zeroed"), 1)
                split_hi(act, n0 + 2)
                take_val(n0, 0)
                split_hi(act, n0 + 3)
                take_gate(n0 + 1, 0)
                with act.Fori(0, FI - 1) as i:
                    split_hi(act, n0 + 4, i)
                    hidden_hi(g0, 0, i)
                    take_val(n0 + 2, 1, i)
                    act.wait_ge(block_done, n0 + 2 + RING * i)
                    hidden_copy(g0, 0, n0, i)
                    split_hi(act, n0 + 5, i)
                    take_gate(n0 + 3, 1, i)
                    split_hi(act, n0 + 6, i)
                hidden_hi(g0, FI - 1)
                act.wait_ge(block_done, n0 + 3 * FI - 1)
                hidden_copy(g0, FI - 1, n0)
                split_hi(act, n0 + 3 * FI + 1)

            act.wait_ge(consts_landed, 16 * 6)
            split_hi(act, 0)
            split_hi(act, 1)
            squares(0)
            nc.scalar.activation(small[:, 0:8], vec("c_2", 0, 8), ACT.Silu).then_inc(sem("silu_c_ready"), 1)
            norm_split(0)
            act.wait_ge(sem("rank_rows"), 1)
            nc.scalar.activation(R16, PS[3][0:16, :].rearrange("p (d t) -> p d t", d=2), ACT.Copy)\
                .then_inc(sem("rank_rows_taken"), 1)
            act.wait_ge(sem("gate_logits"), 1)
            for d in range(2):
                name = "gla_b_gate_b" if d else "gla_b_gate_f"
                for h in range(GH_):
                    last = nc.scalar.activation(LA[:, 4 * d + h, :], PS[4 + 2 * d + h // 2][:, (h % 2) * T:(h % 2 + 1) * T],
                                                ACT.Identity, bias=vec(name, h))
            ch.step(last)
            ch.step(nc.scalar.activation(TMP8, LA, ACT.Abs))
            ch.step(nc.scalar.activation(TMP8, TMP8, ACT.Exp, scale=-1.0))
            nc.scalar.activation(TMP8, TMP8, ACT.Ln, bias=1.0).then_inc(sem("softplus_ready"), 1)
            for j in range(2):
                take(N_GIN + j, j, E_GIN, Q[:, 2 * j:2 * j + 2, :], scale=float(P) ** -0.5)
            for j in range(2):
                take(N_GIN + 2 + j, j, E_GIN, K[:, 2 * j:2 * j + 2, :])
            act.wait_ge(sem("gla_sums_ready"), 1)
            nc.scalar.activation(QD, HF, ACT.Exp, scale=1.0 / 16).then_inc(sem("gla_exps"), 1)
            nc.scalar.activation(KI, HF, ACT.Exp, scale=-1.0 / 16).then_inc(sem("gla_exps"), 1)
            nc.scalar.activation(DEC[:, 0:16].rearrange("p (h c) -> p h c", c=NC),
                                 HF[:, 0:4, CH - 1:T:CH], ACT.Exp, scale=1.0 / 16)
            nc.scalar.activation(DEC[:, 16:32].rearrange("p (h c) -> p h c", c=NC),
                                 HF[:, 4:8, 0:T:CH], ACT.Exp, scale=1.0 / 16)
            act.wait_ge(sem("gla_to_end"), 1)
            nc.scalar.activation(KE, KE, ACT.Exp, scale=1.0 / 16).then_inc(sem("gla_exps"), 1)
            for j in range(4):
                take(N_GIN + 4 + j, j, E_GIN, VT[:, :, j * 256:(j + 1) * 256])

            def turn_taken(h):
                act.wait_ge(sem("ke_turned"), h + 1)
                if h < 2:
                    act.wait_ge(sem("gla_decayed"), 1)
                else:
                    act.wait_ge(sem("chunk_kv"), h - 1)
                nc.scalar.activation(KET[h % 2], PS[4][:, :], ACT.Copy).then_inc(sem("ket_taken"), 1)

            turn_taken(0)
            for h in range(GH_):
                split_hi(act, N_GIN + 10 + h)
                if h + 1 < GH_:
                    turn_taken(h + 1)
                n = N_GIN + 8 + h
                act.wait_ge(block_done, n + 1)
                nc.scalar.activation(SG[:, 2 * h:2 * h + 2, :], PS[1][:, :].rearrange("p (m t) -> p m t", m=2),
                                     ACT.Silu).then_inc(evacuated, 1)
                act.wait_ge(sem("gla_out_summed"), h + 1)
                nc.scalar.activation(OT[:, 2 * h:2 * h + 2, :], PS[0][:, :].rearrange("p (v t) -> p v t", v=2),
                                     ACT.Copy).then_inc(sem("gla_out_taken"), 1)
            for q in range(2):
                act.wait_ge(sem("gla_square_sums"), q + 1)
                rsqrt(GRS[:, 2 * q:2 * q + 2, :], PS[5 + q][:, :].rearrange("p (m t) -> p m t", m=2), 1.0 / 256,
                      eps_rms, "gla_rstd")
            for q in range(2):
                act.wait_ge(sem("gla_out_normed"), q + 1)
                nc.scalar.activation(GH[:, 4 * q:4 * q + 4, :], OT[:, 4 * q:4 * q + 4, :], ACT.Copy)\
                    .then_inc(sem("gla_out_hi"), 1)
            split_for_projection(N_GOUT)

            squares(1)
            norm_split(1)
            mlp(0, N_F0)

            squares(2)
            norm_split(2)
            for j in range(5):
                take(N_QKV + j, j, E_QKV, QK[:, 2 * j:2 * j + 2, :])
            take(N_QKV + 5, 5, E_QKV, VA)
            act.wait_ge(evacuated, E_QKV + 5)
            for g in range(5):
                nc.scalar.activation(SQ10[:, 2 * g:2 * g + 2, :], QK[:, 2 * g:2 * g + 2, :], ACT.Square)\
                    .then_inc(sem("qk_squares"), 1)
            for g in range(5):
                act.wait_ge(sem("qk_square_sums"), g + 1)
                rsqrt(SQ10[:, 2 * g:2 * g + 2, :], PS[3 + g][:, :].rearrange("p (m t) -> p m t", m=2), 1.0 / P,
                      eps_rms, "qk_rstd")
            for h in range(QH):
                act.wait_ge(sem("neg_max_ready"), h + 1)
                if h:
                    act.wait_ge(sem("probs_turned"), h)
                for tt in range(2):
                    last = nc.scalar.activation(PR[:, tt, :], PS[3 + h % 2][:, tt * T:(tt + 1) * T], ACT.Exp,
                                                bias=small[:, 44 + 2 * (h % 2) + tt:45 + 2 * (h % 2) + tt],
                                                scale=float(P) ** -0.5,
                                                accum_out=small[:, 48 + 2 * (h % 2) + tt:49 + 2 * (h % 2) + tt])
                last.then_inc(sem("exps_ready"), 1)
                act.wait_ge(sem("probs_turned"), h + 1)
                if h:
                    act.wait_ge(sem("attn_out"), h)
                nc.scalar.activation(PT, PS[5 + h % 2][:, :].rearrange("p (s q) -> p s q", s=2), ACT.Copy)\
                    .then_inc(sem("probs_t_taken"), 1)
                act.wait_ge(sem("attn_out"), h + 1)
                nc.scalar.activation(GH[:, h, :], (PS[7] if h % 2 else PS[0])[:, 0:T], ACT.Copy)\
                    .then_inc(sem("attn_hi"), 1)
            split_for_projection(N_AOUT)

            squares(3)
            norm_split(3)
            mlp(1, N_F1)

            squares(4)
            norm_split(4)
            act.wait_ge(sem("lora_rows"), 1)
            act.wait_ge(sem("gate_convolved"), 2 * FI)
            nc.scalar.activation(U[:, 1, 0, 1:T + 1], PS[3][:, 0:T], ACT.Copy).then_inc(sem("lora_taken"), 1)
            act.wait_ge(sem("lora_shifted"), 1)
            nc.scalar.activation(LORA[0:64, :], LORA[0:64, :], ACT.Tanh).then_inc(sem("lora_ready"), 1)

            def take_block(n):
                name, j = NAME_AT[n]
                js = slice(2 * j, 2 * j + 2)
                act.wait_ge(block_done, n + 1)
                ps = PS[bank_of(n)][:, :].rearrange("p (m t) -> p m t", m=2)
                gates = ["gate", "og", "gc", "gr"]
                if name in gates:
                    turn = 4 * gates.index(name) + j
                    if turn >= 2:
                        act.wait_ge(sem("gate_applied"), turn - 1)
                    nc.scalar.activation(GT[:, turn % 2, :, :], ps, ACT.Silu if name == "og" else ACT.Sigmoid)\
                        .then_inc(evacuated, 1)
                elif name in "rkv":
                    turn = 3 * j + "rkv".index(name)
                    if turn:
                        act.wait_ge(sem("shifted"), turn)
                    nc.scalar.activation(U[:, 1, :, 1:T + 1], ps, ACT.Copy).then_inc(evacuated, 1)
                elif name == "val":
                    act.wait_ge(sem("u31_zeroed"), 1)
                    nc.scalar.activation(U31[:, js, 30:], ps, ACT.Copy).then_inc(evacuated, 1)
                elif name == "rog":
                    act.wait_ge(sem("x_aside_stored"), 16)
                    nc.scalar.activation(ROG[:, js, :], ps, ACT.Silu).then_inc(evacuated, 1)
                elif name == "cout":
                    nc.scalar.activation(HF[:, js, :], ps, ACT.Copy).then_inc(evacuated, 1)
                elif name == "rout":
                    nc.scalar.activation(YM[:, js, :], ps, ACT.Copy).then_inc(evacuated, 1)
                if name in ("og", "gr"):
                    ready, src, hi = (("conv_y_ready", CONV, "conv_y_hi") if name == "og" else
                                      ("m_ready", YM, "m_hi"))
                    act.wait_ge(sem(ready), j + 1)
                    nc.scalar.activation(GH[:, js, :], src[:, js, :], ACT.Copy).then_inc(sem(hi), 1)

            def split_ahead(n):
                if n + 2 < N_END:
                    split_hi(act, n + 2)

            def ln(step):
                if step == 2:
                    act.wait_ge(sem("conv_centred"), 1)
                    nc.scalar.activation(S8, CONV, ACT.Square).then_inc(sem("ln_squares"), 1)
                if step == 4:
                    act.wait_ge(sem("ln_sums"), 2)
                    rsqrt(LNR, PS[2][:, 0:T], 1.0 / D, eps_ln, "ln_rstd")
                if step == 6:
                    act.wait_ge(sem("conv_normed"), 1)
                    for g in range(KT):
                        ins = nc.scalar.activation(CONV[:, g, :], CONV[:, g, :], ACT.Silu, bias=vec("conv_ln_b_2", g))
                    ins.then_inc(sem("conv_silu"), 1)

            def slot(p, k):
                for item in between.get((p, k), ()):
                    if item[0] == "quarter" and item[2] == 0:
                        split_ahead(item[1])
                    elif item[0] == "take":
                        take_block(item[1])
                    elif item[0] == "ln":
                        ln(item[1])

            def front(p, part):
                if part == 0:
                    act.wait_ge(sem("pre_acts"), p + 1)
                    nc.scalar.activation(SIG, PS[6][:, 0:T], ACT.Sigmoid, bias=vec("rwkv_w0_2", p))
                    nc.scalar.activation(AA, PS[2][:, 0:T], ACT.Sigmoid, bias=vec("rwkv_a0_2", p))\
                        .then_inc(sem("sigmoids_ready"), 1)
                elif part == 1:
                    act.wait_ge(sem("kk_sums_kept"), p + 1)
                    ch.step(nc.scalar.activation(BB, BB, ACT.Ln, scale=65536.0))
                    nc.scalar.activation(BB, BB, ACT.Exp, scale=-0.5, bias=half_ln)\
                        .then_inc(sem("kk_rsqrt"), 1)

            def middle(p):
                slot(p, 0)
                act.wait_ge(sem("cums_ready"), p + 1)
                if p:
                    act.wait_ge(sem("rwkv_out_summed"), p)
                nc.scalar.activation(KR[:, :, 0, :], ck(TMP), ACT.Exp, scale=DECAY)
                nc.scalar.activation(KR[:, :, 1, :], ck(CUM), ACT.Exp, scale=DECAY)
                nc.scalar.activation(BK[:, :, 0, :], ck(CUM), ACT.Exp, scale=-DECAY)
                nc.scalar.activation(BKE[:, :, 0, :], ck(SIG), ACT.Exp, scale=DECAY)
                nc.scalar.activation(DECR, CUM[:, CH - 1:T:CH], ACT.Exp, scale=DECAY).then_inc(sem("rwkv_exps"), 1)
                slot(p, 1)
                slot(p, 2)
                act.wait_ge(sem("v_turned"), p + 1)
                act.wait_ge(sem("uv_zeroed"), p + 1)
                for c in range(NC):
                    r = 64 * (c % 2)
                    nc.scalar.activation(UV[64:128, c, :, :],
                                         PS[7][r:r + 64, (c // 2) * P:(c // 2 + 1) * P].rearrange("p (h v) -> p h v", h=2),
                                         ACT.Copy)
                slot(p, 3)
                act.wait_ge(sem("bke_turned"), p + 1)
                nc.scalar.activation(TK, PS[2][:, :].rearrange("p (c n) -> p c n", c=NC), ACT.Copy)\
                    .then_inc(sem("uv_ready"), 1)
                slot(p, 4)
                act.wait_ge(sem("xt_turned"), p + 1)
                nc.scalar.activation(XI, PS[3][0:64, :], ACT.Copy).then_inc(sem("x_inv_ready"), 1)
                for lev in range(5):
                    act.wait_ge(sem("y_summed"), 5 * p + lev + 1)
                    nc.scalar.activation(YI, PS[4][0:64, :], ACT.Copy).then_inc(sem("y_ready"), 1)
                    slot(p, 5 + 2 * lev)
                    slot(p, 6 + 2 * lev)

            def chain(p, c):
                act.wait_ge(sem("u_summed"), 4 * p + c + 1)
                nc.scalar.activation(UV[0:64, c, :, :], PS[4][0:64, 0:P].rearrange("p (h v) -> p h v", h=2),
                                     ACT.Copy, scale=-1.0).then_inc(sem("u_ready"), 1)
                if c < NC - 1:
                    slot(p, 15 + c)
                else:
                    act.wait_ge(sem("rwkv_out_summed"), p + 1)
                    nc.scalar.activation(R_[:, p, :], PS[7][:, 0:T], ACT.Copy).then_inc(sem("o_taken"), 1)

            for n in range(N_L3, N_RKV + 3):
                split_ahead(n)
                take_block(n)
            for part in range(3):
                front(0, part)
            for p in range(8):
                middle(p)
                for c in range(NC):
                    chain(p, c)
                    if p < 7 and c < 3:
                        front(p + 1, c)
            for g in range(4):
                act.wait_ge(sem("gn_centred"), g + 1)
                nc.scalar.activation(S8[:, 2 * g:2 * g + 2, :], R_[:, 2 * g:2 * g + 2, :], ACT.Square)\
                    .then_inc(sem("gn_squares"), 1)
            for g in range(4):
                act.wait_ge(sem("gn_sums"), 5 + g)
                rsqrt(S8[:, 2 * g:2 * g + 2, :], PS[3 + g][:, :].rearrange("p (m t) -> p m t", m=2),
                      1.0 / 64, eps_gn, "gn_rstd")
            for g in range(4):
                act.wait_ge(sem("rwkv_y_ready"), g + 1)
                nc.scalar.activation(GH[:, 2 * g:2 * g + 2, :], R_[:, 2 * g:2 * g + 2, :], ACT.Copy)\
                    .then_inc(sem("rwkv_y_hi"), 1)
            for n in range(PLACE["rout", 0], N_END):
                split_ahead(n)
                if NAME_AT[n][0] != "out":
                    take_block(n)
            squares(5)
            norm_split(5, last=True)

        @block.vector
        def _(dve):
            ch = Chain(dve, sem("dve_steps"))
            v = nc.vector

            def spread(ap, shape):
                return ap.broadcast_to(shape)

            def norm(i, w, modulate=False, last=False):
                dve.wait_ge(sem("rstd_ready"), i + 1)
                for g in range(4):
                    for k in (2 * g, 2 * g + 1):
                        ins = v.scalar_tensor_tensor(HF[:, k, :], X[:, k, :], vec(*w(k)), RS[:, :], ALU.mult, ALU.mult)
                        if modulate:
                            ch.step(ins)
                            ins = v.tensor_scalar(HF[:, k, :], HF[:, k, :], mod[:, 24 + k:25 + k], mod[:, k:k + 1],
                                                  ALU.mult, ALU.add)
                    ins.then_inc(sem("normed"), 1)
                if last:
                    return
                for g in range(4):
                    gs = slice(2 * g, 2 * g + 2)
                    dve.wait_ge(sem("rms_hi"), 4 * i + g + 1)
                    v.tensor_tensor(XL[:, gs, :], HF[:, gs, :], XH[:, gs, :].bitcast(F32), ALU.subtract)\
                        .then_inc(sem("rms_split"), 1)

            def lo(n):
                if n < N_END:
                    split_lo(dve, n)

            def add_projection(n0, a0, dst, add=True):
                for j in range(4):
                    lo(n0 + j + 2)
                    dve.wait_ge(block_done, n0 + j + 1)
                    ps = PS[(n0 + j) % RING][:, :].rearrange("p (m t) -> p m t", m=2)
                    d = dst[:, 2 * j:2 * j + 2, :]
                    if add:
                        ins = v.tensor_tensor(d, d, ps, ALU.add)
                    else:
                        ins = v.tensor_copy(d, ps)
                    ins.then_inc(out_added, 1)

            def mlp(layer, n0, e0):
                g0 = layer * FI
                cw, cb = COL["ffn_w_conv"] + 132 * layer, COL["ffn_b_conv"] + 44 * layer

                def tap(j, half, s, m, i):
                    base = (cb if j is None else cw + 44 * j) + 22 * half + 2 * s + m
                    return V[:, bass.ds(i * 2 + base, 1)] if not isinstance(i, int) else V[:, base:base + 1]

                def convolve(dst, half, s, ch, i=0):
                    for m in range(2):
                        ch.done(v.tensor_scalar(dst[:, m, :], U[:, half, m, 1:T + 1], tap(1, half, s, m, i),
                                                tap(None, half, s, m, i), ALU.mult, ALU.add))
                    for j, at in ((0, 0), (2, 2)):
                        for m in range(2):
                            ch.all(1)
                            ins = v.scalar_tensor_tensor(dst[:, m, :], U[:, half, m, at:at + T],
                                                         tap(j, half, s, m, i), dst[:, m, :], ALU.mult, ALU.add)
                            if j == 2 and m == 1:
                                ins.then_inc(sem("gate_convolved" if half else "val_convolved"), 1)
                            else:
                                ch.done(ins)

                def hidden(s, i=0):
                    dve.wait_ge(sem("gate_silu"), g0 + s + 1 + i)
                    if s or not isinstance(i, int):
                        dve.wait_ge(sem("val_convolved"), g0 + s + 1 + i)
                    v.tensor_tensor(HID, SGT, CV, ALU.mult).then_inc(sem("hidden_ready"), 1)
                    dve.wait_ge(sem("hidden_hi"), g0 + s + 1 + i)
                    v.tensor_tensor(GL[:, 0:2, :], HID, GH[:, 0:2, :].bitcast(F32), ALU.subtract)\
                        .then_inc(sem("hidden_split"), 1)

                split_lo(dve, n0 + 2)
                dve.wait_ge(evacuated, e0 + 1)
                convolve(CV, 0, 0, ch)
                split_lo(dve, n0 + 3)
                dve.wait_ge(evacuated, e0 + 2)
                convolve(CG, 1, 0, ch)
                with dve.Fori(0, FI - 1) as i:
                    ch.enter(i, 10)
                    split_lo(dve, n0 + 4, i)
                    hidden(0, i)
                    dve.wait_ge(evacuated, e0 + 3 + 2 * i)
                    convolve(CV, 0, 1, ch, i)
                    split_lo(dve, n0 + 5, i)
                    dve.wait_ge(evacuated, e0 + 4 + 2 * i)
                    convolve(CG, 1, 1, ch, i)
                    split_lo(dve, n0 + 6, i)
                ch.leave(FI - 1)
                hidden(FI - 1)
                split_lo(dve, n0 + 3 * FI + 1)
                dve.wait_ge(block_done, n0 + 3 * FI)
                for q in range(4):
                    x = X[:, 2 * q:2 * q + 2, :]
                    ins = v.tensor_tensor(x, x, PS[4 + q][:, :].rearrange("p (m t) -> p m t", m=2), ALU.add)
                ins.then_inc(sem("x_ready"), 1)

            ch.done(v.memset(ATT[:, :, :], 0.0))
            ch.done(v.memset(U[:, :, :, 0:1], 0.0))
            ch.step(v.memset(U[:, :, :, T + 1:T + 2], 0.0))
            dve.sem_inc(sem("u_zeroed"), 1)
            dve.wait_ge(consts_landed, 16 * 6)
            lo(0)
            lo(1)
            norm(0, lambda k: ("norm_mix", k))
            dve.wait_ge(sem("softplus_ready"), 1)
            ch.step(v.scalar_tensor_tensor(LA, LA, 0.0, TMP8, ALU.min, ALU.subtract))
            dve.wait_ge(sem("rank_rows"), 1)
            for t in range(8):
                ins = v.tensor_tensor_scan(HF[:, t, :], cst("scan"), LA[:, t, :], 0.0, ALU.mult, ALU.add)
            ch.step(ins)

            def chunks(ap):
                return ap.rearrange("p k (c t) -> p (k c) t", t=CH)

            hf, hb = chunks(HF[:, 0:4, :]), chunks(HF[:, 4:8, :])
            shape = [P, 16, CH]
            ch.step(v.tensor_tensor(chunks(TMP8[:, 0:4, :]), spread(hb[:, :, CH - 1:CH], shape), hb, ALU.subtract))
            ins = v.tensor_tensor(HF[:, 4:8, :], TMP8[:, 0:4, :], LA[:, 4:8, :], ALU.add)
            ins.then_inc(sem("gla_sums_ready"), 1)
            dve.wait_ge(sem("gla_sums_ready"), 1)
            v.tensor_tensor(chunks(KE[:, 0:4, :]), spread(hf[:, :, CH - 1:CH], shape), hf, ALU.subtract)
            v.tensor_tensor(chunks(KE[:, 4:8, :]), spread(hb[:, :, 0:1], shape), hb, ALU.subtract)\
                .then_inc(sem("gla_to_end"), 1)
            for n in range(2, 6):
                lo(n)
            dve.wait_ge(evacuated, E_GIN + 4)
            for e, (dst, src) in enumerate(((QD, Q), (KI, K), (KE, K))):
                dve.wait_ge(sem("gla_exps"), e + 1)
                for d in range(2):
                    ins = v.tensor_tensor(dst[:, 4 * d:4 * d + 4, :], dst[:, 4 * d:4 * d + 4, :], src, ALU.mult)
            ins.then_inc(sem("gla_decayed"), 1)
            dve.wait_ge(sem("gla_decayed"), 1)
            ch.done(v.memset(ATTS[1], 0.0))
            for n in range(6, 10):
                lo(n)

            def masked(h):
                dve.wait_ge(sem("att_scores"), h + 1)
                if h >= 2:
                    dve.wait_ge(sem("gla_out_summed"), h - 1)
                for d, m in enumerate(("mask_f", "mask_b")):
                    mask = cst(m).bitcast(I32).unsqueeze(1)
                    ch.all()
                    ins = v.copy_predicated(ATTS[h % 2], spread(mask, [P, 2, P]),
                                            PS[3][:, 2 * d * P:(2 * d + 2) * P].rearrange("p (a b) -> p a b", a=2))
                    if d == 0:
                        ch.done(ins)
                ins.then_inc(sem("att_masked"), 1)

            def states(h):
                sf, sbk = SF[h % 2], SBK[h % 2]
                dve.wait_ge(sem("chunk_kv"), h + 1)

                def decay(d, c):
                    j = 16 * d + 4 * h + c
                    return DEC[:, j:j + 1]

                ch.done(v.tensor_copy(sf[:, 0, :], kv_piece(0)))
                ch.done(v.tensor_copy(sbk[:, 0, :], kv_piece(3)))
                for j in range(1, 3):
                    ch.all(1)
                    ch.done(v.scalar_tensor_tensor(sf[:, j, :], sf[:, j - 1, :], decay(0, j), kv_piece(j), ALU.mult, ALU.add))
                    ch.all(1)
                    ins = v.scalar_tensor_tensor(sbk[:, j, :], sbk[:, j - 1, :], decay(1, 3 - j), kv_piece(3 + j),
                                                 ALU.mult, ALU.add)
                    if j == 1:
                        ch.done(ins)
                ins.then_inc(sem("states_ready"), 1)

            masked(0)
            for h in range(GH_):
                if h >= 2:
                    dve.wait_ge(sem("gla_out_summed"), h - 1)
                states(h)
                if h + 1 < GH_:
                    masked(h + 1)
                lo(N_GIN + 10 + h)
            oh = OT.rearrange("p (h w) t -> p h w t", w=2)
            for q in range(2):
                qs = slice(4 * q, 4 * q + 4)
                dve.wait_ge(sem("gla_rstd"), q + 1)
                for w in range(2):
                    o = oh[:, 2 * q:2 * q + 2, w, :]
                    ins = v.scalar_tensor_tensor(o, o, vec("gla_norm", w), GRS[:, 2 * q:2 * q + 2, :],
                                                 ALU.mult, ALU.mult)
                ch.step(ins)
                v.tensor_tensor(OT[:, qs, :], OT[:, qs, :], SG[:, qs, :], ALU.mult).then_inc(sem("gla_out_normed"), 1)
            for q in range(2):
                qs = slice(4 * q, 4 * q + 4)
                dve.wait_ge(sem("gla_out_hi"), q + 1)
                v.tensor_tensor(GL[:, qs, :], OT[:, qs, :], GH[:, qs, :].bitcast(F32), ALU.subtract)\
                    .then_inc(sem("gla_out_split"), 1)
            add_projection(N_GOUT, 0, X)
            dve.wait_ge(out_added, 4)
            dve.sem_inc(sem("x_ready"), 1)

            norm(1, lambda k: ("norm_ffn", k))
            mlp(0, N_F0, E_F0)

            norm(2, lambda k: ("norm_mix", 8 + k))
            for n in range(N_QKV + 2, N_QKV + 8):
                lo(n)
            for g in range(5):
                gs = slice(2 * g, 2 * g + 2)
                dve.wait_ge(sem("qk_rstd"), g + 1)
                v.scalar_tensor_tensor(QK[:, gs, :], QK[:, gs, :], vec("attn_k_norm" if g == 4 else "attn_q_norm"),
                                       SQ10[:, gs, :], ALU.mult, ALU.mult).then_inc(sem("qk_normed"), 1)
            for g in range(5):
                gs = slice(2 * g, 2 * g + 2)
                hs = slice(2 * (g % 4), 2 * (g % 4) + 2)
                dve.wait_ge(sem("qk_turned"), g + 1)
                two = [P, 2, T]
                ch.done(v.tensor_tensor(HF[:, hs, :], PS[3 + g][:, :].rearrange("p (m t) -> p m t", m=2),
                                        spread(cst("sin").unsqueeze(1), two), ALU.mult))
                ch.step(v.tensor_tensor(QK[:, gs, :], QK[:, gs, :], spread(cst("cos").unsqueeze(1), two), ALU.mult))
                v.tensor_tensor(QK[:, gs, :], QK[:, gs, :], HF[:, hs, :], ALU.add).then_inc(sem("qk_roped"), 1)
            for h in range(QH):
                dve.wait_ge(sem("scores_ready"), h + 1)
                mx = small[:, 44 + 2 * (h % 2):46 + 2 * (h % 2)]
                den = small[:, 48 + 2 * (h % 2):50 + 2 * (h % 2)]
                ch.step(v.tensor_reduce(mx, PS[3 + h % 2][:, :].rearrange("p (m t) -> p m t", m=2), AX_X, ALU.max))
                v.tensor_scalar(mx, mx, -float(P) ** -0.5, None, ALU.mult).then_inc(sem("neg_max_ready"), 1)
                dve.wait_ge(sem("exps_ready"), h + 1)
                ch.step(v.reciprocal(den, den))
                for tt in range(2):
                    ins = v.tensor_scalar(PR[:, tt, :], PR[:, tt, :], den[:, tt:tt + 1], None, ALU.mult)
                ins.then_inc(sem("probs_ready"), 1)
                dve.wait_ge(sem("attn_hi"), h + 1)
                v.tensor_tensor(GL[:, h, :], (PS[7] if h % 2 else PS[0])[:, 0:T], GH[:, h, :].bitcast(F32),
                                ALU.subtract).then_inc(sem("attn_split"), 1)
            add_projection(N_AOUT, 4, X)
            dve.wait_ge(out_added, 8)
            dve.sem_inc(sem("x_ready"), 1)

            norm(3, lambda k: ("norm_ffn", 8 + k))
            mlp(1, N_F1, E_F1)

            dve.wait_ge(sem("mod_summed"), 1)
            ch.step(v.tensor_tensor(mod[:, 0:24], PS[2][:, 0:24], vec("ada_b_2", 0, 24), ALU.add))
            ch.step(v.tensor_scalar(mod[:, 24:32], mod[:, 8:16], 1.0, None, ALU.add))
            norm(4, lambda k: ("norm_g_2", k), modulate=True)

            def shift(dst, half, mu0, name, m_count=2):
                z, before = U[:, half, 0:m_count, 1:T + 1], U[:, half, 0:m_count, 0:T]
                ch.step(v.tensor_tensor(dst, before, z, ALU.subtract))
                for m in range(m_count):
                    ins = v.scalar_tensor_tensor(dst[:, m, :], dst[:, m, :], vec("rwkv_mu_2", mu0 + m), z[:, m, :],
                                                 ALU.mult, ALU.add)
                ins.then_inc(sem(name), 1)

            dve.wait_ge(sem("lora_taken"), 1)
            shift(LORA.unsqueeze(1), 1, 24, "lora_shifted", 1)
            v.memset(U31[:, :, 0:30], 0.0).then_inc(sem("u31_zeroed"), 1)

            def use_block(n):
                name, j = NAME_AT[n]
                js = slice(2 * j, 2 * j + 2)
                if name in ("val", "rog", "cout", "rout"):
                    return
                dve.wait_ge(evacuated, taken(n))
                if name in "rkv":
                    first = 8 * "rkv".index(name) + 2 * j
                    shift(RKV[:, first:first + 2, :], 1, first, "shifted")
                    return
                gates = ["gate", "og", "gc", "gr"]
                g = GT[:, (4 * gates.index(name) + j) % 2, :, :]
                if name == "gate":
                    v.tensor_tensor(U31[:, js, 30:], U31[:, js, 30:], g, ALU.mult).then_inc(sem("gate_applied"), 1)
                elif name == "og":
                    if j == 0:
                        dve.wait_ge(sem("conv_silu"), 1)
                    v.tensor_tensor(CONV[:, js, :], CONV[:, js, :], g, ALU.mult).then_inc(sem("gate_applied"), 1)
                    dve.wait_ge(sem("gate_applied"), 4 + j + 1)
                    dve.sem_inc(sem("conv_y_ready"), 1)
                    low(CONV, "conv_y", j)
                elif name == "gc":
                    v.tensor_tensor(HF[:, js, :], HF[:, js, :], g, ALU.mult).then_inc(sem("gate_applied"), 1)
                else:
                    v.tensor_tensor(YM[:, js, :], YM[:, js, :], g, ALU.mult).then_inc(sem("gate_applied"), 1)
                    dve.wait_ge(sem("gate_applied"), 12 + j + 1)
                    v.tensor_tensor(YM[:, js, :], YM[:, js, :], HF[:, js, :], ALU.add).then_inc(sem("m_ready"), 1)
                    low(YM, "m", j)

            def low(src, name, g):
                gs = slice(2 * g, 2 * g + 2)
                dve.wait_ge(sem(name + "_hi"), g + 1)
                v.tensor_tensor(GL[:, gs, :], src[:, gs, :], GH[:, gs, :].bitcast(F32), ALU.subtract)\
                    .then_inc(sem(name + "_split"), 1)

            tap_at = []

            def taps(first, last):
                for u in range(first, last):
                    j, k = u // KT, u % KT
                    if j == 0:
                        if k == 0:
                            dve.wait_ge(sem("gate_applied"), 4)
                        ins = v.tensor_scalar(CONV[:, k, :], U31[:, k, 0:T], vec("conv_k_2", k), vec("conv_b_2", k),
                                              ALU.mult, ALU.add)
                    else:
                        dve.wait_ge(sem("dve_steps"), tap_at[u - KT])
                        ins = v.scalar_tensor_tensor(CONV[:, k, :], U31[:, k, j:j + T], vec("conv_k_2", KT * j + k),
                                                     CONV[:, k, :], ALU.mult, ALU.add)
                    ch.done(ins)
                    tap_at.append(ch.n)
                if last == TAPS:
                    ch.all()
                    dve.sem_inc(sem("conv_done"), 1)

            def ln(step):
                if step == 1:
                    dve.wait_ge(sem("ln_sums"), 1)
                    for g in range(KT):
                        ins = v.scalar_tensor_tensor(CONV[:, g, :], PS[2][:, 0:T], -1.0 / D, CONV[:, g, :],
                                                     ALU.mult, ALU.add)
                    ins.then_inc(sem("conv_centred"), 1)
                if step == 5:
                    dve.wait_ge(sem("ln_rstd"), 1)
                    for g in range(KT):
                        ins = v.scalar_tensor_tensor(CONV[:, g, :], CONV[:, g, :], vec("conv_ln_g_2", g), LNR,
                                                     ALU.mult, ALU.mult)
                    ins.then_inc(sem("conv_normed"), 1)

            def slot(p, k):
                for item in between.get((p, k), ()):
                    if item[0] == "take":
                        use_block(item[1])
                    elif item[0] == "taps":
                        taps(item[1], item[2])
                    elif item[0] == "ln":
                        ln(item[1])

            def ck(ap):
                return ap.rearrange("p (c t) -> p c t", c=NC)

            def systems(ap, h):
                return ap[:, h * 256:(h + 1) * 256].rearrange("p (c t) -> p c t", c=NC)

            lev_shape = [64, NC, 64]

            def front(p, part):
                if part == 0:
                    dve.wait_ge(sem("shifted"), 3 * (p // 2) + 3)
                    ch.step(v.tensor_scalar(KK, K_[:, p, :], vec("rwkv_k_k_2", p), None, ALU.mult))
                    v.tensor_tensor(TMP, KK, KK, ALU.mult).then_inc(sem("kk_squares"), 1)
                elif part == 1:
                    dve.wait_ge(sem("kk_sums"), p + 1)
                    v.tensor_scalar(BB, PS[6][:, 0:T], 1e-24, None, ALU.max).then_inc(sem("kk_sums_kept"), 1)
                    ch.step(v.tensor_scalar(K2, AA, -1.0, vec("rwkv_k_a_2", p), ALU.add, ALU.mult))
                    ch.step(v.scalar_tensor_tensor(K2, K2, 1.0, K_[:, p, :], ALU.add, ALU.mult))
                    v.scalar_tensor_tensor(TMP, R_[:, p, :], vec("rwkv_r_k_2", p), K2, ALU.mult, ALU.mult)\
                        .then_inc(sem("rkrk_ready"), 1)
                    ch.done(v.tensor_tensor_scan(CUM, cst("scan"), SIG, 0.0, ALU.mult, ALU.add))
                else:
                    ch.all()
                    dve.wait_ge(sem("rkrk_sums"), p + 1)
                    ch.step(v.tensor_tensor(TMP, CUM, SIG, ALU.subtract))
                    v.tensor_tensor(ck(SIG), spread(ck(CUM)[:, :, CH - 1:CH], [P, NC, CH]), ck(CUM), ALU.subtract)\
                        .then_inc(sem("cums_ready"), 1)
                    dve.wait_ge(sem("kk_rsqrt"), p + 1)
                    ch.step(v.tensor_tensor(KK, KK, BB, ALU.mult))
                    ch.done(v.tensor_tensor(BB, KK, AA, ALU.mult))
                    ch.done(v.tensor_tensor(K_[:, p, :], PS[2][:, 0:T], V_[:, p, :], ALU.mult))
                    ch.all()

            def middle(p):
                if p:
                    dve.wait_ge(sem("rwkv_out_summed"), p)
                v.memset(UV[0:64, :, :, :], 0.0).then_inc(sem("uv_zeroed"), 1)
                v.memset(ST, 0.0).then_inc(sem("state_ready"), 1)
                slot(p, 0)
                dve.wait_ge(sem("rwkv_exps"), p + 1)
                v.tensor_tensor(KR[:, :, 0, :], KR[:, :, 0, :], ck(KK), ALU.mult)
                v.tensor_tensor(KR[:, :, 1, :], KR[:, :, 1, :], ck(R_[:, p, :]), ALU.mult)
                ch.step(v.tensor_tensor(BK[:, :, 1, :], BK[:, :, 0, :], ck(K2), ALU.mult))
                v.tensor_tensor(BK[:, :, 0, :], BK[:, :, 0, :], ck(BB), ALU.mult).then_inc(sem("rwkv_decayed"), 1)
                ch.step(v.tensor_tensor(BKE[:, :, 1, :], BKE[:, :, 0, :], ck(K2), ALU.mult))
                v.tensor_tensor(BKE[:, :, 0, :], BKE[:, :, 0, :], ck(BB), ALU.mult).then_inc(sem("bke_ready"), 1)
                slot(p, 1)
                slot(p, 2)
                dve.wait_ge(sem("rwkv_scores"), p + 1)
                for h in range(2):
                    ins = v.tensor_tensor(SC[h], PS[5 + h][:, :].rearrange("p (c n) -> p c n", c=NC),
                                          spread(cst("scmask").unsqueeze(1), [P, NC, P]), ALU.mult)
                ch.step(ins)

                def level(lev):
                    m = spread(cst("lev")[0:64, 64 * lev:64 * (lev + 1)].unsqueeze(1), lev_shape)
                    for h in range(2):
                        ins = v.tensor_tensor(systems(LM, h), SC[h][0:64, :, 0:64], m, ALU.mult)
                    return ins

                ch.step(level(0))
                for h in range(2):
                    ins = v.tensor_tensor(systems(XT, h), spread(ident[0:64, 0:64].unsqueeze(1), lev_shape),
                                          systems(LM, h), ALU.subtract)
                ins.then_inc(sem("xt_ready"), 1)
                dve.wait_ge(sem("xt_ready"), 5 * p + 1)
                level(1).then_inc(sem("level_ready"), 1)
                slot(p, 3)
                slot(p, 4)
                for lev in range(5):
                    q = 5 * p + lev + 1
                    if lev < 4:
                        dve.wait_ge(sem("y_summed"), q)
                        level(lev + 2).then_inc(sem("level_ready"), 1)
                    slot(p, 5 + 2 * lev)
                    if lev < 4:
                        dve.wait_ge(sem("x_summed"), 4 * p + lev + 1)
                    else:
                        dve.wait_ge(sem("xt_summed"), q)
                    v.tensor_tensor(XT, XT, PS[5][0:64, :], ALU.subtract)\
                        .then_inc(sem("xt_ready" if lev < 4 else "inverse_ready"), 1)
                    if lev < 4:
                        v.tensor_tensor(XI, XI, PS[6][0:64, :], ALU.subtract).then_inc(sem("x_inv_ready"), 1)
                    slot(p, 6 + 2 * lev)

            def chain(p, c):
                dve.wait_ge(sem("rhs_summed"), 4 * p + c + 1)
                v.tensor_copy(RHS, PS[3][0:64, 0:P]).then_inc(sem("rhs_ready"), 1)
                if c < NC - 1:
                    slot(p, 15 + c)
                    dve.wait_ge(sem("update_summed"), 4 * p + c + 1)
                    for h in range(2):
                        hs = slice(64 * h, 64 * h + 64)
                        ins = v.scalar_tensor_tensor(ST[hs, hs], ST[hs, hs], DECR[hs, c:c + 1], PS[5][hs, hs],
                                                     ALU.mult, ALU.add)
                    ins.then_inc(sem("state_ready"), 1)

            for n in range(N_L3, N_RKV + 3):
                use_block(n)
            taps(0, TAPS_BEFORE)
            for part in range(3):
                front(0, part)
            for p in range(8):
                middle(p)
                for c in range(NC):
                    chain(p, c)
                    if p < 7 and c < 3:
                        front(p + 1, c)

            for g in range(4):
                gs = slice(2 * g, 2 * g + 2)
                dve.wait_ge(sem("gn_sums"), g + 1)
                v.scalar_tensor_tensor(R_[:, gs, :], PS[3 + g][:, :].rearrange("p (m t) -> p m t", m=2), -1.0 / 64,
                                       R_[:, gs, :], ALU.mult, ALU.add).then_inc(sem("gn_centred"), 1)
            for g in range(4):
                gs = slice(2 * g, 2 * g + 2)
                dve.wait_ge(sem("gn_rstd"), g + 1)
                for k in (2 * g, 2 * g + 1):
                    ch.done(v.scalar_tensor_tensor(R_[:, k, :], R_[:, k, :], vec("rwkv_gn_g_2", k), S8[:, k, :],
                                                   ALU.mult, ALU.mult))
                ch.all()
                for k in (2 * g, 2 * g + 1):
                    ch.done(v.scalar_tensor_tensor(R_[:, k, :], R_[:, k, :], vec("rwkv_gn_b_2", k), K_[:, k, :],
                                                   ALU.add, ALU.add))
                ch.all()
                v.tensor_tensor(R_[:, gs, :], R_[:, gs, :], ROG[:, gs, :], ALU.mult).then_inc(sem("rwkv_y_ready"), 1)
                low(R_, "rwkv_y", g)
            for n in range(PLACE["rout", 0], PLACE["out", 0]):
                use_block(n)
            dve.wait_ge(sem("x_back"), 16)
            for j in range(4):
                n = PLACE["out", j]
                dve.wait_ge(block_done, n + 1)
                for m in range(2):
                    k = 2 * j + m
                    ins = v.scalar_tensor_tensor(X[:, k, :], PS[bank_of(n)][:, m * T:(m + 1) * T],
                                                 mod[:, 16 + k:17 + k], X[:, k, :], ALU.mult, ALU.add)
                ins.then_inc(out_added, 1)
            dve.wait_ge(out_added, 12)
            dve.sem_inc(sem("x_ready"), 1)
            norm(5, lambda k: ("final_g_2", k), last=True)
            dve.wait_ge(sem("normed"), 24)
            dve.sem_inc(sem("result_ready"), 1)


_WEIGHTS = ["gla_w_in", "gla_w_gate_up_f", "gla_w_gate_up_b", "gla_w_out", "attn_w_qkv", "attn_w_out", "ada_w_2",
            "w_in_2", "w_conv_out_2", "rwkv_w2_2", "rwkv_a2_2", "w_rwkv_out_2", "w_out_2"]


def kernel(**inputs):
    import concourse.bacc as bacc
    from concourse.bass_utils import run_bass_kernel_spmd as run

    x = np.asarray(inputs["x"])
    arrays = {
        "in_x": np.ascontiguousarray(x[0].T.reshape(KT, P, T).transpose(1, 0, 2)),
        "in_vecs": np.ascontiguousarray(
            np.concatenate([np.asarray(inputs[n]).reshape(-1, P) for n, _ in VECS], axis=0).T),
        "in_consts": constants(),
    }
    for n in _WEIGHTS:
        arrays["in_" + n] = np.ascontiguousarray(np.asarray(inputs[n])[0])
    for n in ("ffn_w_up", "ffn_w_down"):
        arrays["in_" + n] = np.ascontiguousarray(inputs[n])
    nc = bacc.Bacc("TRN2", target_bir_lowering=False, num_devices=1)
    a = {n[3:]: nc.dram_tensor(n, v.shape, mybir.dt.from_np(v.dtype), kind="ExternalInput").ap()
         for n, v in arrays.items()}
    out = nc.dram_tensor("out", (P, KT, T), F32, kind="ExternalOutput").ap()
    a["x_aside"] = nc.dram_tensor("x_aside", (P, KT, T), F32, kind="Internal").ap()
    program(nc, a, out)
    r = run(nc, [arrays], core_ids=[0])
    y = r.results[0]["out"]
    return np.ascontiguousarray(y.transpose(1, 0, 2).reshape(D, T).T)[None]
```

```python
from contextlib import ExitStack

import numpy as np

import concourse.bass as bass
from concourse import mybir

F32 = mybir.dt.float32
F32R = mybir.dt.float32r
I32 = mybir.dt.int32
ALU = mybir.AluOpType
ACT = mybir.ActivationFunctionType
AX_X = mybir.AxisListType.X

P = 128
D = 1024
T = 256
KT = D // P
FF = 2816
FI = FF // 256
CH = 64
NC = T // CH
GH_ = 4
QH, KVH = 8, 2
RING = 3
BW = 256
EPS = 1e-6
LN_EPS = 1e-5
GN_EPS = 64e-5
DECAY = -float(np.exp(np.float32(-0.5)))
W2 = 1024
N_GIN = 0
N_GOUT = N_GIN + 12
N_F0 = N_GOUT + 4
N_QKV = N_F0 + 3 * FI
N_AOUT = N_QKV + 6
N_F1 = N_AOUT + 4
N_L3 = N_F1 + 3 * FI
N_CV = N_L3
N_RKV = N_CV + 4
N_CG = N_RKV + 3
N_PAIRS = N_CG + 4
ORDER = []
for _j in range(1, 4):
    ORDER += [("r", _j), ("k", _j), ("v", _j)]
    ORDER += [("rog", 2 * _j - 2), ("rog", 2 * _j - 1)] if _j < 3 else []
for _name in ("og", "cout", "gc", "gr", "rout", "out"):
    ORDER += [(_name, _j) for _j in range(4)]
PLACE = {_item: N_PAIRS + _i for _i, _item in enumerate(ORDER)}
PLACE.update({("r", 0): N_RKV, ("k", 0): N_RKV + 1, ("v", 0): N_RKV + 2})
N_END = N_PAIRS + len(ORDER)
NAME_AT = {_n: _item for _item, _n in PLACE.items()}
for _j in range(4):
    NAME_AT[N_CV + _j], NAME_AT[N_CG + _j] = ("val", _j), ("gate", _j)


QKV_ORDER = (4, 5, 0, 1, 2, 3)


def bank_of(n):
    if N_GIN + 8 <= n < N_GOUT:
        return 1
    if N_AOUT <= n < N_F1:
        return 5 + (n - N_AOUT) % RING
    return n % RING if n < N_L3 else n % 2


VECS = [("norm_mix", 16), ("norm_ffn", 16), ("gla_b_gate_f", 4), ("gla_b_gate_b", 4), ("gla_norm", 2),
        ("attn_q_norm", 1), ("attn_k_norm", 1), ("ffn_w_conv", 264), ("ffn_b_conv", 88), ("c_2", 8),
        ("ada_b_2", 24), ("norm_g_2", 8), ("conv_k_2", 248), ("conv_b_2", 8), ("conv_ln_g_2", 8),
        ("conv_ln_b_2", 8), ("rwkv_mu_2", 25), ("rwkv_w0_2", 8), ("rwkv_a0_2", 8), ("rwkv_k_k_2", 8),
        ("rwkv_k_a_2", 8), ("rwkv_r_k_2", 8), ("rwkv_gn_g_2", 8), ("rwkv_gn_b_2", 8), ("final_g_2", 8)]
COL = {}
_at = 0
for _name, _n in VECS:
    COL[_name] = _at
    _at += _n
NV = _at

CONSTS = [("ident", 128), ("ones", 128), ("blk", 128), ("rot", 128), ("cos", 256), ("sin", 256),
          ("scan", 256), ("scmask", 128), ("lev", 6 * 64), ("mask_f", 128), ("mask_b", 128), ("eps", 4)]
CC = {}
_at = 0
for _name, _n in CONSTS:
    CC[_name] = (_at, _at + _n)
    _at += _n
NCST = _at


def constants():
    c = np.zeros((P, NCST), np.float32)
    i = np.arange(P)

    def put(name, a):
        c[:, CC[name][0]:CC[name][1]] = a

    put("eps", np.array([[EPS, LN_EPS, GN_EPS, 0.5 * np.log(65536.0)]]))
    put("ident", np.eye(P))
    put("ones", 1.0)
    put("blk", i[:, None] // 64 == i[None, :] // 64)
    rot = np.zeros((P, P), np.float32)
    rot[i[64:], i[:64]] = -1.0
    rot[i[:64], i[64:]] = 1.0
    put("rot", rot)
    f = np.float32
    tok = np.arange(T)
    inv = f(10000.0) ** (-np.arange(32, dtype=f) / f(32))
    ang = np.concatenate([(tok // 64).astype(f)[:, None] * inv, (tok % 64).astype(f)[:, None] * inv], -1)
    put("cos", np.tile(np.cos(ang).T, (2, 1)))
    put("sin", np.tile(np.sin(ang).T, (2, 1)))
    put("scan", (np.arange(T) % CH != 0)[None, :])
    s, t = i[:, None], i[None, :]
    src = s % CH
    put("scmask", np.where(t < CH, src < t % CH, src <= t % CH))
    for lev in range(6):
        a, b = np.arange(P)[:, None], np.arange(64)[None, :]
        h = 1 << lev
        c[:, CC["lev"][0] + 64 * lev:CC["lev"][0] + 64 * (lev + 1)] = (
            (a // (2 * h) == b // (2 * h)) & (a // h % 2 == 0) & (b // h % 2 == 1))
    same = s // CH == t // CH
    c.view(np.int32)[:, CC["mask_f"][0]:CC["mask_f"][1]] = same & (s <= t)
    c.view(np.int32)[:, CC["mask_b"][0]:CC["mask_b"][1]] = same & (s > t)
    return c


class Chain:

    def __init__(self, eng, sem):
        self.eng, self.sem, self.n, self.turn = eng, sem, 0, None

    def done(self, ins):
        ins.then_inc(self.sem, 1)
        self.n += 1

    def value(self, back=0):
        n = self.n - back
        return n if self.turn is None else self.turn[0] * self.turn[1] + n

    def all(self, back=0):
        self.eng.wait_ge(self.sem, self.value(back))

    def step(self, ins):
        self.done(ins)
        self.all()

    def enter(self, i, per):
        self.turn, self.first = (i, per), self.n

    def leave(self, trips):
        assert self.n - self.first == self.turn[1], (self.n - self.first, self.turn[1])
        self.n = self.first + trips * self.turn[1]
        self.turn = None


def program(nc, a, out):
    with ExitStack() as ctx:
        def sb(name, shape, dt=F32):
            return ctx.enter_context(nc.sbuf_tensor(name, shape, dt))[:]

        sems = {}

        def sem(name):
            if name not in sems:
                sems[name] = ctx.enter_context(nc.semaphore(name))
            return sems[name]

        X = sb("x", [P, KT, T])
        HF = sb("hf", [P, KT, T])
        XH, XL = sb("xh", [P, KT, T], F32R), sb("xl", [P, KT, T], F32R)
        GH, GL = sb("gh", [P, KT, T], F32R), sb("gl", [P, KT, T], F32R)
        RAW = sb("raw", [P, RING, KT, BW])
        WH, WL = sb("wh", [P, RING, KT, BW], F32R), sb("wl", [P, RING, KT, BW], F32R)
        BIG = sb("big", [P, 8, KT, T])
        V = sb("vecs", [P, NV])
        C = sb("consts", [P, NCST])
        U = sb("u", [P, 2, 2, T + 2])
        RS = sb("rs", [P, T])
        small = sb("small", [P, 64])
        mod = sb("mod", [P, 32])
        LNR = sb("ln_rstd_tile", [P, T])
        eps_rms, eps_ln, eps_gn, half_ln = (C[:, NCST - 4 + j:NCST - 3 + j] for j in range(4))
        PS = [ctx.enter_context(nc.psum_tensor(f"bank{i}", [P, 512], F32)) for i in range(8)]

        def cst(name):
            return C[:, CC[name][0]:CC[name][1]]

        def vec(name, j=0, n=1):
            return V[:, COL[name] + j:COL[name] + j + n]

        ident, ones, blk, rot = cst("ident"), cst("ones"), cst("blk"), cst("rot")

        def big(j, n=KT):
            return BIG[:, j, 0:n, :]

        BT = BIG[:, :, :, :].rearrange("p j k t -> p (j k) t")

        def tiles(j, n=1):
            return BT[:, j:j + n, :]

        def flat(j, n):
            return BT[:, j:j + n, :].rearrange("p k t -> p (k t)")

        raw_landed = [sem(f"raw_landed{i}") for i in range(RING)]
        w_hi_ready, w_lo_ready, block_done = sem("w_hi_ready"), sem("w_lo_ready"), sem("block_done")
        evacuated = sem("evacuated")
        out_added = sem("out_added")
        consts_landed = sem("consts_landed")

        def split_hi(act, n, i=0):
            act.wait_ge(raw_landed[n % RING], 16 * (n // RING + 1) + 16 * i)
            if n >= RING:
                act.wait_ge(block_done, n - RING + 1 + RING * i)
            nc.scalar.activation(WH[:, n % RING, :, :], RAW[:, n % RING, :, :], ACT.Copy)\
                .then_inc(w_hi_ready, 1)

        def split_lo(eng, n, i=0):
            eng.wait_ge(w_hi_ready, n + 1 + RING * i)
            eng.tensor_tensor(WL[:, n % RING, :, :], RAW[:, n % RING, :, :],
                              WH[:, n % RING, :, :].bitcast(F32), ALU.subtract).then_inc(w_lo_ready, 1)

        def load(sp, n, src, i=0):
            if n >= RING:
                sp.wait_ge(w_lo_ready, n - RING + 1 + RING * i)
            dst = RAW[:, n % RING, :, :]
            if len(src.shape) == 4:
                dst = dst.rearrange("p (k c) n -> p k c n", k=2)
            sp.dma_start(dst, src).then_inc(raw_landed[n % RING], 16)

        def cols(w, c0):
            return w[:, c0:c0 + BW].rearrange("(k p) n -> p k n", p=P)

        def three(ps, wh, wl, xh, xl, start, stop, moving_weights=False):
            if moving_weights:
                nc.tensor.matmul(ps, xh, wh, start=start, stop=False)
                nc.tensor.matmul(ps, xh, wl, start=False, stop=False)
                return nc.tensor.matmul(ps, xl, wh, start=False, stop=stop)
            nc.tensor.matmul(ps, wh, xh, start=start, stop=False)
            nc.tensor.matmul(ps, wh, xl, start=False, stop=False)
            return nc.tensor.matmul(ps, wl, xh, start=False, stop=stop)

        def product(pe, n, bank, xh, xl, i=0, moving_weights=False, ready=None, between_halves=None):
            pe.wait_ge(w_lo_ready, n + 1 + RING * i)
            s = n % RING
            for m in range(2):
                ps = PS[bank][:, m * T:(m + 1) * T]
                ms = slice(m * P, (m + 1) * P)
                if m and between_halves:
                    between_halves()
                for k in range(KT):
                    if ready and m == 0:
                        ready(k)
                    if moving_weights:
                        last = three(ps, WH[:, s, k, :], WL[:, s, k, :], xh[:, k, ms], xl[:, k, ms],
                                     k == 0, k == KT - 1, True)
                    else:
                        last = three(ps, WH[:, s, k, ms], WL[:, s, k, ms], xh[:, k, :], xl[:, k, :],
                                     k == 0, k == KT - 1)
            last.then_inc(block_done, 1)

        E_GIN = 0
        E_F0 = E_GIN + 12
        E_QKV = E_F0 + 2 * FI
        E_F1 = E_QKV + 6
        E_L3 = E_F1 + 2 * FI

        def taken(n):
            return E_L3 + n - N_L3 + 1

        w_r = sb("w_r", [P, KT, 32])
        w_up = BT[0:16, 48:52, :].rearrange("p (d a) t -> p d (a t)", d=2)
        w_lora = BT[:, 24:28, :].rearrange("p a (b c) -> p (a b) c", c=128)
        w2a2 = BT[:, 28:32, :].rearrange("p a b -> p (a b)")

        w_in = a["w_in_2"]
        block = ctx.enter_context(nc.Block())

        @block.sync
        def _(sp):
            sp.dma_start(X[:, :, :], a["x"]).then_inc(sem("x_landed"), 16)
            sp.dma_start(C[:, :], a["consts"]).then_inc(consts_landed, 16)
            sp.dma_start(V[:, :], a["vecs"]).then_inc(consts_landed, 16)
            load(sp, N_GIN, cols(a["gla_w_in"], 0))
            sp.dma_start(w_r[:, :, :], a["gla_w_in"][:, 3072:3104].rearrange("(k p) n -> p k n", p=P))\
                .then_inc(sem("rank_landed"), 16)
            sp.dma_start(w_up[:, 0, :], a["gla_w_gate_up_f"]).then_inc(sem("rank_landed"), 16)
            sp.dma_start(w_up[:, 1, :], a["gla_w_gate_up_b"]).then_inc(sem("rank_landed"), 16)

            def columns(w, n0, c0, count):
                for j in range(count):
                    load(sp, n0 + j, cols(w, c0 + j * BW))

            columns(a["gla_w_in"], N_GIN + 1, BW, 11)
            columns(a["gla_w_out"], N_GOUT, 0, 4)

            def mlp(layer, n0):
                up, down = a["ffn_w_up"][layer], a["ffn_w_down"][layer]
                down_b = down.rearrange("(i k p) n -> i p k n", k=2, p=P)
                load(sp, n0, cols(up, 0))
                load(sp, n0 + 1, cols(up, FF))
                with sp.Fori(0, FI - 1) as i:
                    def upc(first):
                        return up[:, bass.ds(i * BW + (first + BW), BW)].rearrange("(k p) n -> p k n", p=P)
                    load(sp, n0 + 2, upc(0), i)
                    load(sp, n0 + 3, upc(FF), i)
                    load(sp, n0 + 4, down[bass.ds(i * BW, BW), :].rearrange("(k p) (c n) -> p k c n", p=P, n=BW), i)
                load(sp, n0 + 3 * FI - 1, down[(FI - 1) * BW:FF, :].rearrange("(k p) (c n) -> p k c n", p=P, n=BW))

            mlp(0, N_F0)
            for j, part in enumerate(QKV_ORDER):
                load(sp, N_QKV + j, cols(a["attn_w_qkv"], part * BW))
            columns(a["attn_w_out"], N_AOUT, 0, 4)
            mlp(1, N_F1)
            sp.wait_ge(sem("attn_split"), QH)
            sp.dma_start(w_lora, w_in[:, 6 * D:6 * D + P].rearrange("(k p) n -> p k n", p=P))\
                .then_inc(sem("lora_landed"), 16)
            sp.dma_start(w2a2[0:64, :], a["rwkv_w2_2"]).then_inc(sem("lora_landed"), 16)
            sp.dma_start(w2a2[64:128, :], a["rwkv_a2_2"]).then_inc(sem("lora_landed"), 16)
            sources = {"val": (w_in, 0), "gate": (w_in, D), "og": (w_in, 2 * D), "r": (w_in, 3 * D),
                       "k": (w_in, 4 * D), "v": (w_in, 5 * D), "rog": (w_in, 6 * D + P),
                       "gc": (w_in, 7 * D + P), "gr": (w_in, 8 * D + P), "cout": (a["w_conv_out_2"], 0),
                       "rout": (a["w_rwkv_out_2"], 0), "out": (a["w_out_2"], 0)}
            for n in range(N_L3, N_END):
                name, j = NAME_AT[n]
                w, c0 = sources[name]
                load(sp, n, cols(w, c0 + j * BW))
                if n == N_RKV + 1:
                    sp.wait_ge(sem("normed"), 20)
                    sp.dma_start(a["x_aside"], X[:, :, :]).then_inc(sem("x_aside_stored"), 16)
                if NAME_AT[n] == ("rout", 3):
                    sp.wait_ge(sem("rwkv_y_split"), 4)
                    sp.wait_ge(sem("x_aside_stored"), 16)
                    sp.dma_start(X[:, :, :], a["x_aside"]).then_inc(sem("x_back"), 16)
            sp.wait_ge(sem("result_ready"), 1)
            sp.dma_start(out, HF[:, :, :]).then_inc(sem("result_stored"), 16)
            sp.wait_ge(sem("result_stored"), 16)

        Q, K = tiles(0, 4), tiles(4, 4)
        VT = BIG[:, 1, :, :].rearrange("p (a b) t -> p a (b t)", a=2)
        SG = tiles(16, 8)
        LA = tiles(24, 8)
        QD, KI, KE = tiles(32, 8), tiles(40, 8), tiles(48, 8)
        TMP8 = tiles(56, 8)
        OT = tiles(56, 8)
        SF = [tiles(24, 3), tiles(0, 3)]
        SBK = [tiles(27, 3), flat(3, 3).rearrange("p (a t) -> p a t", a=3)]
        KET = [flat(30, 2), flat(6, 2)]
        ATT = sb("att", [P, 2, P])
        ATTS = [ATT, HF[:, 6, :].rearrange("p (a t) -> p a t", a=2)]
        GSQ = [HF[:, 2 * h:2 * h + 2, :] for h in range(3)] + [tiles(44, 2)]
        GRS = tiles(40, 4)
        DEC = small[:, 8:40]
        R16 = U[0:16, 0, :, 1:T + 1]
        CV, CG = tiles(32, 2), tiles(34, 2)
        SGT, HID = tiles(36, 2), tiles(38, 2)

        def kv_piece(q):
            bank, at = [(5, 0), (7, 0), (5, 1), (7, 1), (6, 0), (2, 0)][q]
            return PS[bank][:, at * T:(at + 1) * T]

        QK = tiles(0, 10)
        VA = tiles(16, 2)
        PR = [tiles(18, 2), tiles(22, 2)]
        PT = [tiles(20, 2), tiles(34, 2)]
        QK_AT = (8, 0, 2, 4, 6)
        SQ10 = tiles(24, 10)
        RKV = tiles(0, 24)
        R_, K_, V_ = tiles(0, 8), tiles(8, 8), tiles(16, 8)
        SIG, AA, CUM, KK, K2, BB, TMP = (flat(40 + j, 1) for j in range(7))
        KR = flat(47, 2).rearrange("p (c s t) -> p c s t", c=NC, s=2)
        BK = flat(49, 2).rearrange("p (c s t) -> p c s t", c=NC, s=2)
        BKE = flat(51, 2).rearrange("p (c s t) -> p c s t", c=NC, s=2)
        SC = [flat(24 + 2 * h, 2).rearrange("p (c n) -> p c n", c=NC) for h in range(2)]
        TK = flat(53, 2).rearrange("p (c n) -> p c n", c=NC)
        XI, XT, YI = (flat(32 + 2 * j, 2)[0:64, :] for j in range(3))
        LM = flat(38, 2)[0:64, :]
        UV = U[:, :, :, :].rearrange("p a b t -> p (a b t)")[:, 0:512].rearrange("p (c h v) -> p c h v", c=NC, h=2)
        ST = ATT[:, 0, :]
        LORA = RS
        RHS = ATT[0:64, 1, :]
        DECR = small[:, 40:44]
        ROG = X
        YM = tiles(32, 8)
        U31 = flat(55, 9)[:, 0:KT * (T + 30)].rearrange("p (k t) -> p k t", k=KT)
        S8 = tiles(55, 8)
        CONV = HF
        GT = sb("gate_tiles", [P, 2, 2, T])
        TAPS = 31 * KT

        ada_acc = [flat(40 + 4 * h, 4) for h in range(3)]
        ada_ring = [flat(52 + 4 * h, 4) for h in range(2)]
        ada_tmp = flat(60, 4)
        sc_col = small[:, 0:8]
        ADA_STEPS = 3 + 21 * 2
        ada_v = a["ada_w_2"].rearrange("(k p) (h n) -> p k h n", p=P, h=3)

        @block.gpsimd
        def _(pool):
            split_lo(pool, 0)
            split_lo(pool, 1)
            pool.wait_ge(w_lo_ready, 4)
            split_lo(pool, 4)
            split_lo(pool, 5)
            for h in range(GH_):
                pool.wait_ge(sem("gla_out_taken"), h + 1)
                if h == GH_ - 1:
                    pool.wait_ge(sem("att_scores"), GH_)
                o = OT[:, 2 * h:2 * h + 2, :]
                nc.gpsimd.tensor_tensor(GSQ[h], o, o, ALU.mult).then_inc(sem("gla_squares"), 1)
            ch = Chain(pool, sem("ada_steps"))
            pool.wait_ge(sem("rms_split"), 4 * 2)
            pool.wait_ge(sem("silu_c_ready"), 1)
            for n in range(24):
                k, h = n // 3, n % 3
                if n < 2:
                    pool.dma_start(ada_ring[n], ada_v[:, k, h, :]).then_inc(sem(f"ada_landed{n % 2}"), 16)
            for n in range(24):
                k, h = n // 3, n % 3
                pool.wait_ge(sem(f"ada_landed{n % 2}"), 16 * (n // 2 + 1))
                if k == 0:
                    ch.step(nc.gpsimd.tensor_scalar(ada_acc[h], ada_ring[n % 2], sc_col[:, k:k + 1], None, ALU.mult))
                else:
                    ch.step(nc.gpsimd.tensor_scalar(ada_tmp, ada_ring[n % 2], sc_col[:, k:k + 1], None, ALU.mult))
                    ch.step(nc.gpsimd.tensor_tensor(ada_acc[h], ada_acc[h], ada_tmp, ALU.add))
                if n + 2 < 24:
                    pool.dma_start(ada_ring[n % 2], ada_v[:, (n + 2) // 3, (n + 2) % 3, :])\
                        .then_inc(sem(f"ada_landed{n % 2}"), 16)

            def qk_square(e):
                pool.wait_ge(evacuated, E_QKV + (e + 2 if e else 1))
                x = QK[:, QK_AT[e]:QK_AT[e] + 2, :]
                nc.gpsimd.tensor_tensor(SQ10[:, 2 * e:2 * e + 2, :], x, x, ALU.mult).then_inc(sem("qk_squares"), 1)

            def qk_cosine(e):
                pool.wait_ge(sem("qk_normed"), e + 1)
                nc.gpsimd.tensor_tensor(SQ10[:, 2 * e:2 * e + 2, :], QK[:, QK_AT[e]:QK_AT[e] + 2, :],
                                        cst("cos").unsqueeze(1).broadcast_to([P, 2, T]), ALU.mult)\
                    .then_inc(sem("qk_cosines"), 1)

            for e in (0, 1, 2):
                qk_square(e)
            qk_cosine(0)
            qk_cosine(1)
            qk_square(3)
            qk_square(4)
            for e in (2, 3, 4):
                qk_cosine(e)

            pool.wait_ge(w_lo_ready, N_L3 + 2)
            for n in range(N_L3 + 2, N_END):
                split_lo(pool, n)

        SLOTS = 18
        between = {}

        def put(p, slot, item):
            between.setdefault((p, slot), []).append(item)

        def put_blocks(p, names, first=0, step=1):
            slot = first
            for name in names:
                n = PLACE[name]
                for q in range(4):
                    put(p, min(slot, SLOTS - 1), ("quarter", n, q))
                    slot += step
                put(p, min(slot, SLOTS - 1), ("take", n))

        put_blocks(0, [("r", 1), ("k", 1), ("v", 1)])
        put_blocks(1, [("rog", 0), ("rog", 1)], 1, 2)
        put_blocks(2, [("r", 2), ("k", 2), ("v", 2)])
        put_blocks(3, [("rog", 2), ("rog", 3)], 1, 2)
        put_blocks(4, [("r", 3), ("k", 3), ("v", 3)])
        for k in range(7):
            put(4, 10 + k, ("ln", k))
        put_blocks(5, [("og", j) for j in range(4)])
        put_blocks(6, [("cout", j) for j in range(4)])
        put_blocks(7, [("gc", j) for j in range(4)])
        TAP_SLOTS = 4 * SLOTS + 8
        TAPS_BEFORE = 8
        for k in range(TAP_SLOTS):
            a0 = TAPS_BEFORE + (TAPS - TAPS_BEFORE) * k // TAP_SLOTS
            a1 = TAPS_BEFORE + (TAPS - TAPS_BEFORE) * (k + 1) // TAP_SLOTS
            put(k // SLOTS, k % SLOTS, ("taps", a0, a1))

        @block.tensor
        def _(pe):
            def sums(i):
                for g in range(4):
                    pe.wait_ge(sem("squares_ready"), 4 * i + g + 1)
                    for k in (2 * g, 2 * g + 1):
                        last = nc.tensor.matmul(PS[3][:, 0:T], ones, HF[:, k, :], start=k == 0, stop=k == KT - 1)
                last.then_inc(sem("square_sums"), 1)

            def out_projection(n0, a0, xh, xl, ready=None):
                for j in range(4):
                    if j >= RING:
                        pe.wait_ge(out_added, a0 + j - RING + 1)
                    product(pe, n0 + j, bank_of(n0 + j), xh, xl, ready=None if j else ready)

            def mlp(layer, n0, e0):
                g0 = layer * FI
                def ready(k):
                    if k % 2 == 0:
                        pe.wait_ge(sem("rms_split"), 4 * (2 * layer + 1) + k // 2 + 1)

                def up(n, s, i=0):
                    if s:
                        pe.wait_ge(evacuated, e0 + 2 * s - 1 + 2 * i)
                    product(pe, n, 0, XH, XL, i, ready=None if s else ready)
                    if s:
                        pe.wait_ge(evacuated, e0 + 2 * s + 2 * i)
                    product(pe, n + 1, 1, XH, XL, i)

                def down(n, s, i=0, first=False, last=False):
                    pe.wait_ge(w_lo_ready, n + 1 + RING * i)
                    pe.wait_ge(sem("hidden_split"), g0 + s + 1 + i)
                    wh = WH[:, n % RING, :, :].rearrange("p (k c) n -> p k (c n)", k=2)
                    wl = WL[:, n % RING, :, :].rearrange("p (k c) n -> p k (c n)", k=2)
                    for k in range(2):
                        for m in range(KT):
                            ps = PS[4 + m // 2][:, (m % 2) * T:(m % 2 + 1) * T]
                            ms = slice(m * P, (m + 1) * P)
                            start = first and k == 0 and m % 2 == 0
                            stop = last and k == 1
                            nc.tensor.matmul(ps, wh[:, k, ms], GH[:, k, :], start=start, stop=False,
                                             skip_group_check=True)
                            nc.tensor.matmul(ps, wh[:, k, ms], GL[:, k, :], start=False, stop=False,
                                             skip_group_check=True)
                            ins = nc.tensor.matmul(ps, wl[:, k, ms], GH[:, k, :], start=False, stop=stop,
                                                   skip_group_check=True)
                    ins.then_inc(block_done, 1)

                up(n0, 0)
                up(n0 + 2, 1)
                down(n0 + 4, 0, first=True)
                with pe.Fori(1, FI - 1) as i:
                    up(n0 + 2, 1, i)
                    down(n0 + 4, 0, i)
                down(n0 + 3 * FI - 1, FI - 1, last=True)

            pe.wait_ge(consts_landed, 32)
            sums(0)

            def normed_tile(k):
                if k % 2 == 0:
                    pe.wait_ge(sem("rms_split"), k // 2 + 1)

            product(pe, N_GIN, 0, XH, XL, ready=normed_tile)
            pe.wait_ge(sem("rank_landed"), 48)
            for d in range(2):
                for k in range(KT):
                    last = nc.tensor.matmul(PS[3][0:16, d * T:(d + 1) * T], w_r[:, k, 16 * d:16 * d + 16],
                                            HF[:, k, :], start=k == 0, stop=k == KT - 1)
            last.then_inc(sem("rank_rows"), 1)
            product(pe, N_GIN + 1, 1, XH, XL)
            pe.wait_ge(sem("rank_rows_taken"), 1)
            for d in range(2):
                for h in range(GH_):
                    last = nc.tensor.matmul(PS[4 + 2 * d + h // 2][:, (h % 2) * T:(h % 2 + 1) * T],
                                            w_up[:, d, h * P:(h + 1) * P], R16[:, d, :], start=True, stop=True)
            last.then_inc(sem("gate_logits"), 1)
            for j in range(2, 8):
                if j >= RING:
                    pe.wait_ge(evacuated, E_GIN + j - RING + 1)
                product(pe, N_GIN + j, bank_of(N_GIN + j), XH, XL, moving_weights=j >= 4)

            def gla_scores(h):
                if h:
                    pe.wait_ge(sem("att_masked"), h)
                for d in range(2):
                    for tt in range(2):
                        ts = slice(tt * P, (tt + 1) * P)
                        last = nc.tensor.matmul(PS[3][:, (2 * d + tt) * P:(2 * d + tt + 1) * P],
                                                KI[:, 4 * d + h, ts], QD[:, 4 * d + h, ts], start=True, stop=True)
                last.then_inc(sem("att_scores"), 1)
                if h:
                    pe.wait_ge(sem("ket_taken"), h)
                for d in range(2):
                    for tt in range(2):
                        last = nc.tensor.transpose(PS[4][:, (2 * d + tt) * P:(2 * d + tt + 1) * P],
                                                   KE[:, 4 * d + h, tt * P:(tt + 1) * P], ident)
                last.then_inc(sem("ke_turned"), 1)

            def gla_states(h):
                pe.wait_ge(sem("ket_taken"), h + 1)
                if h:
                    pe.wait_ge(sem("states_ready"), h)
                for d in range(2):
                    for j in range(3):
                        c = j if d == 0 else 3 - j
                        q = 3 * d + j
                        rows = slice(64 * (c % 2), 64 * (c % 2) + 64)
                        last = nc.tensor.matmul(kv_piece(q),
                                                KET[h % 2][rows, (2 * d + c // 2) * P:(2 * d + c // 2 + 1) * P],
                                                VT[rows, c // 2, h * 256:(h + 1) * 256], start=True, stop=True)
                last.then_inc(sem("chunk_kv"), 1)

            def gla_out(h):
                bank = PS[0]
                sf, sbk, att = SF[h % 2], SBK[h % 2], ATTS[h % 2]
                if h:
                    pe.wait_ge(sem("gla_out_taken"), h)
                pe.wait_ge(sem("att_masked"), h + 1)
                pe.wait_ge(sem("states_ready"), h + 1)
                for v in range(2):
                    c0 = h * 256 + v * P
                    for tt in range(2):
                        nc.tensor.matmul(bank[:, v * T + tt * P:v * T + (tt + 1) * P], VT[:, tt, c0:c0 + P],
                                         att[:, tt, :], start=tt == 0, stop=False, skip_group_check=True)
                    for c in range(1, NC):
                        nc.tensor.matmul(bank[:, v * T + c * CH:v * T + (c + 1) * CH],
                                         sf[:, c - 1, v * P:(v + 1) * P], QD[:, h, c * CH:(c + 1) * CH],
                                         start=False, stop=False, skip_group_check=True)
                    for c in range(NC - 1):
                        last = nc.tensor.matmul(bank[:, v * T + c * CH:v * T + (c + 1) * CH],
                                                sbk[:, 2 - c, v * P:(v + 1) * P],
                                                QD[:, 4 + h, c * CH:(c + 1) * CH],
                                                start=False, stop=c == NC - 2, skip_group_check=True)
                last.then_inc(sem("gla_out_summed"), 1)

            def gla_gate(j, m):
                n = N_GIN + 8 + j
                if m == 0:
                    pe.wait_ge(w_lo_ready, n + 1)
                    pe.wait_ge(evacuated, E_GIN + 8 + j)
                for k in range(KT):
                    last = three(PS[1][:, m * T:(m + 1) * T], WH[:, n % RING, k, m * P:(m + 1) * P],
                                 WL[:, n % RING, k, m * P:(m + 1) * P], XH[:, k, :], XL[:, k, :],
                                 k == 0, k == KT - 1)
                if m:
                    last.then_inc(block_done, 1)

            def gla_sums(pair):
                pe.wait_ge(sem("gla_squares"), 2 * pair + 2)
                for h in (2 * pair, 2 * pair + 1):
                    for v in range(2):
                        last = nc.tensor.matmul(PS[5 + pair][:, (h % 2) * T:(h % 2 + 1) * T], ones,
                                                GSQ[h][:, v, :], start=v == 0, stop=v == 1)
                last.then_inc(sem("gla_square_sums"), 1)

            pe.wait_ge(sem("gla_decayed"), 1)
            pe.wait_ge(evacuated, E_GIN + 8)
            gla_scores(0)
            for h in range(GH_):
                gla_gate(h, 0)
                gla_states(h)
                if h + 1 < GH_:
                    gla_scores(h + 1)
                gla_gate(h, 1)
                if h == GH_ - 1:
                    pe.wait_ge(sem("states_ready"), GH_)
                    gla_sums(0)
                gla_out(h)
            gla_sums(1)
            out_projection(N_GOUT, 0, GH, GL,
                           lambda k: k % 4 == 0 and pe.wait_ge(sem("gla_out_split"), k // 4 + 1))

            sums(1)
            mlp(0, N_F0, E_F0)

            sums(2)

            def qk_ready(k):
                if k % 2 == 0:
                    pe.wait_ge(sem("rms_split"), 8 + k // 2 + 1)

            def qk_sums(*groups):
                for e in groups:
                    pe.wait_ge(sem("qk_squares"), e + 1)
                    nc.tensor.matmul(PS[3 + e][:, :], ones, SQ10[:, 2 * e:2 * e + 2, :], start=True, stop=True)\
                        .then_inc(sem("qk_square_sums"), 1)

            def qk_turns(*groups):
                for e in groups:
                    pe.wait_ge(sem("qk_normed"), e + 1)
                    nc.tensor.matmul(PS[3 + e][:, :], rot, QK[:, QK_AT[e]:QK_AT[e] + 2, :], start=True, stop=True)\
                        .then_inc(sem("qk_turned"), 1)

            work = {3: lambda: qk_sums(0, 1), 4: lambda: qk_turns(0, 1), 5: lambda: qk_sums(2, 3)}
            for j in range(6):
                if j >= RING:
                    pe.wait_ge(evacuated, E_QKV + j - RING + 1)
                product(pe, N_QKV + j, bank_of(N_QKV + j), XH, XL, moving_weights=j == 1,
                        ready=None if j else qk_ready, between_halves=work.get(j))
            pe.wait_ge(evacuated, E_QKV + 6)

            def attend_scores(h):
                pe.wait_ge(sem("qk_roped"), 2 + h // 2)
                if h >= 2:
                    pe.wait_ge(sem("exps_ready"), h - 1)
                for tt in range(2):
                    last = nc.tensor.matmul(PS[3 + h % 2][:, tt * T:(tt + 1) * T], QK[:, h, tt * P:(tt + 1) * P],
                                            QK[:, 8 + h // 4, :], start=True, stop=True)
                last.then_inc(sem("scores_ready"), 1)

            def turn_probs(h):
                pe.wait_ge(sem("probs_ready"), h + 1)
                if h >= 2:
                    pe.wait_ge(sem("probs_t_taken"), h - 1)
                for st in range(2):
                    for tt in range(2):
                        last = nc.tensor.transpose(PS[1 + h % 2][:, st * T + tt * P:st * T + (tt + 1) * P],
                                                   PR[h % 2][:, tt, st * P:(st + 1) * P], ident)
                last.then_inc(sem("probs_turned"), 1)

            def attend_out(h):
                pe.wait_ge(sem("probs_t_taken"), h + 1)
                if h:
                    pe.wait_ge(sem("attn_split"), h)
                for st in range(2):
                    last = nc.tensor.matmul(PS[0][:, 0:T], VA[:, st, (h // 4) * P:(h // 4 + 1) * P],
                                            PT[h % 2][:, st, :], start=st == 0, stop=st == 1)
                last.then_inc(sem("attn_out"), 1)

            def out_part(j, half):
                n = N_AOUT + j
                if half == 0:
                    pe.wait_ge(w_lo_ready, n + 1)
                    if j == RING:
                        pe.wait_ge(out_added, 5)
                for k in range(4 * half, 4 * half + 4):
                    for m in range(2):
                        ps = PS[bank_of(n)][:, m * T:(m + 1) * T]
                        wh, wl = (w[:, n % RING, k, m * P:(m + 1) * P] for w in (WH, WL))
                        if j == 0 or half == 0:
                            pe.wait_ge(sem("attn_split"), k + 1)
                        nc.tensor.matmul(ps, wh, GH[:, k, :], start=k == 0 and m == 0, stop=False,
                                         skip_group_check=True)
                        nc.tensor.matmul(ps, wh, GL[:, k, :], start=False, stop=False, skip_group_check=True)
                        last = nc.tensor.matmul(ps, wl, GH[:, k, :], start=False, stop=k == KT - 1,
                                                skip_group_check=True)
                if half:
                    last.then_inc(block_done, 1)

            attend_scores(0)
            attend_scores(1)
            qk_sums(4)
            qk_turns(2)
            for h in range(QH):
                if h == 1:
                    qk_turns(3)
                if h == 3:
                    qk_turns(4)
                if h + 2 < QH:
                    attend_scores(h + 2)
                turn_probs(h)
                if h:
                    attend_out(h - 1)
                if h >= 5:
                    if h == 5:
                        pe.wait_ge(sem("qk_roped"), 5)
                    out_part(h - 5, 0)
            attend_out(QH - 1)
            pe.wait_ge(sem("ada_steps"), ADA_STEPS)
            for j in range(24):
                last = nc.tensor.matmul(PS[2][:, j:j + 1], ada_acc[j // 8][:, (j % 8) * P:(j % 8 + 1) * P],
                                        ones[:, 0:1], start=True, stop=True)
            last.then_inc(sem("mod_summed"), 1)
            for j in range(4):
                if j == RING:
                    out_part(j, 0)
                out_part(j, 1)

            sums(3)
            mlp(1, N_F1, E_F1)

            sums(4)

            def lora():
                pe.wait_ge(sem("lora_landed"), 48)
                for k in range(KT):
                    last = nc.tensor.matmul(PS[3][:, 0:T], w_lora[:, k, :], HF[:, k, :], start=k == 0, stop=k == KT - 1)
                last.then_inc(sem("lora_rows"), 1)

            needs = {"cout": "conv_y_split", "rout": "rwkv_y_split", "out": "m_split"}

            def quarter(n, q):
                name, j = NAME_AT[n]
                if q == 0:
                    pe.wait_ge(w_lo_ready, n + 1)
                    if name in needs and j:
                        pe.wait_ge(sem(needs[name]), 4)
                    if n >= N_L3 + 2:
                        if n - 2 >= PLACE["rout", 0]:
                            pe.wait_ge(out_added, 8 + n - 2 - PLACE["rout", 0] + 1)
                        else:
                            pe.wait_ge(evacuated, taken(n - 2))
                xh, xl = (GH, GL) if name in ("cout", "rout") else (XH, XL)
                s, m = n % RING, q // 2
                ms = slice(m * P, (m + 1) * P)
                for k in range(4 * (q % 2), 4 * (q % 2) + 4):
                    if n == N_L3 and k % 2 == 0:
                        pe.wait_ge(sem("rms_split"), 16 + k // 2 + 1)
                    if name in needs and j == 0 and k % 2 == 0:
                        pe.wait_ge(sem(needs[name]), k // 2 + 1)
                    last = three(PS[bank_of(n)][:, m * T:(m + 1) * T], WH[:, s, k, ms], WL[:, s, k, ms],
                                 xh[:, k, :], xl[:, k, :], k == 0, k == KT - 1)
                if q == 3:
                    last.then_inc(block_done, 1)

            def whole(n):
                for q in range(4):
                    quarter(n, q)

            def ln(step):
                if step == 0:
                    pe.wait_ge(sem("conv_done"), 1)
                    for g in range(KT):
                        last = nc.tensor.matmul(PS[2][:, 0:T], ones, CONV[:, g, :], start=g == 0, stop=g == KT - 1)
                    last.then_inc(sem("ln_sums"), 1)
                if step == 3:
                    pe.wait_ge(sem("ln_squares"), 1)
                    for g in range(KT):
                        last = nc.tensor.matmul(PS[2][:, 0:T], ones, S8[:, g, :], start=g == 0, stop=g == KT - 1)
                    last.then_inc(sem("ln_sums"), 1)

            def slot(p, k):
                for item in between.get((p, k), ()):
                    if item[0] == "quarter":
                        quarter(item[1], item[2])
                    elif item[0] == "ln":
                        ln(item[1])

            def front(p, part):
                if part == 0:
                    pe.wait_ge(sem("shifted"), 3 * (p // 2) + 3)
                    if p == 0:
                        pe.wait_ge(sem("lora_ready"), 1)
                    if p:
                        pe.wait_ge(sem("uv_ready"), p)
                        pe.wait_ge(sem("inverse_ready"), p)
                    nc.tensor.matmul(PS[6][:, 0:T], w2a2[0:64, p * P:(p + 1) * P], LORA[0:64, :],
                                     start=True, stop=True)
                    nc.tensor.matmul(PS[2][:, 0:T], w2a2[64:128, p * P:(p + 1) * P], LORA[64:128, :],
                                     start=True, stop=True).then_inc(sem("pre_acts"), 1)
                elif part == 1:
                    pe.wait_ge(sem("kk_squares"), p + 1)
                    pe.wait_ge(sem("sigmoids_ready"), p + 1)
                    nc.tensor.matmul(PS[6][:, 0:T], blk, TMP, start=True, stop=True).then_inc(sem("kk_sums"), 1)
                else:
                    pe.wait_ge(sem("rkrk_ready"), p + 1)
                    nc.tensor.matmul(PS[2][:, 0:T], blk, TMP, start=True, stop=True).then_inc(sem("rkrk_sums"), 1)

            def middle(p):
                slot(p, 0)
                if p:
                    pe.wait_ge(sem("o_taken"), p)
                for tt in range(2):
                    last = nc.tensor.transpose(PS[7][:, tt * P:(tt + 1) * P], V_[:, p, tt * P:(tt + 1) * P], ident)
                last.then_inc(sem("v_turned"), 1)
                slot(p, 1)
                slot(p, 2)
                pe.wait_ge(sem("bke_ready"), p + 1)
                pe.wait_ge(sem("rwkv_decayed"), p + 1)
                for h in range(2):
                    rows = slice(64 * h, 64 * h + 64)
                    for c in range(NC):
                        last = nc.tensor.matmul(PS[5 + h][:, c * P:(c + 1) * P], BK[rows, c, :, :], KR[rows, c, :, :],
                                                start=True, stop=True)
                last.then_inc(sem("rwkv_scores"), 1)
                slot(p, 3)
                pe.wait_ge(sem("bke_ready"), p + 1)
                for c in range(NC):
                    last = nc.tensor.transpose(PS[2][:, c * P:(c + 1) * P], BKE[:, c, :, :], ident)
                last.then_inc(sem("bke_turned"), 1)
                slot(p, 4)
                q0 = p * 5
                for lev in range(5):
                    if lev == 0:
                        pe.wait_ge(sem("xt_ready"), q0 + 1)
                        for s in range(8):
                            last = nc.tensor.transpose(PS[3][0:64, s * 64:(s + 1) * 64], XT[:, s * 64:(s + 1) * 64],
                                                       ident[0:64, 0:64])
                        last.then_inc(sem("xt_turned"), 1)
                    pe.wait_ge(sem("x_inv_ready"), q0 + lev + 1)
                    pe.wait_ge(sem("level_ready"), q0 + lev + 1)
                    for s in range(8):
                        ss = slice(s * 64, (s + 1) * 64)
                        last = nc.tensor.matmul(PS[4][0:64, ss], LM[:, ss], XI[:, ss], start=True, stop=True)
                    last.then_inc(sem("y_summed"), 1)
                    slot(p, 5 + 2 * lev)
                    pe.wait_ge(sem("xt_ready"), q0 + lev + 1)
                    pe.wait_ge(sem("y_ready"), q0 + lev + 1)
                    if lev < 4:
                        for s in range(8):
                            ss = slice(s * 64, (s + 1) * 64)
                            last = nc.tensor.matmul(PS[6][0:64, ss], XT[:, ss], YI[:, ss], start=True, stop=True)
                        last.then_inc(sem("x_summed"), 1)
                    for s in range(8):
                        ss = slice(s * 64, (s + 1) * 64)
                        last = nc.tensor.matmul(PS[5][0:64, ss], YI[:, ss], XT[:, ss], start=True, stop=True)
                    last.then_inc(sem("xt_summed"), 1)
                    slot(p, 6 + 2 * lev)

            def chain(p, c):
                r0 = 4 * p + c
                if c == 0:
                    pe.wait_ge(sem("inverse_ready"), p + 1)
                    pe.wait_ge(sem("uv_ready"), p + 1)
                pe.wait_ge(sem("state_ready"), r0 + 1)
                nc.tensor.matmul(PS[3][0:64, 0:P], KR[:, c, 0, :], ST, start=True, stop=False,
                                 skip_group_check=True)
                for h in range(2):
                    last = nc.tensor.matmul(PS[3][0:64, h * 64:(h + 1) * 64], SC[h][:, c, 0:64], UV[:, c, h, :],
                                            start=False, stop=True, skip_group_check=True)
                last.then_inc(sem("rhs_summed"), 1)
                oc = slice(c * CH, (c + 1) * CH)
                nc.tensor.matmul(PS[7][:, oc], ST, KR[:, c, 1, :], start=c == 0, stop=False,
                                 skip_group_check=True)
                pe.wait_ge(sem("rhs_ready"), r0 + 1)
                for h in range(2):
                    s = h * NC + c
                    last = nc.tensor.matmul(PS[4][0:64, h * 64:(h + 1) * 64], XT[:, s * 64:(s + 1) * 64],
                                            RHS[:, h * 64:(h + 1) * 64], start=True, stop=True)
                last.then_inc(sem("u_summed"), 1)
                if c < NC - 1:
                    slot(p, 15 + c)
                pe.wait_ge(sem("u_ready"), r0 + 1)
                nc.tensor.matmul(PS[5][:, 0:P], TK[:, c, :], UV[:, c, :, :], start=True, stop=True)\
                    .then_inc(sem("update_summed"), 1)
                for h in range(2):
                    last = nc.tensor.matmul(PS[7][64 * h:64 * h + 64, oc], UV[:, c, h, :], SC[h][:, c, 64:128],
                                            start=False, stop=c == NC - 1, skip_group_check=True)
                if c == NC - 1:
                    last.then_inc(sem("rwkv_out_summed"), 1)

            pe.wait_ge(evacuated, E_L3)
            whole(N_L3)
            lora()
            for n in range(N_L3 + 1, N_PAIRS):
                whole(n)
                if N_CG <= n < N_CG + 3:
                    front(0, n - N_CG)
            for p in range(8):
                middle(p)
                for c in range(NC):
                    chain(p, c)
                    if p < 7 and c < 3:
                        front(p + 1, c)
            pe.wait_ge(sem("o_taken"), 8)
            for k in range(2):
                for g in range(4):
                    if k:
                        pe.wait_ge(sem("gn_squares"), g + 1)
                    nc.tensor.matmul(PS[3 + g][:, :], blk, (S8 if k else R_)[:, 2 * g:2 * g + 2, :],
                                     start=True, stop=True).then_inc(sem("gn_sums"), 1)
                whole(PLACE["gr", k])
            for n in range(PLACE["gr", 2], N_END):
                whole(n)
            sums(5)

        @block.scalar
        def _(act):
            ch = Chain(act, sem("act_steps"))

            def ck(ap):
                return ap.rearrange("p (c t) -> p c t", c=NC)

            def rsqrt(dst, sums, scale, eps, name):
                ch.step(nc.scalar.activation(dst, sums, ACT.Ln, scale=scale, bias=eps))
                nc.scalar.activation(dst, dst, ACT.Exp, scale=-0.5).then_inc(sem(name), 1)

            def squares(i):
                for g in range(4):
                    if i:
                        act.wait_ge(sem("x_ready"), 4 * (i - 1) + g + 1)
                    nc.scalar.activation(HF[:, 2 * g:2 * g + 2, :], X[:, 2 * g:2 * g + 2, :], ACT.Square)\
                        .then_inc(sem("squares_ready"), 1)

            def norm_split(i, last=False, then=None):
                ch.step(nc.scalar.activation(small[:, 63:64], eps_rms, ACT.Ln))
                act.wait_ge(sem("square_sums"), i + 1)
                rsqrt(RS, PS[3][:, 0:T], 1.0 / D, eps_rms, "rstd_ready")
                if last:
                    return
                if then is not None:
                    split_hi(act, then)
                for g in range(4):
                    act.wait_ge(sem("normed"), 4 * i + g + 1)
                    nc.scalar.activation(XH[:, 2 * g:2 * g + 2, :], HF[:, 2 * g:2 * g + 2, :], ACT.Copy)\
                        .then_inc(sem("rms_hi"), 1)

            def take(n, j, e0, dst, func=ACT.Copy, scale=1.0):
                if n + 2 < N_END:
                    split_hi(act, n + 2)
                act.wait_ge(block_done, n + 1)
                src = PS[bank_of(n)][:, :].rearrange("p (m t) -> p m t", m=2)
                nc.scalar.activation(dst, src, func, scale=scale).then_inc(evacuated, 1)

            def split_for_projection(n0):
                for j in range(4):
                    if n0 + j + 2 < N_END:
                        split_hi(act, n0 + j + 2)

            def hidden_hi(g0, s, i=0):
                act.wait_ge(sem("gate_convolved"), g0 + s + 1 + i)
                nc.scalar.activation(SGT, CG, ACT.Silu).then_inc(sem("gate_silu"), 1)

            def hidden_copy(g0, s, n, i=0):
                act.wait_ge(sem("hidden_ready"), g0 + s + 1 + i)
                nc.scalar.activation(GH[:, 0:2, :], HID, ACT.Copy).then_inc(sem("hidden_hi"), 1)

            def mlp(layer, n0):
                g0 = layer * FI

                def take_val(n, s, i=0):
                    act.wait_ge(block_done, n + 1 + RING * i)
                    if s:
                        act.wait_ge(sem("val_convolved"), g0 + s + i)
                    nc.scalar.activation(U[:, 0, :, 1:T + 1], PS[0][:, :].rearrange("p (m t) -> p m t", m=2),
                                         ACT.Copy).then_inc(evacuated, 1)

                def take_gate(n, s, i=0):
                    act.wait_ge(block_done, n + 1 + RING * i)
                    if s:
                        act.wait_ge(sem("gate_convolved"), g0 + s + i)
                    nc.scalar.activation(U[:, 1, :, 1:T + 1], PS[1][:, :].rearrange("p (m t) -> p m t", m=2),
                                         ACT.Copy).then_inc(evacuated, 1)

                act.wait_ge(sem("u_zeroed"), 1)
                split_hi(act, n0 + 2)
                take_val(n0, 0)
                split_hi(act, n0 + 3)
                take_gate(n0 + 1, 0)
                with act.Fori(0, FI - 1) as i:
                    split_hi(act, n0 + 4, i)
                    hidden_hi(g0, 0, i)
                    take_val(n0 + 2, 1, i)
                    act.wait_ge(block_done, n0 + 2 + RING * i)
                    hidden_copy(g0, 0, n0, i)
                    split_hi(act, n0 + 5, i)
                    take_gate(n0 + 3, 1, i)
                    split_hi(act, n0 + 6, i)
                hidden_hi(g0, FI - 1)
                act.wait_ge(block_done, n0 + 3 * FI - 1)
                hidden_copy(g0, FI - 1, n0)
                split_hi(act, n0 + 3 * FI + 1)

            act.wait_ge(sem("x_landed"), 16)
            squares(0)
            act.wait_ge(consts_landed, 32)
            norm_split(0, then=0)
            split_hi(act, 1)
            nc.scalar.activation(small[:, 0:8], vec("c_2", 0, 8), ACT.Silu).then_inc(sem("silu_c_ready"), 1)
            take(N_GIN, 0, E_GIN, Q[:, 0:2, :], scale=float(P) ** -0.5)
            act.wait_ge(sem("rank_rows"), 1)
            nc.scalar.activation(R16, PS[3][0:16, :].rearrange("p (d t) -> p d t", d=2), ACT.Copy)\
                .then_inc(sem("rank_rows_taken"), 1)
            take(N_GIN + 1, 1, E_GIN, Q[:, 2:4, :], scale=float(P) ** -0.5)
            act.wait_ge(sem("gate_logits"), 1)
            for d in range(2):
                name = "gla_b_gate_b" if d else "gla_b_gate_f"
                for h in range(GH_):
                    last = nc.scalar.activation(LA[:, 4 * d + h, :], PS[4 + 2 * d + h // 2][:, (h % 2) * T:(h % 2 + 1) * T],
                                                ACT.Identity, bias=vec(name, h))
            ch.step(last)
            ch.step(nc.scalar.activation(TMP8, LA, ACT.Abs))
            ch.step(nc.scalar.activation(TMP8, TMP8, ACT.Exp, scale=-1.0))
            nc.scalar.activation(TMP8, TMP8, ACT.Ln, bias=1.0).then_inc(sem("softplus_ready"), 1)
            for j in range(2):
                take(N_GIN + 2 + j, j, E_GIN, K[:, 2 * j:2 * j + 2, :])
            act.wait_ge(sem("gla_sums_ready"), 1)
            nc.scalar.activation(QD, HF, ACT.Exp, scale=1.0 / 16).then_inc(sem("gla_exps"), 1)
            nc.scalar.activation(KI, HF, ACT.Exp, scale=-1.0 / 16).then_inc(sem("gla_exps"), 1)
            nc.scalar.activation(DEC[:, 0:16].rearrange("p (h c) -> p h c", c=NC),
                                 HF[:, 0:4, CH - 1:T:CH], ACT.Exp, scale=1.0 / 16)
            nc.scalar.activation(DEC[:, 16:32].rearrange("p (h c) -> p h c", c=NC),
                                 HF[:, 4:8, 0:T:CH], ACT.Exp, scale=1.0 / 16)
            act.wait_ge(sem("gla_to_end"), 1)
            nc.scalar.activation(KE, KE, ACT.Exp, scale=1.0 / 16).then_inc(sem("gla_exps"), 1)
            for j in range(4):
                take(N_GIN + 4 + j, j, E_GIN, VT[:, :, j * 256:(j + 1) * 256])

            def turn_taken(h):
                act.wait_ge(sem("ke_turned"), h + 1)
                if h < 2:
                    act.wait_ge(sem("gla_decayed"), 1)
                else:
                    act.wait_ge(sem("chunk_kv"), h - 1)
                nc.scalar.activation(KET[h % 2], PS[4][:, :], ACT.Copy).then_inc(sem("ket_taken"), 1)

            turn_taken(0)
            for h in range(GH_):
                split_hi(act, N_GIN + 10 + h)
                if h + 1 < GH_:
                    turn_taken(h + 1)
                n = N_GIN + 8 + h
                act.wait_ge(block_done, n + 1)
                nc.scalar.activation(SG[:, 2 * h:2 * h + 2, :], PS[1][:, :].rearrange("p (m t) -> p m t", m=2),
                                     ACT.Silu).then_inc(evacuated, 1)
                act.wait_ge(sem("gla_out_summed"), h + 1)
                nc.scalar.activation(OT[:, 2 * h:2 * h + 2, :], PS[0][:, :].rearrange("p (v t) -> p v t", v=2),
                                     ACT.Copy).then_inc(sem("gla_out_taken"), 1)
            for q in range(2):
                act.wait_ge(sem("gla_square_sums"), q + 1)
                rsqrt(GRS[:, 2 * q:2 * q + 2, :], PS[5 + q][:, :].rearrange("p (m t) -> p m t", m=2), 1.0 / 256,
                      eps_rms, "gla_rstd")
            for q in range(2):
                act.wait_ge(sem("gla_out_normed"), q + 1)
                nc.scalar.activation(GH[:, 4 * q:4 * q + 4, :], OT[:, 4 * q:4 * q + 4, :], ACT.Copy)\
                    .then_inc(sem("gla_out_hi"), 1)
            split_for_projection(N_GOUT)

            squares(1)
            norm_split(1)
            mlp(0, N_F0)

            squares(2)
            norm_split(2)
            def qk_rsqrt(*groups):
                for e in groups:
                    act.wait_ge(sem("qk_square_sums"), e + 1)
                    ch.done(nc.scalar.activation(SQ10[:, 2 * e:2 * e + 2, :],
                                                 PS[3 + e][:, :].rearrange("p (m t) -> p m t", m=2), ACT.Ln,
                                                 scale=1.0 / P, bias=eps_rms))
                for e in groups:
                    ch.all()
                    nc.scalar.activation(SQ10[:, 2 * e:2 * e + 2, :], SQ10[:, 2 * e:2 * e + 2, :], ACT.Exp,
                                         scale=-0.5).then_inc(sem("qk_rstd"), 1)

            for j in range(6):
                take(N_QKV + j, j, E_QKV, VA if j == 1 else QK[:, QK_AT[max(j - 1, 0)]:QK_AT[max(j - 1, 0)] + 2, :])
                if j == 2:
                    qk_rsqrt(0, 1)
                if j == 4:
                    qk_rsqrt(2, 3)

            def turned_taken(h):
                act.wait_ge(sem("probs_turned"), h + 1)
                if h >= 2:
                    act.wait_ge(sem("attn_out"), h - 1)
                nc.scalar.activation(PT[h % 2], PS[1 + h % 2][:, :].rearrange("p (s q) -> p s q", s=2), ACT.Copy)\
                    .then_inc(sem("probs_t_taken"), 1)

            def out_hi(h):
                act.wait_ge(sem("attn_out"), h + 1)
                nc.scalar.activation(GH[:, h, :], PS[0][:, 0:T], ACT.Copy).then_inc(sem("attn_hi"), 1)

            for h in range(QH):
                act.wait_ge(sem("neg_max_ready"), h + 1)
                if h >= 2:
                    act.wait_ge(sem("probs_turned"), h - 1)
                for tt in range(2):
                    last = nc.scalar.activation(PR[h % 2][:, tt, :], PS[3 + h % 2][:, tt * T:(tt + 1) * T], ACT.Exp,
                                                bias=small[:, 44 + 2 * (h % 2) + tt:45 + 2 * (h % 2) + tt],
                                                scale=float(P) ** -0.5,
                                                accum_out=small[:, 48 + 2 * (h % 2) + tt:49 + 2 * (h % 2) + tt])
                last.then_inc(sem("exps_ready"), 1)
                if h == 0:
                    qk_rsqrt(4)
                if h == 3:
                    split_hi(act, N_AOUT + 2)
                if h:
                    turned_taken(h - 1)
                if h >= 2:
                    out_hi(h - 2)
            turned_taken(QH - 1)
            out_hi(QH - 2)
            out_hi(QH - 1)
            for n in range(N_AOUT + 3, N_AOUT + 6):
                split_hi(act, n)

            squares(3)
            norm_split(3)
            mlp(1, N_F1)

            squares(4)
            norm_split(4)
            act.wait_ge(sem("lora_rows"), 1)
            act.wait_ge(sem("gate_convolved"), 2 * FI)
            nc.scalar.activation(U[:, 1, 0, 1:T + 1], PS[3][:, 0:T], ACT.Copy).then_inc(sem("lora_taken"), 1)
            act.wait_ge(sem("lora_shifted"), 1)
            nc.scalar.activation(LORA[0:64, :], LORA[0:64, :], ACT.Tanh).then_inc(sem("lora_ready"), 1)

            def take_block(n):
                name, j = NAME_AT[n]
                js = slice(2 * j, 2 * j + 2)
                act.wait_ge(block_done, n + 1)
                ps = PS[bank_of(n)][:, :].rearrange("p (m t) -> p m t", m=2)
                gates = ["gate", "og", "gc"]
                if name in gates:
                    turn = 4 * gates.index(name) + j
                    if turn >= 2:
                        act.wait_ge(sem("gate_applied"), turn - 1)
                    nc.scalar.activation(GT[:, turn % 2, :, :], ps, ACT.Silu if name == "og" else ACT.Sigmoid)\
                        .then_inc(evacuated, 1)
                elif name in "rkv":
                    turn = 3 * j + "rkv".index(name)
                    if turn:
                        act.wait_ge(sem("shifted"), turn)
                    nc.scalar.activation(U[:, 1, :, 1:T + 1], ps, ACT.Copy).then_inc(evacuated, 1)
                elif name == "val":
                    act.wait_ge(sem("u31_zeroed"), 1)
                    nc.scalar.activation(U31[:, js, 30:], ps, ACT.Copy).then_inc(evacuated, 1)
                elif name == "rog":
                    act.wait_ge(sem("x_aside_stored"), 16)
                    nc.scalar.activation(ROG[:, js, :], ps, ACT.Silu).then_inc(evacuated, 1)
                elif name == "cout":
                    nc.scalar.activation(HF[:, js, :], ps, ACT.Copy).then_inc(evacuated, 1)
                elif name == "gr":
                    nc.scalar.activation(YM[:, js, :], ps, ACT.Sigmoid).then_inc(evacuated, 1)
                if name == "og":
                    high(CONV, "conv_y", j)

            def high(src, name, g, dst=GH):
                gs = slice(2 * g, 2 * g + 2)
                act.wait_ge(sem(name + "_ready"), g + 1)
                nc.scalar.activation(dst[:, gs, :], src[:, gs, :], ACT.Copy).then_inc(sem(name + "_hi"), 1)

            def split_ahead(n):
                if n + 2 < N_END:
                    split_hi(act, n + 2)

            def ln(step):
                if step == 2:
                    act.wait_ge(sem("conv_centred"), 1)
                    nc.scalar.activation(S8, CONV, ACT.Square).then_inc(sem("ln_squares"), 1)
                if step == 4:
                    act.wait_ge(sem("ln_sums"), 2)
                    rsqrt(LNR, PS[2][:, 0:T], 1.0 / D, eps_ln, "ln_rstd")
                if step == 6:
                    act.wait_ge(sem("conv_normed"), 1)
                    for g in range(KT):
                        ins = nc.scalar.activation(CONV[:, g, :], CONV[:, g, :], ACT.Silu, bias=vec("conv_ln_b_2", g))
                    ins.then_inc(sem("conv_silu"), 1)

            def slot(p, k):
                for item in between.get((p, k), ()):
                    if item[0] == "quarter" and item[2] == 0:
                        split_ahead(item[1])
                    elif item[0] == "take":
                        take_block(item[1])
                    elif item[0] == "ln":
                        ln(item[1])

            def front(p, part):
                if part == 0:
                    act.wait_ge(sem("pre_acts"), p + 1)
                    nc.scalar.activation(SIG, PS[6][:, 0:T], ACT.Sigmoid, bias=vec("rwkv_w0_2", p))
                    nc.scalar.activation(AA, PS[2][:, 0:T], ACT.Sigmoid, bias=vec("rwkv_a0_2", p))\
                        .then_inc(sem("sigmoids_ready"), 1)
                elif part == 1:
                    act.wait_ge(sem("kk_sums_kept"), p + 1)
                    ch.step(nc.scalar.activation(BB, BB, ACT.Ln, scale=65536.0))
                    nc.scalar.activation(BB, BB, ACT.Exp, scale=-0.5, bias=half_ln)\
                        .then_inc(sem("kk_rsqrt"), 1)

            def middle(p):
                act.wait_ge(sem("cums_ready"), p + 1)
                nc.scalar.activation(BK[:, :, 0, :], ck(CUM), ACT.Exp, scale=-DECAY)
                nc.scalar.activation(BKE[:, :, 0, :], ck(SIG), ACT.Exp, scale=DECAY)\
                    .then_inc(sem("sources_exps"), 1)
                slot(p, 0)
                if p:
                    act.wait_ge(sem("rwkv_out_summed"), p)
                nc.scalar.activation(KR[:, :, 0, :], ck(TMP), ACT.Exp, scale=DECAY)
                nc.scalar.activation(KR[:, :, 1, :], ck(CUM), ACT.Exp, scale=DECAY)
                nc.scalar.activation(DECR, CUM[:, CH - 1:T:CH], ACT.Exp, scale=DECAY).then_inc(sem("rwkv_exps"), 1)
                slot(p, 1)
                slot(p, 2)
                act.wait_ge(sem("v_turned"), p + 1)
                act.wait_ge(sem("uv_zeroed"), p + 1)
                for c in range(NC):
                    r = 64 * (c % 2)
                    nc.scalar.activation(UV[64:128, c, :, :],
                                         PS[7][r:r + 64, (c // 2) * P:(c // 2 + 1) * P].rearrange("p (h v) -> p h v", h=2),
                                         ACT.Copy)
                slot(p, 3)
                act.wait_ge(sem("bke_turned"), p + 1)
                nc.scalar.activation(TK, PS[2][:, :].rearrange("p (c n) -> p c n", c=NC), ACT.Copy)\
                    .then_inc(sem("uv_ready"), 1)
                slot(p, 4)
                act.wait_ge(sem("xt_turned"), p + 1)
                nc.scalar.activation(XI, PS[3][0:64, :], ACT.Copy).then_inc(sem("x_inv_ready"), 1)
                for lev in range(5):
                    act.wait_ge(sem("y_summed"), 5 * p + lev + 1)
                    nc.scalar.activation(YI, PS[4][0:64, :], ACT.Copy).then_inc(sem("y_ready"), 1)
                    slot(p, 5 + 2 * lev)
                    slot(p, 6 + 2 * lev)

            def chain(p, c):
                act.wait_ge(sem("u_summed"), 4 * p + c + 1)
                nc.scalar.activation(UV[0:64, c, :, :], PS[4][0:64, 0:P].rearrange("p (h v) -> p h v", h=2),
                                     ACT.Copy, scale=-1.0).then_inc(sem("u_ready"), 1)
                if c < NC - 1:
                    slot(p, 15 + c)
                else:
                    act.wait_ge(sem("rwkv_out_summed"), p + 1)
                    nc.scalar.activation(R_[:, p, :], PS[7][:, 0:T], ACT.Copy).then_inc(sem("o_taken"), 1)

            for n in range(N_L3, N_PAIRS):
                split_ahead(n)
                take_block(n)
                if N_CG <= n < N_CG + 3:
                    front(0, n - N_CG)
            for p in range(8):
                middle(p)
                for c in range(NC):
                    chain(p, c)
                    if p < 7 and c < 3:
                        front(p + 1, c)
            for g in range(4):
                act.wait_ge(sem("gn_centred"), g + 1)
                nc.scalar.activation(S8[:, 2 * g:2 * g + 2, :], R_[:, 2 * g:2 * g + 2, :], ACT.Square)\
                    .then_inc(sem("gn_squares"), 1)
            split_ahead(PLACE["gr", 0])
            take_block(PLACE["gr", 0])
            split_ahead(PLACE["gr", 1])
            for g in range(4):
                act.wait_ge(sem("gn_sums"), 5 + g)
                ch.done(nc.scalar.activation(S8[:, 2 * g:2 * g + 2, :],
                                             PS[3 + g][:, :].rearrange("p (m t) -> p m t", m=2), ACT.Ln,
                                             scale=1.0 / 64, bias=eps_gn))
            ch.all()
            for g in range(4):
                nc.scalar.activation(S8[:, 2 * g:2 * g + 2, :], S8[:, 2 * g:2 * g + 2, :], ACT.Exp, scale=-0.5)\
                    .then_inc(sem("gn_rstd"), 1)
            take_block(PLACE["gr", 1])
            for j in (2, 3):
                split_ahead(PLACE["gr", j])
                high(R_, "rwkv_y", 2 * j - 4)
                take_block(PLACE["gr", j])
                high(R_, "rwkv_y", 2 * j - 3)
            for j in range(4):
                split_ahead(PLACE["rout", j])
                high(YM, "m", j, XH)
            for j in range(4):
                split_ahead(PLACE["out", j])
            squares(5)
            norm_split(5, last=True)

        @block.vector
        def _(dve):
            ch = Chain(dve, sem("dve_steps"))
            v = nc.vector

            def spread(ap, shape):
                return ap.broadcast_to(shape)

            def norm(i, w, modulate=False, last=False):
                dve.wait_ge(sem("rstd_ready"), i + 1)
                def low(g):
                    gs = slice(2 * g, 2 * g + 2)
                    dve.wait_ge(sem("rms_hi"), 4 * i + g + 1)
                    v.tensor_tensor(XL[:, gs, :], HF[:, gs, :], XH[:, gs, :].bitcast(F32), ALU.subtract)\
                        .then_inc(sem("rms_split"), 1)

                for g in range(4):
                    for k in (2 * g, 2 * g + 1):
                        ins = v.scalar_tensor_tensor(HF[:, k, :], X[:, k, :], vec(*w(k)), RS[:, :], ALU.mult, ALU.mult)
                    if modulate:
                        ch.step(ins)
                        for k in (2 * g, 2 * g + 1):
                            ins = v.tensor_scalar(HF[:, k, :], HF[:, k, :], mod[:, 24 + k:25 + k], mod[:, k:k + 1],
                                                  ALU.mult, ALU.add)
                    ins.then_inc(sem("normed"), 1)
                    if g and not last:
                        low(g - 1)
                if not last:
                    low(3)

            def lo(n):
                if n < N_END:
                    split_lo(dve, n)

            def add_projection(n0, a0, dst, add=True, lo_from=0):
                for j in range(4):
                    if j >= lo_from:
                        lo(n0 + j + 2)
                    dve.wait_ge(block_done, n0 + j + 1)
                    ps = PS[bank_of(n0 + j)][:, :].rearrange("p (m t) -> p m t", m=2)
                    d = dst[:, 2 * j:2 * j + 2, :]
                    if add:
                        ins = v.tensor_tensor(d, d, ps, ALU.add)
                    else:
                        ins = v.tensor_copy(d, ps)
                    ins.then_inc(out_added, 1)
                    if add:
                        dve.wait_ge(out_added, a0 + j + 1)
                        dve.sem_inc(sem("x_ready"), 1)

            def mlp(layer, n0, e0):
                g0 = layer * FI
                cw, cb = COL["ffn_w_conv"] + 132 * layer, COL["ffn_b_conv"] + 44 * layer

                def tap(j, half, s, m, i):
                    base = (cb if j is None else cw + 44 * j) + 22 * half + 2 * s + m
                    return V[:, bass.ds(i * 2 + base, 1)] if not isinstance(i, int) else V[:, base:base + 1]

                def convolve(dst, half, s, ch, i=0):
                    for m in range(2):
                        ch.done(v.tensor_scalar(dst[:, m, :], U[:, half, m, 1:T + 1], tap(1, half, s, m, i),
                                                tap(None, half, s, m, i), ALU.mult, ALU.add))
                    for j, at in ((0, 0), (2, 2)):
                        for m in range(2):
                            ch.all(1)
                            ins = v.scalar_tensor_tensor(dst[:, m, :], U[:, half, m, at:at + T],
                                                         tap(j, half, s, m, i), dst[:, m, :], ALU.mult, ALU.add)
                            if j == 2 and m == 1:
                                ins.then_inc(sem("gate_convolved" if half else "val_convolved"), 1)
                            else:
                                ch.done(ins)

                def hidden(s, i=0):
                    dve.wait_ge(sem("gate_silu"), g0 + s + 1 + i)
                    if s or not isinstance(i, int):
                        dve.wait_ge(sem("val_convolved"), g0 + s + 1 + i)
                    v.tensor_tensor(HID, SGT, CV, ALU.mult).then_inc(sem("hidden_ready"), 1)
                    dve.wait_ge(sem("hidden_hi"), g0 + s + 1 + i)
                    v.tensor_tensor(GL[:, 0:2, :], HID, GH[:, 0:2, :].bitcast(F32), ALU.subtract)\
                        .then_inc(sem("hidden_split"), 1)

                split_lo(dve, n0 + 2)
                dve.wait_ge(evacuated, e0 + 1)
                convolve(CV, 0, 0, ch)
                split_lo(dve, n0 + 3)
                dve.wait_ge(evacuated, e0 + 2)
                convolve(CG, 1, 0, ch)
                with dve.Fori(0, FI - 1) as i:
                    ch.enter(i, 10)
                    split_lo(dve, n0 + 4, i)
                    hidden(0, i)
                    dve.wait_ge(evacuated, e0 + 3 + 2 * i)
                    convolve(CV, 0, 1, ch, i)
                    split_lo(dve, n0 + 5, i)
                    dve.wait_ge(evacuated, e0 + 4 + 2 * i)
                    convolve(CG, 1, 1, ch, i)
                    split_lo(dve, n0 + 6, i)
                ch.leave(FI - 1)
                hidden(FI - 1)
                split_lo(dve, n0 + 3 * FI + 1)
                dve.wait_ge(block_done, n0 + 3 * FI)
                for q in range(4):
                    x = X[:, 2 * q:2 * q + 2, :]
                    v.tensor_tensor(x, x, PS[4 + q][:, :].rearrange("p (m t) -> p m t", m=2), ALU.add)\
                        .then_inc(sem("x_ready"), 1)

            ch.done(v.memset(ATT[:, :, :], 0.0))
            ch.done(v.memset(U[:, :, :, 0:1], 0.0))
            ch.step(v.memset(U[:, :, :, T + 1:T + 2], 0.0))
            dve.sem_inc(sem("u_zeroed"), 1)
            dve.wait_ge(consts_landed, 32)
            dve.wait_ge(sem("x_landed"), 16)
            norm(0, lambda k: ("norm_mix", k))
            dve.wait_ge(w_lo_ready, 2)
            lo(2)
            lo(3)
            dve.wait_ge(sem("softplus_ready"), 1)
            ch.step(v.scalar_tensor_tensor(LA, LA, 0.0, TMP8, ALU.min, ALU.subtract))
            dve.wait_ge(sem("rank_rows"), 1)
            for t in range(8):
                ins = v.tensor_tensor_scan(HF[:, t, :], cst("scan"), LA[:, t, :], 0.0, ALU.mult, ALU.add)
            ch.step(ins)

            def chunks(ap):
                return ap.rearrange("p k (c t) -> p (k c) t", t=CH)

            hf, hb = chunks(HF[:, 0:4, :]), chunks(HF[:, 4:8, :])
            shape = [P, 16, CH]
            ch.step(v.tensor_tensor(chunks(TMP8[:, 0:4, :]), spread(hb[:, :, CH - 1:CH], shape), hb, ALU.subtract))
            ins = v.tensor_tensor(HF[:, 4:8, :], TMP8[:, 0:4, :], LA[:, 4:8, :], ALU.add)
            ins.then_inc(sem("gla_sums_ready"), 1)
            dve.wait_ge(sem("gla_sums_ready"), 1)
            v.tensor_tensor(chunks(KE[:, 0:4, :]), spread(hf[:, :, CH - 1:CH], shape), hf, ALU.subtract)
            v.tensor_tensor(chunks(KE[:, 4:8, :]), spread(hb[:, :, 0:1], shape), hb, ALU.subtract)\
                .then_inc(sem("gla_to_end"), 1)
            dve.wait_ge(evacuated, E_GIN + 4)
            for e, (dst, src) in enumerate(((QD, Q), (KI, K), (KE, K))):
                dve.wait_ge(sem("gla_exps"), e + 1)
                for d in range(2):
                    ins = v.tensor_tensor(dst[:, 4 * d:4 * d + 4, :], dst[:, 4 * d:4 * d + 4, :], src, ALU.mult)
            ins.then_inc(sem("gla_decayed"), 1)
            dve.wait_ge(sem("gla_decayed"), 1)
            ch.done(v.memset(ATTS[1], 0.0))
            dve.wait_ge(w_lo_ready, 6)
            for n in range(6, 10):
                lo(n)

            def masked(h):
                dve.wait_ge(sem("att_scores"), h + 1)
                if h >= 2:
                    dve.wait_ge(sem("gla_out_summed"), h - 1)
                for d, m in enumerate(("mask_f", "mask_b")):
                    mask = cst(m).bitcast(I32).unsqueeze(1)
                    ch.all()
                    ins = v.copy_predicated(ATTS[h % 2], spread(mask, [P, 2, P]),
                                            PS[3][:, 2 * d * P:(2 * d + 2) * P].rearrange("p (a b) -> p a b", a=2))
                    if d == 0:
                        ch.done(ins)
                ins.then_inc(sem("att_masked"), 1)

            def states(h):
                sf, sbk = SF[h % 2], SBK[h % 2]
                dve.wait_ge(sem("chunk_kv"), h + 1)

                def decay(d, c):
                    j = 16 * d + 4 * h + c
                    return DEC[:, j:j + 1]

                ch.done(v.tensor_copy(sf[:, 0, :], kv_piece(0)))
                ch.done(v.tensor_copy(sbk[:, 0, :], kv_piece(3)))
                for j in range(1, 3):
                    ch.all(1)
                    ch.done(v.scalar_tensor_tensor(sf[:, j, :], sf[:, j - 1, :], decay(0, j), kv_piece(j), ALU.mult, ALU.add))
                    ch.all(1)
                    ins = v.scalar_tensor_tensor(sbk[:, j, :], sbk[:, j - 1, :], decay(1, 3 - j), kv_piece(3 + j),
                                                 ALU.mult, ALU.add)
                    if j == 1:
                        ch.done(ins)
                ins.then_inc(sem("states_ready"), 1)

            masked(0)
            for h in range(GH_):
                if h >= 2:
                    dve.wait_ge(sem("gla_out_summed"), h - 1)
                states(h)
                if h + 1 < GH_:
                    masked(h + 1)
                lo(N_GIN + 10 + h)
            oh = OT.rearrange("p (h w) t -> p h w t", w=2)
            for q in range(2):
                qs = slice(4 * q, 4 * q + 4)
                dve.wait_ge(sem("gla_rstd"), q + 1)
                for w in range(2):
                    o = oh[:, 2 * q:2 * q + 2, w, :]
                    ins = v.scalar_tensor_tensor(o, o, vec("gla_norm", w), GRS[:, 2 * q:2 * q + 2, :],
                                                 ALU.mult, ALU.mult)
                ch.step(ins)
                v.tensor_tensor(OT[:, qs, :], OT[:, qs, :], SG[:, qs, :], ALU.mult).then_inc(sem("gla_out_normed"), 1)
            for q in range(2):
                qs = slice(4 * q, 4 * q + 4)
                dve.wait_ge(sem("gla_out_hi"), q + 1)
                v.tensor_tensor(GL[:, qs, :], OT[:, qs, :], GH[:, qs, :].bitcast(F32), ALU.subtract)\
                    .then_inc(sem("gla_out_split"), 1)
            add_projection(N_GOUT, 0, X)

            norm(1, lambda k: ("norm_ffn", k))
            mlp(0, N_F0, E_F0)

            norm(2, lambda k: ("norm_mix", 8 + k))

            def qk_norm(*groups):
                for e in groups:
                    gs = slice(QK_AT[e], QK_AT[e] + 2)
                    dve.wait_ge(sem("qk_rstd"), e + 1)
                    v.scalar_tensor_tensor(QK[:, gs, :], QK[:, gs, :], vec("attn_q_norm" if e else "attn_k_norm"),
                                           SQ10[:, 2 * e:2 * e + 2, :], ALU.mult, ALU.mult).then_inc(sem("qk_normed"), 1)

            def rope(*groups):
                for e in groups:
                    gs = slice(QK_AT[e], QK_AT[e] + 2)
                    hs = slice(2 * (e % 4), 2 * (e % 4) + 2)
                    dve.wait_ge(sem("qk_turned"), e + 1)
                    ch.step(v.tensor_tensor(HF[:, hs, :], PS[3 + e][:, :].rearrange("p (m t) -> p m t", m=2),
                                            spread(cst("sin").unsqueeze(1), [P, 2, T]), ALU.mult))
                    dve.wait_ge(sem("qk_cosines"), e + 1)
                    v.tensor_tensor(QK[:, gs, :], SQ10[:, 2 * e:2 * e + 2, :], HF[:, hs, :], ALU.add)\
                        .then_inc(sem("qk_roped"), 1)

            lo(N_QKV + 2)
            lo(N_QKV + 3)
            lo(N_QKV + 4)
            qk_norm(0, 1)
            lo(N_QKV + 5)
            rope(0, 1)
            lo(N_QKV + 6)
            qk_norm(2, 3)
            lo(N_QKV + 7)

            def negated_max(h):
                mx = small[:, 44 + 2 * (h % 2):46 + 2 * (h % 2)]
                dve.wait_ge(sem("scores_ready"), h + 1)
                if h >= 2:
                    dve.wait_ge(sem("exps_ready"), h - 1)
                ch.step(v.tensor_reduce(mx, PS[3 + h % 2][:, :].rearrange("p (m t) -> p m t", m=2), AX_X, ALU.max))
                v.tensor_scalar(mx, mx, -float(P) ** -0.5, None, ALU.mult).then_inc(sem("neg_max_ready"), 1)

            def normalise(h):
                den = small[:, 48 + 2 * (h % 2):50 + 2 * (h % 2)]
                dve.wait_ge(sem("exps_ready"), h + 1)
                ch.step(v.reciprocal(den, den))
                for tt in range(2):
                    ins = v.tensor_scalar(PR[h % 2][:, tt, :], PR[h % 2][:, tt, :], den[:, tt:tt + 1], None, ALU.mult)
                ins.then_inc(sem("probs_ready"), 1)

            def out_lo(h):
                dve.wait_ge(sem("attn_hi"), h + 1)
                v.tensor_tensor(GL[:, h, :], PS[0][:, 0:T], GH[:, h, :].bitcast(F32), ALU.subtract)\
                    .then_inc(sem("attn_split"), 1)

            negated_max(0)
            negated_max(1)
            normalise(0)
            rope(2)
            for h in range(1, QH):
                if h == 1:
                    rope(3)
                    qk_norm(4)
                if h == 3:
                    rope(4)
                    lo(N_AOUT + 2)
                if h + 1 < QH:
                    negated_max(h + 1)
                normalise(h)
                if h >= 2:
                    out_lo(h - 2)
            out_lo(QH - 2)
            out_lo(QH - 1)
            dve.wait_ge(sem("mod_summed"), 1)
            ch.step(v.tensor_tensor(mod[:, 0:24], PS[2][:, 0:24], vec("ada_b_2", 0, 24), ALU.add))
            ch.step(v.tensor_scalar(mod[:, 24:32], mod[:, 8:16], 1.0, None, ALU.add))

            add_projection(N_AOUT, 4, X, lo_from=1)

            norm(3, lambda k: ("norm_ffn", 8 + k))
            mlp(1, N_F1, E_F1)

            norm(4, lambda k: ("norm_g_2", k), modulate=True)

            def shift(dst, half, mu0, name, m_count=2):
                z, before = U[:, half, 0:m_count, 1:T + 1], U[:, half, 0:m_count, 0:T]
                ch.step(v.tensor_tensor(dst, before, z, ALU.subtract))
                for m in range(m_count):
                    ins = v.scalar_tensor_tensor(dst[:, m, :], dst[:, m, :], vec("rwkv_mu_2", mu0 + m), z[:, m, :],
                                                 ALU.mult, ALU.add)
                ins.then_inc(sem(name), 1)

            dve.wait_ge(sem("lora_taken"), 1)
            shift(LORA.unsqueeze(1), 1, 24, "lora_shifted", 1)
            v.memset(U31[:, :, 0:30], 0.0).then_inc(sem("u31_zeroed"), 1)

            def use_block(n):
                name, j = NAME_AT[n]
                js = slice(2 * j, 2 * j + 2)
                if name in ("val", "rog", "cout"):
                    return
                dve.wait_ge(evacuated, taken(n))
                if name in "rkv":
                    first = 8 * "rkv".index(name) + 2 * j
                    shift(RKV[:, first:first + 2, :], 1, first, "shifted")
                    return
                gates = ["gate", "og", "gc"]
                g = GT[:, (4 * gates.index(name) + j) % 2, :, :]
                if name == "gate":
                    v.tensor_tensor(U31[:, js, 30:], U31[:, js, 30:], g, ALU.mult).then_inc(sem("gate_applied"), 1)
                elif name == "og":
                    if j == 0:
                        dve.wait_ge(sem("conv_silu"), 1)
                    v.tensor_tensor(CONV[:, js, :], CONV[:, js, :], g, ALU.mult).then_inc(sem("gate_applied"), 1)
                    dve.wait_ge(sem("gate_applied"), 4 + j + 1)
                    dve.sem_inc(sem("conv_y_ready"), 1)
                    low(CONV, "conv_y", j)
                else:
                    v.tensor_tensor(HF[:, js, :], HF[:, js, :], g, ALU.mult).then_inc(sem("gate_applied"), 1)

            def low(src, name, g, hi=GH, dst=GL):
                gs = slice(2 * g, 2 * g + 2)
                dve.wait_ge(sem(name + "_hi"), g + 1)
                v.tensor_tensor(dst[:, gs, :], src[:, gs, :], hi[:, gs, :].bitcast(F32), ALU.subtract)\
                    .then_inc(sem(name + "_split"), 1)

            tap_at = []

            def taps(first, last):
                for u in range(first, last):
                    j, k = u // KT, u % KT
                    if j == 0:
                        if k == 0:
                            dve.wait_ge(sem("gate_applied"), 4)
                        ins = v.tensor_scalar(CONV[:, k, :], U31[:, k, 0:T], vec("conv_k_2", k), vec("conv_b_2", k),
                                              ALU.mult, ALU.add)
                    else:
                        dve.wait_ge(sem("dve_steps"), tap_at[u - KT])
                        ins = v.scalar_tensor_tensor(CONV[:, k, :], U31[:, k, j:j + T], vec("conv_k_2", KT * j + k),
                                                     CONV[:, k, :], ALU.mult, ALU.add)
                    ch.done(ins)
                    tap_at.append(ch.n)
                if last == TAPS:
                    ch.all()
                    dve.sem_inc(sem("conv_done"), 1)

            def ln(step):
                if step == 1:
                    dve.wait_ge(sem("ln_sums"), 1)
                    for g in range(KT):
                        ins = v.scalar_tensor_tensor(CONV[:, g, :], PS[2][:, 0:T], -1.0 / D, CONV[:, g, :],
                                                     ALU.mult, ALU.add)
                    ins.then_inc(sem("conv_centred"), 1)
                if step == 5:
                    dve.wait_ge(sem("ln_rstd"), 1)
                    for g in range(KT):
                        ins = v.scalar_tensor_tensor(CONV[:, g, :], CONV[:, g, :], vec("conv_ln_g_2", g), LNR,
                                                     ALU.mult, ALU.mult)
                    ins.then_inc(sem("conv_normed"), 1)

            def slot(p, k):
                for item in between.get((p, k), ()):
                    if item[0] == "take":
                        use_block(item[1])
                    elif item[0] == "taps":
                        taps(item[1], item[2])
                    elif item[0] == "ln":
                        ln(item[1])

            def ck(ap):
                return ap.rearrange("p (c t) -> p c t", c=NC)

            def systems(ap, h):
                return ap[:, h * 256:(h + 1) * 256].rearrange("p (c t) -> p c t", c=NC)

            lev_shape = [64, NC, 64]

            def front(p, part):
                if part == 0:
                    dve.wait_ge(sem("shifted"), 3 * (p // 2) + 3)
                    ch.step(v.tensor_scalar(KK, K_[:, p, :], vec("rwkv_k_k_2", p), None, ALU.mult))
                    v.tensor_tensor(TMP, KK, KK, ALU.mult).then_inc(sem("kk_squares"), 1)
                elif part == 1:
                    dve.wait_ge(sem("kk_sums"), p + 1)
                    v.tensor_scalar(BB, PS[6][:, 0:T], 1e-24, None, ALU.max).then_inc(sem("kk_sums_kept"), 1)
                    ch.step(v.tensor_scalar(K2, AA, -1.0, vec("rwkv_k_a_2", p), ALU.add, ALU.mult))
                    ch.step(v.scalar_tensor_tensor(K2, K2, 1.0, K_[:, p, :], ALU.add, ALU.mult))
                    v.scalar_tensor_tensor(TMP, R_[:, p, :], vec("rwkv_r_k_2", p), K2, ALU.mult, ALU.mult)\
                        .then_inc(sem("rkrk_ready"), 1)
                    ch.done(v.tensor_tensor_scan(CUM, cst("scan"), SIG, 0.0, ALU.mult, ALU.add))
                else:
                    ch.all()
                    dve.wait_ge(sem("rkrk_sums"), p + 1)
                    ch.step(v.tensor_tensor(TMP, CUM, SIG, ALU.subtract))
                    v.tensor_tensor(ck(SIG), spread(ck(CUM)[:, :, CH - 1:CH], [P, NC, CH]), ck(CUM), ALU.subtract)\
                        .then_inc(sem("cums_ready"), 1)
                    dve.wait_ge(sem("kk_rsqrt"), p + 1)
                    ch.step(v.tensor_tensor(KK, KK, BB, ALU.mult))
                    ch.done(v.tensor_tensor(BB, KK, AA, ALU.mult))
                    ch.done(v.tensor_tensor(K_[:, p, :], PS[2][:, 0:T], V_[:, p, :], ALU.mult))
                    ch.all()

            def middle(p):
                dve.wait_ge(sem("sources_exps"), p + 1)
                ch.done(v.tensor_tensor(BK[:, :, 1, :], BK[:, :, 0, :], ck(K2), ALU.mult))
                ch.step(v.tensor_tensor(BKE[:, :, 1, :], BKE[:, :, 0, :], ck(K2), ALU.mult))
                v.tensor_tensor(BK[:, :, 0, :], BK[:, :, 0, :], ck(BB), ALU.mult)
                v.tensor_tensor(BKE[:, :, 0, :], BKE[:, :, 0, :], ck(BB), ALU.mult).then_inc(sem("bke_ready"), 1)
                if p:
                    dve.wait_ge(sem("rwkv_out_summed"), p)
                v.memset(UV[0:64, :, :, :], 0.0).then_inc(sem("uv_zeroed"), 1)
                v.memset(ST, 0.0).then_inc(sem("state_ready"), 1)
                slot(p, 0)
                dve.wait_ge(sem("rwkv_exps"), p + 1)
                v.tensor_tensor(KR[:, :, 0, :], KR[:, :, 0, :], ck(KK), ALU.mult)
                v.tensor_tensor(KR[:, :, 1, :], KR[:, :, 1, :], ck(R_[:, p, :]), ALU.mult)\
                    .then_inc(sem("rwkv_decayed"), 1)
                slot(p, 1)
                slot(p, 2)
                dve.wait_ge(sem("rwkv_scores"), p + 1)
                for h in range(2):
                    ins = v.tensor_tensor(SC[h], PS[5 + h][:, :].rearrange("p (c n) -> p c n", c=NC),
                                          spread(cst("scmask").unsqueeze(1), [P, NC, P]), ALU.mult)
                ch.step(ins)

                def level(lev):
                    m = spread(cst("lev")[0:64, 64 * lev:64 * (lev + 1)].unsqueeze(1), lev_shape)
                    for h in range(2):
                        ins = v.tensor_tensor(systems(LM, h), SC[h][0:64, :, 0:64], m, ALU.mult)
                    return ins

                ch.step(level(0))
                for h in range(2):
                    ins = v.tensor_tensor(systems(XT, h), spread(ident[0:64, 0:64].unsqueeze(1), lev_shape),
                                          systems(LM, h), ALU.subtract)
                ins.then_inc(sem("xt_ready"), 1)
                dve.wait_ge(sem("xt_ready"), 5 * p + 1)
                level(1).then_inc(sem("level_ready"), 1)
                slot(p, 3)
                slot(p, 4)
                for lev in range(5):
                    q = 5 * p + lev + 1
                    if lev < 4:
                        dve.wait_ge(sem("y_summed"), q)
                        level(lev + 2).then_inc(sem("level_ready"), 1)
                    slot(p, 5 + 2 * lev)
                    if lev < 4:
                        dve.wait_ge(sem("x_summed"), 4 * p + lev + 1)
                        v.tensor_tensor(XI, XI, PS[6][0:64, :], ALU.subtract).then_inc(sem("x_inv_ready"), 1)
                    dve.wait_ge(sem("xt_summed"), q)
                    v.tensor_tensor(XT, XT, PS[5][0:64, :], ALU.subtract)\
                        .then_inc(sem("xt_ready" if lev < 4 else "inverse_ready"), 1)
                    slot(p, 6 + 2 * lev)

            def chain(p, c):
                dve.wait_ge(sem("rhs_summed"), 4 * p + c + 1)
                v.tensor_copy(RHS, PS[3][0:64, 0:P]).then_inc(sem("rhs_ready"), 1)
                if c < NC - 1:
                    slot(p, 15 + c)
                    dve.wait_ge(sem("update_summed"), 4 * p + c + 1)
                    for h in range(2):
                        hs = slice(64 * h, 64 * h + 64)
                        ins = v.scalar_tensor_tensor(ST[hs, hs], ST[hs, hs], DECR[hs, c:c + 1], PS[5][hs, hs],
                                                     ALU.mult, ALU.add)
                    ins.then_inc(sem("state_ready"), 1)

            for n in range(N_L3, N_PAIRS):
                use_block(n)
                if N_CG <= n < N_CG + 3:
                    front(0, n - N_CG)
            taps(0, TAPS_BEFORE)
            for p in range(8):
                middle(p)
                for c in range(NC):
                    chain(p, c)
                    if p < 7 and c < 3:
                        front(p + 1, c)

            for g in range(4):
                gs = slice(2 * g, 2 * g + 2)
                dve.wait_ge(sem("gn_sums"), g + 1)
                v.scalar_tensor_tensor(R_[:, gs, :], PS[3 + g][:, :].rearrange("p (m t) -> p m t", m=2), -1.0 / 64,
                                       R_[:, gs, :], ALU.mult, ALU.add).then_inc(sem("gn_centred"), 1)
            for g in range(4):
                gs = slice(2 * g, 2 * g + 2)
                dve.wait_ge(sem("gn_rstd"), g + 1)
                for k in (2 * g, 2 * g + 1):
                    ch.done(v.scalar_tensor_tensor(R_[:, k, :], R_[:, k, :], vec("rwkv_gn_g_2", k), S8[:, k, :],
                                                   ALU.mult, ALU.mult))
                ch.all()
                for k in (2 * g, 2 * g + 1):
                    ch.done(v.scalar_tensor_tensor(R_[:, k, :], R_[:, k, :], vec("rwkv_gn_b_2", k), K_[:, k, :],
                                                   ALU.add, ALU.add))
                ch.all()
                v.tensor_tensor(R_[:, gs, :], R_[:, gs, :], ROG[:, gs, :], ALU.mult).then_inc(sem("rwkv_y_ready"), 1)
                if g:
                    low(R_, "rwkv_y", g - 1)
            low(R_, "rwkv_y", 3)
            dve.wait_ge(sem("gate_applied"), 12)
            for j in range(4):
                n, js = PLACE["rout", j], slice(2 * j, 2 * j + 2)
                dve.wait_ge(evacuated, taken(PLACE["gr", j]))
                dve.wait_ge(block_done, n + 1)
                v.tensor_tensor(YM[:, js, :], YM[:, js, :], PS[bank_of(n)][:, :].rearrange("p (m t) -> p m t", m=2),
                                ALU.mult).then_inc(out_added, 1)
                dve.wait_ge(out_added, 8 + j + 1)
                v.tensor_tensor(YM[:, js, :], YM[:, js, :], HF[:, js, :], ALU.add).then_inc(sem("m_ready"), 1)
                if j:
                    low(YM, "m", j - 1, XH, XL)
            low(YM, "m", 3, XH, XL)
            dve.wait_ge(sem("x_back"), 16)
            for j in range(4):
                n = PLACE["out", j]
                dve.wait_ge(block_done, n + 1)
                for m in range(2):
                    k = 2 * j + m
                    ins = v.scalar_tensor_tensor(X[:, k, :], PS[bank_of(n)][:, m * T:(m + 1) * T],
                                                 mod[:, 16 + k:17 + k], X[:, k, :], ALU.mult, ALU.add)
                ins.then_inc(out_added, 1)
                dve.wait_ge(out_added, 12 + j + 1)
                dve.sem_inc(sem("x_ready"), 1)
            norm(5, lambda k: ("final_g_2", k), last=True)
            dve.wait_ge(sem("normed"), 24)
            dve.sem_inc(sem("result_ready"), 1)


_WEIGHTS = ["gla_w_in", "gla_w_gate_up_f", "gla_w_gate_up_b", "gla_w_out", "attn_w_qkv", "attn_w_out", "ada_w_2",
            "w_in_2", "w_conv_out_2", "rwkv_w2_2", "rwkv_a2_2", "w_rwkv_out_2", "w_out_2"]


def kernel(**inputs):
    import concourse.bacc as bacc
    from concourse.bass_utils import run_bass_kernel_spmd as run

    x = np.asarray(inputs["x"])
    arrays = {
        "in_x": np.ascontiguousarray(x[0].T.reshape(KT, P, T).transpose(1, 0, 2)),
        "in_vecs": np.ascontiguousarray(
            np.concatenate([np.asarray(inputs[n]).reshape(-1, P) for n, _ in VECS], axis=0).T),
        "in_consts": constants(),
    }
    for n in _WEIGHTS:
        arrays["in_" + n] = np.ascontiguousarray(np.asarray(inputs[n])[0])
    for n in ("ffn_w_up", "ffn_w_down"):
        arrays["in_" + n] = np.ascontiguousarray(inputs[n])
    nc = bacc.Bacc("TRN2", target_bir_lowering=False, num_devices=1)
    a = {n[3:]: nc.dram_tensor(n, v.shape, mybir.dt.from_np(v.dtype), kind="ExternalInput").ap()
         for n, v in arrays.items()}
    out = nc.dram_tensor("out", (P, KT, T), F32, kind="ExternalOutput").ap()
    a["x_aside"] = nc.dram_tensor("x_aside", (P, KT, T), F32, kind="Internal").ap()
    program(nc, a, out)
    r = run(nc, [arrays], core_ids=[0])
    y = r.results[0]["out"]
    return np.ascontiguousarray(y.transpose(1, 0, 2).reshape(D, T).T)[None]
```
